# Optimizing a Trainium2 kernel written in Bass

```python
import math
import jax, jax.numpy as jnp
from jax import lax
import numpy as np

D_MODEL = 1024
BATCH = 1
SEQ = 256
DEPTH = 1

HEAD_DIM = 64
HEADS_DIFF = 4
HEADS_MOBA = 8
N_HEADS_TOTAL = HEADS_DIFF + HEADS_MOBA
DIFF_WIDTH = HEADS_DIFF * 2 * HEAD_DIM
MOBA_WIDTH = HEADS_MOBA * HEAD_DIM
MIX_WIDTH = DIFF_WIDTH + MOBA_WIDTH
IN_PROJ_WIDTH = 3 * MIX_WIDTH
DIFF_Q_BLOCK = 128
MOBA_BLOCK = 256
MOBA_TOPK = 3
MOBA_Q_CHUNK = 16
NUM_BUCKETS = 32
MAX_DISTANCE = 2048
N_GROUPS = 4
EXPERTS_PER_GROUP = 8
N_EXPERTS = N_GROUPS * EXPERTS_PER_GROUP
EXPERTS_PER_TOKEN = 2
EXPERT_HIDDEN = 256
DISPATCH_CHUNK = 256
RMS_EPS = 1e-6
NEG_INF = -1e30


def rms_norm(x, g):
    xf = x.astype(jnp.float32)
    y = xf * lax.rsqrt(jnp.mean(xf * xf, axis=-1, keepdims=True) + RMS_EPS)
    return (y * g.astype(jnp.float32)).astype(x.dtype)

def t5_bucket(dist):
    n = jnp.maximum(dist, 0)
    max_exact = NUM_BUCKETS // 2
    nf = jnp.maximum(n, 1).astype(jnp.float32)
    large = max_exact + (jnp.log(nf / max_exact) / math.log(MAX_DISTANCE / max_exact)
                         * (NUM_BUCKETS - max_exact)).astype(jnp.int32)
    large = jnp.minimum(large, NUM_BUCKETS - 1)
    return jnp.where(n < max_exact, n, large)

def diff_attention(q, k, v, q_g, k_g, lq1, lk1, lq2, lk2, sub_g, bias_table, lambda_init):
    B, S, H = q.shape[:3]
    q = rms_norm(q, q_g).transpose(0, 2, 3, 1, 4)
    k = rms_norm(k, k_g).transpose(0, 2, 3, 1, 4)
    v = v.transpose(0, 2, 1, 3)
    f32 = jnp.float32
    lam = (jnp.exp(jnp.sum(lq1.astype(f32) * lk1.astype(f32)))
           - jnp.exp(jnp.sum(lq2.astype(f32) * lk2.astype(f32))) + lambda_init)
    scale = HEAD_DIM ** -0.5
    kpos = jnp.arange(S)

    def block(i):
        s0 = i * DIFF_Q_BLOCK
        qb = lax.dynamic_slice_in_dim(q, s0, DIFF_Q_BLOCK, axis=3)
        logits = jnp.einsum('bhmqd,bhmkd->bhmqk', qb, k, preferred_element_type=f32) * scale
        dist = (s0 + jnp.arange(DIFF_Q_BLOCK))[:, None] - kpos[None, :]
        bias = bias_table[t5_bucket(dist)].astype(f32).transpose(2, 0, 1)
        logits = jnp.where(dist >= 0, logits + bias[None, :, None], NEG_INF)
        p = jax.nn.softmax(logits, axis=-1)
        w = p[:, :, 0] - lam * p[:, :, 1]
        return jnp.einsum('bhqk,bhkc->bhqc', w.astype(v.dtype), v)

    out = lax.map(block, jnp.arange(S // DIFF_Q_BLOCK))
    out = out.transpose(1, 0, 3, 2, 4).reshape(B, S, H, 2 * HEAD_DIM)
    out = rms_norm(out, sub_g) * (1.0 - lambda_init)
    return out.reshape(B, S, H * 2 * HEAD_DIM)

def moba_attention(q, k, v, q_g, k_g, bias_table):
    B, S, H, d = q.shape
    f32 = jnp.float32
    q = rms_norm(q, q_g).transpose(0, 2, 1, 3)
    k = rms_norm(k, k_g).transpose(0, 2, 1, 3)
    v = v.transpose(0, 2, 1, 3)
    n_kb = -(-S // MOBA_BLOCK)
    pad = n_kb * MOBA_BLOCK - S
    k_blocks = jnp.pad(k, ((0, 0), (0, 0), (0, pad), (0, 0))).reshape(B, H, n_kb, MOBA_BLOCK, d)
    v_blocks = jnp.pad(v, ((0, 0), (0, 0), (0, pad), (0, 0))).reshape(B, H, n_kb, MOBA_BLOCK, d)
    k_mean = jnp.mean(k_blocks.astype(f32), axis=3)
    top = min(MOBA_TOPK, n_kb)
    scale = HEAD_DIM ** -0.5
    bi = jnp.arange(B)[:, None, None, None]
    hi = jnp.arange(H)[None, :, None, None]
    blk_off = jnp.arange(MOBA_BLOCK)

    def chunk(i):
        s0 = i * MOBA_Q_CHUNK
        qc = lax.dynamic_slice_in_dim(q, s0, MOBA_Q_CHUNK, axis=2)
        qpos = s0 + jnp.arange(MOBA_Q_CHUNK)
        own = s0 // MOBA_BLOCK
        gate = jnp.einsum('bhqd,bhnd->bhqn', qc.astype(f32), k_mean)
        gate = jnp.where(jnp.arange(n_kb) < own, gate, NEG_INF)
        _, sel = lax.top_k(gate, top)
        sel_valid = jnp.arange(top)[:, None] < own
        k_sel = k_blocks[bi, hi, sel]
        v_sel = v_blocks[bi, hi, sel]
        sel_logits = jnp.einsum('bhqd,bhqtkd->bhqtk', qc, k_sel, preferred_element_type=f32) * scale
        sel_pos = sel[..., None] * MOBA_BLOCK + blk_off
        sel_bias = bias_table[t5_bucket(qpos[:, None, None] - sel_pos), hi[..., None]].astype(f32)
        sel_logits = jnp.where(sel_valid, sel_logits + sel_bias, NEG_INF)
        k_own = lax.dynamic_index_in_dim(k_blocks, own, axis=2, keepdims=False)
        v_own = lax.dynamic_index_in_dim(v_blocks, own, axis=2, keepdims=False)
        dist_own = qpos[:, None] - (own * MOBA_BLOCK + blk_off)[None, :]
        own_bias = bias_table[t5_bucket(dist_own)].astype(f32).transpose(2, 0, 1)[None]
        own_logits = jnp.einsum('bhqd,bhkd->bhqk', qc, k_own, preferred_element_type=f32) * scale
        own_logits = jnp.where(dist_own >= 0, own_logits + own_bias, NEG_INF)
        logits = jnp.concatenate([sel_logits.reshape(B, H, MOBA_Q_CHUNK, top * MOBA_BLOCK), own_logits], axis=-1)
        p = jax.nn.softmax(logits, axis=-1).astype(v.dtype)
        p_sel = p[..., :top * MOBA_BLOCK].reshape(B, H, MOBA_Q_CHUNK, top, MOBA_BLOCK)
        p_own = p[..., top * MOBA_BLOCK:]
        return (jnp.einsum('bhqtk,bhqtkd->bhqd', p_sel, v_sel)
                + jnp.einsum('bhqk,bhkd->bhqd', p_own, v_own))

    out = lax.map(chunk, jnp.arange(S // MOBA_Q_CHUNK))
    return out.transpose(1, 0, 3, 2, 4).reshape(B, S, H * d)

def hier_moe(h, router_group, router_expert, w_gate, w_up, w_down):
    B, S, D = h.shape
    N = B * S
    t = h.reshape(N, D)
    f32 = jnp.float32
    g_logits = (t @ router_group).astype(f32)
    g_prob = jax.nn.softmax(g_logits, axis=-1)
    g = jnp.argmax(g_logits, axis=-1)
    p_group = jnp.take_along_axis(g_prob, g[:, None], axis=-1)
    e_logits_all = jnp.einsum('nd,gde->nge', t, router_expert).astype(f32)
    e_logits = jnp.take_along_axis(e_logits_all, g[:, None, None], axis=1)[:, 0]
    top_v, top_e = lax.top_k(e_logits, EXPERTS_PER_TOKEN)
    weight = p_group * jax.nn.softmax(top_v, axis=-1)
    expert_id = g[:, None] * EXPERTS_PER_GROUP + top_e
    A = N * EXPERTS_PER_TOKEN
    C = DISPATCH_CHUNK
    eid = expert_id.reshape(A)
    tok = jnp.repeat(jnp.arange(N, dtype=jnp.int32), EXPERTS_PER_TOKEN)
    w_flat = weight.reshape(A)
    order = jnp.argsort(eid)
    eid_s, tok_s, w_s = eid[order], tok[order], w_flat[order]
    counts = jax.ops.segment_sum(jnp.ones((A,), jnp.int32), eid, num_segments=N_EXPERTS)
    start = jnp.cumsum(counts) - counts
    pad_counts = ((counts + C - 1) // C) * C
    pad_end = jnp.cumsum(pad_counts)
    pad_start = pad_end - pad_counts
    dest = pad_start[eid_s] + (jnp.arange(A, dtype=jnp.int32) - start[eid_s])
    P = A + N_EXPERTS * C
    n_chunks = P // C
    slot_tok = jnp.zeros((P,), jnp.int32).at[dest].set(tok_s)
    slot_w = jnp.zeros((P,), f32).at[dest].set(w_s)
    chunk_e = jnp.minimum(jnp.searchsorted(pad_end, jnp.arange(n_chunks) * C, side='right'), N_EXPERTS - 1)

    def run(args):
        e, toks = args
        xc = t[toks]
        hid = jax.nn.silu(xc @ w_gate[e]) * (xc @ w_up[e])
        return hid @ w_down[e]

    out = lax.map(run, (chunk_e, slot_tok.reshape(n_chunks, C))).reshape(P, D)
    y = jnp.zeros((N, D), t.dtype).at[slot_tok].add((out * slot_w[:, None]).astype(t.dtype))
    return y.reshape(B, S, D)

def first_inputs(seed: int = 0) -> dict:
    key = jax.random.key(seed)
    ks = jax.random.split(key, 20)
    f32 = jnp.float32

    def nrm(k, shape, scale):
        return jax.random.normal(k, shape, f32) * scale

    def gain(k, shape):
        return 1.0 + 0.05 * jax.random.normal(k, shape, f32)

    return {
        'x': nrm(ks[0], (BATCH, SEQ, D_MODEL), 1.0),
        'norm1_g': gain(ks[1], (DEPTH, D_MODEL)),
        'w_in': nrm(ks[2], (DEPTH, D_MODEL, IN_PROJ_WIDTH), D_MODEL ** -0.5),
        'diff_q_g': gain(ks[3], (DEPTH, HEAD_DIM)),
        'diff_k_g': gain(ks[4], (DEPTH, HEAD_DIM)),
        'lambda_q1': nrm(ks[5], (DEPTH, HEAD_DIM), 0.1),
        'lambda_k1': nrm(ks[6], (DEPTH, HEAD_DIM), 0.1),
        'lambda_q2': nrm(ks[7], (DEPTH, HEAD_DIM), 0.1),
        'lambda_k2': nrm(ks[8], (DEPTH, HEAD_DIM), 0.1),
        'diff_sub_g': gain(ks[9], (DEPTH, 2 * HEAD_DIM)),
        'moba_q_g': gain(ks[10], (DEPTH, HEAD_DIM)),
        'moba_k_g': gain(ks[11], (DEPTH, HEAD_DIM)),
        'rel_bias': nrm(ks[12], (NUM_BUCKETS, N_HEADS_TOTAL), 0.5),
        'w_out': nrm(ks[13], (DEPTH, MIX_WIDTH, D_MODEL), MIX_WIDTH ** -0.5),
        'norm2_g': gain(ks[14], (DEPTH, D_MODEL)),
        'router_group': nrm(ks[15], (DEPTH, D_MODEL, N_GROUPS), D_MODEL ** -0.5),
        'router_expert': nrm(ks[16], (DEPTH, N_GROUPS, D_MODEL, EXPERTS_PER_GROUP), D_MODEL ** -0.5),
        'w_gate': nrm(ks[17], (DEPTH, N_EXPERTS, D_MODEL, EXPERT_HIDDEN), D_MODEL ** -0.5),
        'w_up': nrm(ks[18], (DEPTH, N_EXPERTS, D_MODEL, EXPERT_HIDDEN), D_MODEL ** -0.5),
        'w_down': nrm(ks[19], (DEPTH, N_EXPERTS, EXPERT_HIDDEN, D_MODEL), EXPERT_HIDDEN ** -0.5),
    }

def first_block(x, norm1_g, w_in, diff_q_g, diff_k_g, lambda_q1, lambda_k1, lambda_q2, lambda_k2,
              diff_sub_g, moba_q_g, moba_k_g, rel_bias, w_out, norm2_g, router_group,
              router_expert, w_gate, w_up, w_down):
    B, S, _ = x.shape
    bias_diff = rel_bias[:, :HEADS_DIFF]
    bias_moba = rel_bias[:, HEADS_DIFF:]
    splits = [DIFF_WIDTH, 2 * DIFF_WIDTH, 3 * DIFF_WIDTH,
              3 * DIFF_WIDTH + MOBA_WIDTH, 3 * DIFF_WIDTH + 2 * MOBA_WIDTH]
    for layer in range(DEPTH):
        lambda_init = 0.8 - 0.6 * math.exp(-0.3 * layer)
        h = rms_norm(x, norm1_g[layer])
        proj = h @ w_in[layer]
        q_d, k_d, v_d, q_m, k_m, v_m = jnp.split(proj, splits, axis=-1)
        y_d = diff_attention(q_d.reshape(B, S, HEADS_DIFF, 2, HEAD_DIM),
                             k_d.reshape(B, S, HEADS_DIFF, 2, HEAD_DIM),
                             v_d.reshape(B, S, HEADS_DIFF, 2 * HEAD_DIM),
                             diff_q_g[layer], diff_k_g[layer], lambda_q1[layer], lambda_k1[layer],
                             lambda_q2[layer], lambda_k2[layer], diff_sub_g[layer], bias_diff, lambda_init)
        y_m = moba_attention(q_m.reshape(B, S, HEADS_MOBA, HEAD_DIM),
                             k_m.reshape(B, S, HEADS_MOBA, HEAD_DIM),
                             v_m.reshape(B, S, HEADS_MOBA, HEAD_DIM),
                             moba_q_g[layer], moba_k_g[layer], bias_moba)
        x = x + jnp.concatenate([y_d, y_m], axis=-1) @ w_out[layer]
        x = x + hier_moe(rms_norm(x, norm2_g[layer]), router_group[layer], router_expert[layer],
                         w_gate[layer], w_up[layer], w_down[layer])
    return x


DEPTH_2 = 2

N_MIXERS = 2
NORM_EPS = 1e-6
D_RNN = 128 * round(4 * D_MODEL / (3 * 128))
LRU_BLOCKS = 16
LRU_BLOCK = D_RNN // LRU_BLOCKS
LRU_C = 8.0
CONV_WIDTH = 4
FOX_HEADS = 16
FOX_HEAD_DIM = D_MODEL // FOX_HEADS
QUERY_BLOCK = 128
PEER_HEADS = 8
PEER_KEYS = 128
PEER_EXPERTS = PEER_KEYS * PEER_KEYS
PEER_TOPK = 16
PEER_QDIM = 256
PEER_HALF = PEER_QDIM // 2
TOKEN_CHUNK = 128


def rms_norm_2(x, g):
    xf = x.astype(jnp.float32)
    y = xf * lax.rsqrt(jnp.mean(xf * xf, axis=-1, keepdims=True) + NORM_EPS)
    return (y * g.astype(jnp.float32)).astype(x.dtype)

def ada_modulation(c, w, b):
    mod = jax.nn.silu(c) @ w + b
    shift, scale, gate = jnp.split(mod, 3, axis=-1)
    return shift[:, None, :], scale[:, None, :], gate[:, None, :]

def causal_depthwise_conv(x, w, b):
    y = lax.conv_general_dilated(x, w[:, None, :], window_strides=(1,), padding=[(CONV_WIDTH - 1, 0)], dimension_numbers=('NWC', 'WIO', 'NWC'), feature_group_count=x.shape[-1])
    return y + b

def _linear_recurrence_combine(left, right):
    a_l, b_l = left
    a_r, b_r = right
    return a_l * a_r, a_r * b_l + b_r

def rglru_mixer(h, in_w, conv_w, conv_b, ra_w, ra_b, ri_w, ri_b, lam, out_w):
    B, S, _ = h.shape
    xb, gb = jnp.split(h @ in_w, 2, axis=-1)
    xb = causal_depthwise_conv(xb, conv_w, conv_b)
    xblk = xb.reshape(B, S, LRU_BLOCKS, LRU_BLOCK)
    r = jax.nn.sigmoid(jnp.einsum('bsnc,ncd->bsnd', xblk, ra_w).reshape(B, S, D_RNN) + ra_b)
    i = jax.nn.sigmoid(jnp.einsum('bsnc,ncd->bsnd', xblk, ri_w).reshape(B, S, D_RNN) + ri_b)
    log_a = -LRU_C * jax.nn.softplus(-lam.astype(jnp.float32)) * r.astype(jnp.float32)
    a = jnp.exp(log_a)
    u = jnp.sqrt(-jnp.expm1(2.0 * log_a)) * (i * xb).astype(jnp.float32)
    _, hs = lax.associative_scan(_linear_recurrence_combine, (a, u), axis=1)
    y = hs.astype(h.dtype) * jax.nn.gelu(gb, approximate=False)
    return y @ out_w

def fox_mixer(h, in_w, f_b, q_norm_g, k_norm_g, out_w):
    B, S, D = h.shape
    H, E = FOX_HEADS, FOX_HEAD_DIM
    n_blk = S // QUERY_BLOCK
    q, k, v, f_logit, og = jnp.split(h @ in_w, [D, 2 * D, 3 * D, 3 * D + H], axis=-1)
    q = rms_norm_2(q.reshape(B, S, H, E), q_norm_g)
    k = rms_norm_2(k.reshape(B, S, H, E), k_norm_g)
    v = v.reshape(B, S, H, E)
    log_f = jax.nn.log_sigmoid(f_logit.astype(jnp.float32) + f_b.astype(jnp.float32))
    cum = jnp.cumsum(log_f, axis=1).transpose(0, 2, 1)
    q_blocks = q.reshape(B, n_blk, QUERY_BLOCK, H, E).transpose(1, 0, 3, 2, 4)
    cum_blocks = cum.reshape(B, H, n_blk, QUERY_BLOCK).transpose(2, 0, 1, 3)
    pos_blocks = jnp.arange(S, dtype=jnp.int32).reshape(n_blk, QUERY_BLOCK)
    key_pos = jnp.arange(S, dtype=jnp.int32)
    scale = E ** -0.5

    def attend_block(args):
        qb, cq, qpos = args
        s = jnp.einsum('bhqe,bkhe->bhqk', qb, k).astype(jnp.float32) * scale
        s = s + cq[..., None] - cum[:, :, None, :]
        s = jnp.where(qpos[:, None] >= key_pos[None, :], s, -jnp.inf)
        p = jax.nn.softmax(s, axis=-1)
        return jnp.einsum('bhqk,bkhe->bqhe', p.astype(v.dtype), v)

    o = lax.map(attend_block, (q_blocks, cum_blocks, pos_blocks))
    o = o.transpose(1, 0, 2, 3, 4).reshape(B, S, H, E)
    o = o * jax.nn.sigmoid(og).reshape(B, S, H, E)
    return o.reshape(B, S, D) @ out_w

def peer_ffn(h, q_w, subkey1, subkey2, expert_u, expert_v):
    B, S, D = h.shape
    chunks = h.reshape(B * S // TOKEN_CHUNK, TOKEN_CHUNK, D)

    def retrieve_chunk(xc):
        q = (xc @ q_w).reshape(TOKEN_CHUNK, PEER_HEADS, 2, PEER_HALF)
        s1 = jnp.einsum('thd,hnd->thn', q[:, :, 0], subkey1).astype(jnp.float32)
        s2 = jnp.einsum('thd,hnd->thn', q[:, :, 1], subkey2).astype(jnp.float32)
        v1, i1 = lax.top_k(s1, PEER_TOPK)
        v2, i2 = lax.top_k(s2, PEER_TOPK)
        cand = (v1[..., :, None] + v2[..., None, :]).reshape(TOKEN_CHUNK, PEER_HEADS, PEER_TOPK * PEER_TOPK)
        top_s, top_c = lax.top_k(cand, PEER_TOPK)
        e1 = jnp.take_along_axis(i1, top_c // PEER_TOPK, axis=-1)
        e2 = jnp.take_along_axis(i2, top_c % PEER_TOPK, axis=-1)
        expert = e1 * PEER_KEYS + e2
        g = jax.nn.softmax(top_s, axis=-1)
        u = jnp.take(expert_u, expert, axis=0)
        act = jax.nn.gelu(jnp.einsum('thkd,td->thk', u, xc).astype(jnp.float32), approximate=False)
        w = (g * act).astype(xc.dtype)
        return jnp.einsum('thk,thkd->td', w, jnp.take(expert_v, expert, axis=0))

    return lax.map(retrieve_chunk, chunks).reshape(B, S, D)

def _mod_params(nrm):
    return nrm((D_MODEL, 3 * D_MODEL), 0.5 * D_MODEL ** -0.5), nrm((3 * D_MODEL,), 0.02)

def second_inputs(seed: int = 0) -> dict:
    key = jax.random.key(seed)
    ks = iter(jax.random.split(key, 64))

    def nrm(shape, scale):
        return jax.random.normal(next(ks), shape, jnp.float32) * scale

    def gain(n):
        return 1.0 + nrm((n,), 0.05)

    def peer_params():
        return (nrm((D_MODEL, PEER_HEADS * PEER_QDIM), D_MODEL ** -0.5),
                nrm((PEER_HEADS, PEER_KEYS, PEER_HALF), PEER_HALF ** -0.5),
                nrm((PEER_HEADS, PEER_KEYS, PEER_HALF), PEER_HALF ** -0.5),
                nrm((PEER_EXPERTS, D_MODEL), D_MODEL ** -0.5),
                nrm((PEER_EXPERTS, D_MODEL), PEER_HEADS ** -0.5))

    x = nrm((BATCH, SEQ, D_MODEL), 1.0)
    c = nrm((BATCH, D_MODEL), 1.0)
    l0_mix_norm_g = gain(D_MODEL)
    l0_mix_mod_w, l0_mix_mod_b = _mod_params(nrm)
    l0_lru_in_w = nrm((D_MODEL, 2 * D_RNN), D_MODEL ** -0.5)
    l0_lru_conv_w = nrm((CONV_WIDTH, D_RNN), CONV_WIDTH ** -0.5)
    l0_lru_conv_b = nrm((D_RNN,), 0.02)
    l0_lru_ra_w = nrm((LRU_BLOCKS, LRU_BLOCK, LRU_BLOCK), LRU_BLOCK ** -0.5)
    l0_lru_ra_b = nrm((D_RNN,), 0.02)
    l0_lru_ri_w = nrm((LRU_BLOCKS, LRU_BLOCK, LRU_BLOCK), LRU_BLOCK ** -0.5)
    l0_lru_ri_b = nrm((D_RNN,), 0.02)
    a_pow_c = jax.random.uniform(next(ks), (D_RNN,), jnp.float32, minval=0.9, maxval=0.999)
    a0 = a_pow_c ** (1.0 / LRU_C)
    l0_lru_lambda = jnp.log(a0) - jnp.log1p(-a0)
    l0_lru_out_w = nrm((D_RNN, D_MODEL), D_RNN ** -0.5)
    l0_ffn_norm_g = gain(D_MODEL)
    l0_ffn_mod_w, l0_ffn_mod_b = _mod_params(nrm)
    l0_peer_q_w, l0_peer_subkey1, l0_peer_subkey2, l0_peer_u, l0_peer_v = peer_params()
    l1_mix_norm_g = gain(D_MODEL)
    l1_mix_mod_w, l1_mix_mod_b = _mod_params(nrm)
    l1_fox_in_w = nrm((D_MODEL, 4 * D_MODEL + FOX_HEADS), D_MODEL ** -0.5)
    l1_fox_f_b = jax.random.uniform(next(ks), (FOX_HEADS,), jnp.float32, minval=1.0, maxval=6.0)
    l1_fox_q_norm_g = gain(FOX_HEAD_DIM)
    l1_fox_k_norm_g = gain(FOX_HEAD_DIM)
    l1_fox_out_w = nrm((D_MODEL, D_MODEL), D_MODEL ** -0.5)
    l1_ffn_norm_g = gain(D_MODEL)
    l1_ffn_mod_w, l1_ffn_mod_b = _mod_params(nrm)
    l1_peer_q_w, l1_peer_subkey1, l1_peer_subkey2, l1_peer_u, l1_peer_v = peer_params()
    return {'x': x, 'c': c,
            'l0_mix_norm_g': l0_mix_norm_g, 'l0_mix_mod_w': l0_mix_mod_w, 'l0_mix_mod_b': l0_mix_mod_b,
            'l0_lru_in_w': l0_lru_in_w, 'l0_lru_conv_w': l0_lru_conv_w, 'l0_lru_conv_b': l0_lru_conv_b,
            'l0_lru_ra_w': l0_lru_ra_w, 'l0_lru_ra_b': l0_lru_ra_b, 'l0_lru_ri_w': l0_lru_ri_w, 'l0_lru_ri_b': l0_lru_ri_b,
            'l0_lru_lambda': l0_lru_lambda, 'l0_lru_out_w': l0_lru_out_w,
            'l0_ffn_norm_g': l0_ffn_norm_g, 'l0_ffn_mod_w': l0_ffn_mod_w, 'l0_ffn_mod_b': l0_ffn_mod_b,
            'l0_peer_q_w': l0_peer_q_w, 'l0_peer_subkey1': l0_peer_subkey1, 'l0_peer_subkey2': l0_peer_subkey2,
            'l0_peer_u': l0_peer_u, 'l0_peer_v': l0_peer_v,
            'l1_mix_norm_g': l1_mix_norm_g, 'l1_mix_mod_w': l1_mix_mod_w, 'l1_mix_mod_b': l1_mix_mod_b,
            'l1_fox_in_w': l1_fox_in_w, 'l1_fox_f_b': l1_fox_f_b, 'l1_fox_q_norm_g': l1_fox_q_norm_g,
            'l1_fox_k_norm_g': l1_fox_k_norm_g, 'l1_fox_out_w': l1_fox_out_w,
            'l1_ffn_norm_g': l1_ffn_norm_g, 'l1_ffn_mod_w': l1_ffn_mod_w, 'l1_ffn_mod_b': l1_ffn_mod_b,
            'l1_peer_q_w': l1_peer_q_w, 'l1_peer_subkey1': l1_peer_subkey1, 'l1_peer_subkey2': l1_peer_subkey2,
            'l1_peer_u': l1_peer_u, 'l1_peer_v': l1_peer_v}

def second_block(x, c,
              l0_mix_norm_g, l0_mix_mod_w, l0_mix_mod_b,
              l0_lru_in_w, l0_lru_conv_w, l0_lru_conv_b,
              l0_lru_ra_w, l0_lru_ra_b, l0_lru_ri_w, l0_lru_ri_b,
              l0_lru_lambda, l0_lru_out_w,
              l0_ffn_norm_g, l0_ffn_mod_w, l0_ffn_mod_b,
              l0_peer_q_w, l0_peer_subkey1, l0_peer_subkey2, l0_peer_u, l0_peer_v,
              l1_mix_norm_g, l1_mix_mod_w, l1_mix_mod_b,
              l1_fox_in_w, l1_fox_f_b, l1_fox_q_norm_g, l1_fox_k_norm_g, l1_fox_out_w,
              l1_ffn_norm_g, l1_ffn_mod_w, l1_ffn_mod_b,
              l1_peer_q_w, l1_peer_subkey1, l1_peer_subkey2, l1_peer_u, l1_peer_v):
    mix_norms = [(l0_mix_norm_g, l0_mix_mod_w, l0_mix_mod_b), (l1_mix_norm_g, l1_mix_mod_w, l1_mix_mod_b)]
    mixer_params = [(l0_lru_in_w, l0_lru_conv_w, l0_lru_conv_b, l0_lru_ra_w, l0_lru_ra_b, l0_lru_ri_w, l0_lru_ri_b, l0_lru_lambda, l0_lru_out_w),
                    (l1_fox_in_w, l1_fox_f_b, l1_fox_q_norm_g, l1_fox_k_norm_g, l1_fox_out_w)]
    ffn_norms = [(l0_ffn_norm_g, l0_ffn_mod_w, l0_ffn_mod_b), (l1_ffn_norm_g, l1_ffn_mod_w, l1_ffn_mod_b)]
    peer_params = [(l0_peer_q_w, l0_peer_subkey1, l0_peer_subkey2, l0_peer_u, l0_peer_v),
                   (l1_peer_q_w, l1_peer_subkey1, l1_peer_subkey2, l1_peer_u, l1_peer_v)]
    for layer in range(DEPTH_2):
        g, mw, mb = mix_norms[layer]
        shift, scale, gate = ada_modulation(c, mw, mb)
        h = rms_norm_2(x, g) * (1.0 + scale) + shift
        mixer = rglru_mixer if layer % N_MIXERS == 0 else fox_mixer
        x = x + gate * mixer(h, *mixer_params[layer])
        g, mw, mb = ffn_norms[layer]
        shift, scale, gate = ada_modulation(c, mw, mb)
        h = rms_norm_2(x, g) * (1.0 + scale) + shift
        x = x + gate * peer_ffn(h, *peer_params[layer])
    return x


def setup_inputs(seed=0):
    out = dict(first_inputs(seed))
    for name, value in second_inputs(seed + 1).items():
        if name != "x":
            out[name + "_2"] = value
    return out


def reference(
    x, norm1_g, w_in, diff_q_g, diff_k_g, lambda_q1, lambda_k1, lambda_q2, lambda_k2,
    diff_sub_g, moba_q_g, moba_k_g, rel_bias, w_out, norm2_g, router_group, router_expert,
    w_gate, w_up, w_down, c_2, l0_mix_norm_g_2, l0_mix_mod_w_2, l0_mix_mod_b_2, l0_lru_in_w_2,
    l0_lru_conv_w_2, l0_lru_conv_b_2, l0_lru_ra_w_2, l0_lru_ra_b_2, l0_lru_ri_w_2,
    l0_lru_ri_b_2, l0_lru_lambda_2, l0_lru_out_w_2, l0_ffn_norm_g_2, l0_ffn_mod_w_2,
    l0_ffn_mod_b_2, l0_peer_q_w_2, l0_peer_subkey1_2, l0_peer_subkey2_2, l0_peer_u_2,
    l0_peer_v_2, l1_mix_norm_g_2, l1_mix_mod_w_2, l1_mix_mod_b_2, l1_fox_in_w_2, l1_fox_f_b_2,
    l1_fox_q_norm_g_2, l1_fox_k_norm_g_2, l1_fox_out_w_2, l1_ffn_norm_g_2, l1_ffn_mod_w_2,
    l1_ffn_mod_b_2, l1_peer_q_w_2, l1_peer_subkey1_2, l1_peer_subkey2_2, l1_peer_u_2,
    l1_peer_v_2,
):
    x = first_block(
        x, norm1_g, w_in, diff_q_g, diff_k_g, lambda_q1, lambda_k1, lambda_q2, lambda_k2,
        diff_sub_g, moba_q_g, moba_k_g, rel_bias, w_out, norm2_g, router_group, router_expert,
        w_gate, w_up, w_down,
    )
    return second_block(
        x, c_2, l0_mix_norm_g_2, l0_mix_mod_w_2, l0_mix_mod_b_2, l0_lru_in_w_2, l0_lru_conv_w_2,
        l0_lru_conv_b_2, l0_lru_ra_w_2, l0_lru_ra_b_2, l0_lru_ri_w_2, l0_lru_ri_b_2,
        l0_lru_lambda_2, l0_lru_out_w_2, l0_ffn_norm_g_2, l0_ffn_mod_w_2, l0_ffn_mod_b_2,
        l0_peer_q_w_2, l0_peer_subkey1_2, l0_peer_subkey2_2, l0_peer_u_2, l0_peer_v_2,
        l1_mix_norm_g_2, l1_mix_mod_w_2, l1_mix_mod_b_2, l1_fox_in_w_2, l1_fox_f_b_2,
        l1_fox_q_norm_g_2, l1_fox_k_norm_g_2, l1_fox_out_w_2, l1_ffn_norm_g_2, l1_ffn_mod_w_2,
        l1_ffn_mod_b_2, l1_peer_q_w_2, l1_peer_subkey1_2, l1_peer_subkey2_2, l1_peer_u_2,
        l1_peer_v_2,
    )


_drawn_inputs = setup_inputs


def setup_inputs(seed=0):
    import zlib

    import numpy as np

    out = dict(_drawn_inputs(seed))
    spreads = {}
    factors = {'lambda_q1': 8.0,
     'moba_q_g': 3.332,
     'moba_k_g': 3.183,
     'l0_mix_norm_g_2': 2.948,
     'l0_lru_conv_b_2': 3.394,
     'l0_lru_ra_b_2': 8.0,
     'l0_lru_ri_b_2': 8.0,
     'l0_ffn_norm_g_2': 4.503,
     'l0_ffn_mod_b_2': 5.556,
     'l1_mix_norm_g_2': 8.0,
     'l1_mix_mod_b_2': 8.0,
     'l1_fox_f_b_2': 2.713,
     'l1_fox_q_norm_g_2': 8.0,
     'l1_fox_k_norm_g_2': 8.0,
     'l1_ffn_norm_g_2': 4.882,
     'l1_ffn_mod_b_2': 6.735}
    for name, (base, spread) in spreads.items():
        noise = np.random.default_rng([zlib.crc32(name.encode()), seed]).standard_normal(out[name].shape)
        drawn = base * np.exp(spread * noise) if base else spread * noise
        out[name] = __import__('jax').numpy.asarray(drawn.astype(out[name].dtype))
    for name, factor in factors.items():
        out[name] = (out[name] * factor).astype(out[name].dtype)
    return out
```

```python
import math
from contextlib import ExitStack

import numpy as np

import concourse.bass as bass
import concourse.mybir as mybir

ALU = mybir.AluOpType
ACT = mybir.ActivationFunctionType
AX = mybir.AxisListType.X
F32 = mybir.dt.float32
U32 = mybir.dt.uint32

P = 128
SEQ = 256
NT = SEQ // P
D = 1024
KD = D // P
BANK = 512
HD = 64
EPS = 1e-6
NEG = -1e30
N_BUCKETS = 32
MAX_DISTANCE = 2048
N_REL_HEADS = 12
DIFF_MAPS = 8
MAPS = 16
LAMBDA_INIT = 0.8 - 0.6 * math.exp(-0.3 * 0)
GROUPS, PER_GROUP = 4, 8
EXPERTS = GROUPS * PER_GROUP
HIDDEN = 256
MODS = 4
MODW = 3 * D
RNN = 128 * round(4 * D / (3 * 128))
LBLK = 16
LW = RNN // LBLK
CONV = 4
KEYS = 128
PHEADS = 8
TOPK = 16
PICKS = PHEADS * TOPK
CAUSAL = P + SEQ


def spread(ap, axis, n):
    a = ap.unsqueeze(axis)
    shape = list(a.shape)
    shape[axis] = n
    return a.to_broadcast(shape)


def wait_past(eng, sem, n):
    if not (isinstance(n, int) and n <= 0):
        eng.wait_ge(sem, n)


class Chain:

    def __init__(self, eng, sem):
        self.eng, self.sem, self.count = eng, sem, 0

    def step(self, ins):
        ins.then_inc(self.sem, 1)
        self.count += 1
        self.eng.wait_ge(self.sem, self.count)


class Core:

    def __init__(self, nc, ctx, dram):
        self.nc, self.dram, self.sems = nc, dram, []
        self.x = self.sbuf(ctx, "x", [P, NT, D])
        self.hT = self.sbuf(ctx, "hT", [P, KD, SEQ])
        self.ident = self.sbuf(ctx, "ident", [P, P])
        self.ones = self.sbuf(ctx, "ones", [P, P])
        self.psum = ctx.enter_context(nc.psum_tensor("psum", [P, 8, BANK], F32))

    def sbuf(self, ctx, name, shape, dt=F32):
        return ctx.enter_context(self.nc.sbuf_tensor(name, shape, dt))

    def sem(self, name):
        self.sems.append(self.nc.alloc_semaphore(name))
        return self.sems[-1]

    def free_sems(self):
        self.nc.clear_and_free_semaphores(self.sems)
        self.sems = []
        self.nc.all_engine_barrier()


class Norm:

    BANKS = 4

    def __init__(self, core, ctx, name, gain, mod=None):
        self.core, self.gain, self.mod = core, gain, mod
        self.g = core.sbuf(ctx, name + "_gain", [P, D])
        self.h = core.sbuf(ctx, name + "_h", [P, NT, D])
        self.stat = core.sbuf(ctx, name + "_stat", [P, 4, NT])
        if mod is not None:
            self.shift = core.sbuf(ctx, name + "_shift", [P, D])
            self.scale = core.sbuf(ctx, name + "_scale", [P, D])
        self.rows_landed = core.sem(name + "_rows_landed")
        self.squares_summed = core.sem(name + "_squares_summed")
        self.var_ready = core.sem(name + "_var_ready")
        self.std_ready = core.sem(name + "_std_ready")
        self.chain_sem = core.sem(name + "_dve_chain")
        self.h_ready = core.sem(name + "_h_ready")
        self.turned = core.sem(name + "_turned")
        self.hT_act = core.sem(name + "_hT_by_act")
        self.hT_dve = core.sem(name + "_hT_by_dve")

    def load(self, sp):
        sp.dma_start(self.g[:, :], self.gain.partition_broadcast(P)).then_inc(self.rows_landed, 16)
        if self.mod is not None:
            row = self.core.dram["mod_rows"][self.mod]
            sp.dma_start(self.shift[:, :], row[0:D].partition_broadcast(P)).then_inc(self.rows_landed, 16)
            sp.dma_start(self.scale[:, :], row[D:2 * D].partition_broadcast(P)).then_inc(self.rows_landed, 16)

    def bank(self, t, g):
        return self.core.psum[:, 2 * t + g, :].rearrange("p (k n) -> p k n", k=4)

    def act(self, act):
        x = self.core.x
        for t in range(NT):
            act.activation(self.h[:, t, :], x[:, t, :], ACT.Square,
                           accum_out=self.stat[:, 0, t:t + 1]).then_inc(self.squares_summed, 1)
        act.wait_ge(self.var_ready, 1)
        act.activation(self.stat[:, 2, :], self.stat[:, 1, :], ACT.Sqrt).then_inc(self.std_ready, 1)
        for t in range(NT):
            act.wait_ge(self.turned, 2 * t + 1)
            act.copy(self.core.hT[:, 0:4, t * P:(t + 1) * P], self.bank(t, 0)).then_inc(self.hT_act, 1)

    def dve(self, dve):
        chain = Chain(dve, self.chain_sem)
        dve.wait_ge(self.squares_summed, NT)
        dve.tensor_scalar(self.stat[:, 1, :], self.stat[:, 0, :], 1.0 / D, EPS,
                          ALU.mult, ALU.add).then_inc(self.var_ready, 1)
        dve.wait_ge(self.rows_landed, 16 if self.mod is None else 48)
        if self.mod is not None:
            chain.step(dve.scalar_tensor_tensor(self.g[:, :], self.scale[:, :], 1.0, self.g[:, :],
                                                ALU.add, ALU.mult))
        dve.wait_ge(self.std_ready, 1)
        chain.step(dve.reciprocal(self.stat[:, 3, :], self.stat[:, 2, :]))
        for t in range(NT):
            ins = dve.scalar_tensor_tensor(self.h[:, t, :], self.core.x[:, t, :], self.stat[:, 3, t:t + 1],
                                           self.g[:, :], ALU.mult, ALU.mult)
            if self.mod is not None:
                chain.step(ins)
                ins = dve.tensor_tensor(self.h[:, t, :], self.h[:, t, :], self.shift[:, :], ALU.add)
            ins.then_inc(self.h_ready, 1)
        for t in range(NT):
            dve.wait_ge(self.turned, 2 * t + 2)
            dve.tensor_copy(self.core.hT[:, 4:8, t * P:(t + 1) * P], self.bank(t, 1)).then_inc(self.hT_dve, 1)

    def pe(self, pe):
        for t in range(NT):
            pe.wait_ge(self.h_ready, t + 1)
            for g in range(2):
                for k in range(4):
                    c = (4 * g + k) * P
                    ins = pe.transpose(self.bank(t, g)[:, k, :], self.h[:, t, c:c + P], self.core.ident[:, :])
                ins.then_inc(self.turned, 1)

    def hT_done(self, eng):
        eng.wait_ge(self.hT_act, NT)
        eng.wait_ge(self.hT_dve, NT)


class Project:

    def __init__(self, core, ctx, name, w, lT, rows, blocks, chunks, evacuate, slots=3, first_bank=4):
        self.core, self.w, self.lT, self.rows, self.blocks = core, w, lT, rows, blocks
        self.chunks, self.evacuate, self.slots, self.first_bank = chunks, evacuate, slots, first_bank
        self.width = max(c[1] for c in chunks)
        self.buf = core.sbuf(ctx, name + "_w", [rows, slots, blocks, self.width])
        self.landed = [core.sem(f"{name}_w_landed{s}") for s in range(min(slots, len(chunks)))]
        self.product = core.sem(name + "_product")
        self.taken = [core.sem(f"{name}_taken{t}") for t in range(NT)]

    def load(self, sp):
        view = self.w.rearrange("(k p) c -> p k c", p=self.rows)
        for c, (c0, width) in enumerate(self.chunks):
            s = c % self.slots
            if c >= self.slots:
                sp.wait_ge(self.product, NT * (c - self.slots + 1))
            sp.dma_start(self.buf[:, s, :, 0:width], view[:, :, c0:c0 + width]).then_inc(self.landed[s], 16)

    def bank(self, c, t, width):
        return self.core.psum[:, self.first_bank + (NT * c + t) % 4, 0:width]

    def pe(self, pe):
        for c, (c0, width) in enumerate(self.chunks):
            s = c % self.slots
            pe.wait_ge(self.landed[s], 16 * (c // self.slots + 1))
            for t in range(NT):
                if c >= 2:
                    pe.wait_ge(self.taken[t], c - 1)
                for k in range(self.blocks):
                    ins = pe.matmul(self.bank(c, t, width), self.lT[:, k, t * P:(t + 1) * P],
                                    self.buf[:, s, k, 0:width], start=k == 0, stop=k == self.blocks - 1)
                ins.then_inc(self.product, 1)

    def take(self, eng, tiles):
        for c, (c0, width) in enumerate(self.chunks):
            for t in tiles:
                eng.wait_ge(self.product, NT * c + t + 1)
                self.evacuate(eng, c, c0, width, t, self.bank(c, t, width)).then_inc(self.taken[t], 1)


class ProjectT:

    PER = 4

    def __init__(self, core, ctx, name, w, m, blocks, evacuate, slots=3, first_bank=4):
        self.core, self.w, self.m, self.n = core, w, m, blocks
        self.evacuate, self.slots, self.first_bank = evacuate, slots, first_bank
        self.buf = core.sbuf(ctx, name + "_w", [P, slots, KD, self.PER * m])
        self.landed = [core.sem(f"{name}_w_landed{s}") for s in range(slots)]
        self.product = core.sem(name + "_product")
        self.taken = [core.sem(f"{name}_taken{j}") for j in range(2)]

    def load(self, sp):
        view = self.w.rearrange("(k p) c -> p k c", p=P)
        wide = self.PER * self.m
        for c in range(self.n // self.PER):
            if c >= self.slots:
                sp.wait_ge(self.product, self.PER // 2 * (c - self.slots + 1))
            sp.dma_start(self.buf[:, c % self.slots], view[:, :, c * wide:(c + 1) * wide])\
              .then_inc(self.landed[c % self.slots], 16)

    def bank(self, b):
        return self.core.psum[0:self.m, self.first_bank + b // 2 % 4, b % 2 * SEQ:(b % 2 + 1) * SEQ]

    def pe(self, pe):
        for b in range(self.n):
            c = b // self.PER
            if b % self.PER == 0:
                pe.wait_ge(self.landed[c % self.slots], 16 * (c // self.slots + 1))
            if b % 2 == 0 and b >= 8:
                pe.wait_ge(self.taken[b // 2 % 2], 2 * (b // 2 // 2 - 2) + 2)
            j = b % self.PER * self.m
            for k in range(KD):
                ins = pe.matmul(self.bank(b), self.buf[:, c % self.slots, k, j:j + self.m],
                                self.core.hT[:, k, :], start=k == 0, stop=k == KD - 1)
            if b % 2:
                ins.then_inc(self.product, 1)

    def take(self, eng, which):
        for b in range(self.n):
            if b // 2 % 2 == which:
                if b % 2 == 0:
                    eng.wait_ge(self.product, b // 2 + 1)
                self.evacuate(eng, b, self.bank(b)).then_inc(self.taken[which], 1)


def copy_on(eng, out, in_):
    return eng.copy(out, in_) if isinstance(eng, bass.BassScalarEngine) else eng.tensor_copy(out, in_)


class Attention:

    def __init__(self, core, ctx, name, proj, qk, value, bias, lam=None, decay=None, sub_gain=None, gate=None):
        self.core, self.proj, self.qk, self.value, self.bias = core, proj, qk, value, bias
        self.lam, self.decay, self.sub_gain, self.gate = lam, decay, sub_gain, gate
        sb = lambda n, s: core.sbuf(ctx, name + "_" + n, s)
        self.squares = sb("squares", [P, 2, BANK])
        self.stat = sb("stat", [P, 4, NT, 4, 8])
        self.gains = sb("gains", [P, 4, HD])
        self.qT = sb("qT", [P, 8, SEQ])
        self.kT = sb("kT", [P, 8, SEQ])
        self.probs = sb("probs", [P, 2, CAUSAL])
        self.probsT = sb("probsT", [P, 2, CAUSAL])
        self.negmax = sb("negmax", [P, MAPS, NT])
        self.rowsum = sb("rowsum", [P, MAPS, NT])
        self.inv = sb("inv", [P, MAPS, NT])
        self.y = sb("y", [P, NT, D])
        self.yT = sb("yT", [P, KD, SEQ])
        s = lambda n: core.sem(name + "_" + n)
        self.gains_landed, self.gains_ready = s("gains_landed"), s("gains_ready")
        self.squared, self.summed, self.var_ready, self.std_ready = s("squared"), s("summed"), s("var_ready"), s("std_ready")
        self.scaled, self.normed, self.turned = s("scaled"), s("normed"), s("turned")
        self.qkT_act, self.qkT_dve = s("qkT_by_act"), s("qkT_by_dve")
        self.chain_sem = s("dve_chain")
        self.score_done, self.exped = s("score_done"), s("exped")
        self.p_turned, self.pT_ready, self.pv_done, self.y_part = s("p_turned"), s("pT_ready"), s("pv_done"), s("y_part")
        self.maxed = s("maxed")
        self.y_ready, self.y_turned, self.yT_act, self.yT_dve = s("y_ready"), s("y_turned"), s("yT_by_act"), s("yT_by_dve")
        if sub_gain is not None:
            self.sub_sum, self.sub_std = s("sub_sum"), s("sub_std")
            self.sub = sb("sub", [P, 4, NT, 4])

    def load(self, sp):
        for g, (_, gain, _) in enumerate(self.qk):
            sp.dma_start(self.gains[:, g, :], gain.partition_broadcast(P)).then_inc(self.gains_landed, 16)

    def group(self, t, g):
        c = self.qk[g][0]
        return self.proj[:, t, c:c + BANK].rearrange("p (h d) -> p h d", h=8)

    def pool(self, pool):
        pool.wait_ge(self.gains_landed, 64)
        for g, (_, _, query) in enumerate(self.qk):
            pool.tensor_scalar(self.gains[:, g, :], self.gains[:, g, :], HD ** -0.5 if query else 1.0, None,
                               ALU.mult).then_inc(self.gains_ready, 1)
        pool.wait_ge(self.gains_ready, 4)
        for n in range(NT * 4):
            t, g = n // 4, n % 4
            pool.wait_ge(self.scaled, n + 1)
            v = self.group(t, g)
            pool.tensor_tensor(v, v, spread(self.gains[:, g, :], 1, 8), ALU.mult).then_inc(self.normed, 1)

    def act(self, act):
        for n in range(NT * 4):
            t, g = n // 4, n % 4
            if n >= 2:
                act.wait_ge(self.summed, n - 1)
            act.activation(self.squares[:, n % 2, :].rearrange("p (h d) -> p h d", h=8), self.group(t, g),
                           ACT.Square).then_inc(self.squared, 1)
        act.wait_ge(self.var_ready, 1)
        act.activation(self.stat[:, 2], self.stat[:, 1], ACT.Sqrt).then_inc(self.std_ready, 1)
        for n in range(0, NT * 4, 2):
            act.wait_ge(self.turned, n + 1)
            copy_on(act, self.turned_dst(n), self.turned_src(n)).then_inc(self.qkT_act, 1)
        for i in range(MAPS + 1):
            if i < MAPS:
                act.wait_ge(self.maxed, i + 1)
                if i >= 2:
                    act.wait_ge(self.p_turned, i - 1)
                for t in range(NT):
                    a, b = (0, P) if t == 0 else (P, CAUSAL)
                    ins = act.activation(self.probs[:, i % 2, a:b], self.core.psum[:, i % 2, a:b], ACT.Exp,
                                         bias=self.negmax[:, i, t:t + 1],
                                         accum_out=self.rowsum[:, i, t:t + 1])
                    ins.then_inc(self.exped, 1)
            if i >= 1:
                h = i - 1
                act.wait_ge(self.p_turned, h + 1)
                if h >= 2:
                    act.wait_ge(self.pv_done, h - 1)
                act.copy(self.probsT[:, h % 2, :], self.core.psum[:, 2 + h % 2, 0:CAUSAL]).then_inc(self.pT_ready, 1)
        if self.sub_gain is not None:
            act.wait_ge(self.sub_sum, 1)
            act.activation(self.sub[:, 2], self.sub[:, 1], ACT.Sqrt).then_inc(self.sub_std, 1)
        for n in range(0, 4, 2):
            act.wait_ge(self.y_turned, n + 1)
            act.copy(self.yT_dst(n), self.turned_src(n)).then_inc(self.yT_act, 1)

    def turned_src(self, n):
        return self.core.psum[:, n, :].rearrange("p (j q) -> p j q", j=4)

    def turned_dst(self, n):
        t, g = n // 4, n % 4
        dst = self.qT if self.qk[g][2] else self.kT
        half = [j for j in range(4) if self.qk[j][2] == self.qk[g][2]].index(g)
        return dst[:, 4 * half:4 * half + 4, t * P:(t + 1) * P]

    def yT_dst(self, n):
        t, g = n // 2, n % 2
        return self.yT[:, 4 * g:4 * g + 4, t * P:(t + 1) * P]

    def out(self, h, t):
        if self.lam is not None and h < DIFF_MAPS:
            w, c = 2 * HD, (h // 2) * 2 * HD
        else:
            w, c = HD, h * HD
        return self.core.psum[:, 4 + h % 2, t * P:t * P + w], self.y[:, t, c:c + w]

    def dve(self, dve):
        chain = Chain(dve, self.chain_sem)
        for n in range(NT * 4):
            t, g = n // 4, n % 4
            dve.wait_ge(self.squared, n + 1)
            dve.tensor_reduce(self.stat[:, 0, t, g, :], self.squares[:, n % 2, :].rearrange("p (h d) -> p h d", h=8),
                              AX, ALU.add).then_inc(self.summed, 1)
        dve.wait_ge(self.summed, 8)
        dve.tensor_scalar(self.stat[:, 1], self.stat[:, 0], 1.0 / HD, EPS, ALU.mult, ALU.add).then_inc(self.var_ready, 1)
        dve.wait_ge(self.std_ready, 1)
        chain.step(dve.reciprocal(self.stat[:, 3], self.stat[:, 2]))
        for n in range(NT * 4):
            t, g = n // 4, n % 4
            v = self.group(t, g)
            dve.tensor_tensor(v, v, spread(self.stat[:, 3, t, g, :], 2, HD), ALU.mult).then_inc(self.scaled, 1)
        for n in range(1, NT * 4, 2):
            dve.wait_ge(self.turned, n + 1)
            dve.tensor_copy(self.turned_dst(n), self.turned_src(n)).then_inc(self.qkT_dve, 1)
        for i in range(MAPS + 2):
            if i < MAPS:
                dve.wait_ge(self.score_done, i + 1)
                for t in range(NT):
                    a, b = (0, P) if t == 0 else (P, CAUSAL)
                    ins = dve.tensor_reduce(self.negmax[:, i, t:t + 1], self.core.psum[:, i % 2, a:b], AX, ALU.max,
                                            negate=True)
                ins.then_inc(self.maxed, 1)
            if i >= 2:
                h = i - 2
                dve.wait_ge(self.exped, 2 * (h + 1))
                chain.step(dve.reciprocal(self.inv[:, h, :], self.rowsum[:, h, :]))
                second = self.lam is not None and h < DIFF_MAPS and h % 2 == 1
                if second:
                    chain.step(dve.tensor_scalar(self.inv[:, h, :], self.inv[:, h, :], self.lam, None, ALU.mult))
                dve.wait_ge(self.pv_done, h + 1)
                for t in range(NT):
                    o, y = self.out(h, t)
                    if second:
                        dve.wait_ge(self.y_part, h)
                        ins = dve.scalar_tensor_tensor(y, o, self.inv[:, h, t:t + 1], y, ALU.mult, ALU.add)
                    else:
                        ins = dve.tensor_scalar(y, o, self.inv[:, h, t:t + 1], None, ALU.mult)
                ins.then_inc(self.y_part, 1)
        dve.wait_ge(self.y_part, MAPS)
        if self.sub_gain is not None:
            for t in range(NT):
                v = self.y[:, t, 0:BANK].rearrange("p (h d) -> p h d", h=4)
                sq = self.squares[:, t, :].rearrange("p (h d) -> p h d", h=4)
                chain.step(dve.tensor_tensor(sq, v, v, ALU.mult))
                chain.step(dve.tensor_reduce(self.sub[:, 0, t, :], sq, AX, ALU.add))
            dve.tensor_scalar(self.sub[:, 1], self.sub[:, 0], 1.0 / (2 * HD), EPS, ALU.mult, ALU.add)\
               .then_inc(self.sub_sum, 1)
            dve.wait_ge(self.sub_std, 1)
            chain.step(dve.reciprocal(self.sub[:, 3], self.sub[:, 2]))
            chain.step(dve.tensor_scalar(self.sub[:, 3], self.sub[:, 3], 1.0 - LAMBDA_INIT, None, ALU.mult))
            for t in range(NT):
                v = self.y[:, t, 0:BANK].rearrange("p (h d) -> p h d", h=4)
                chain.step(dve.tensor_tensor(v, v, spread(self.sub[:, 3, t, :], 2, 2 * HD), ALU.mult))
                dve.tensor_tensor(v, v, spread(self.sub_gain, 1, 4), ALU.mult).then_inc(self.y_ready, 1)
        elif self.gate is not None:
            for t in range(NT):
                dve.tensor_tensor(self.y[:, t, :], self.y[:, t, :], self.gate(dve, t), ALU.mult)\
                   .then_inc(self.y_ready, 1)
        for n in range(1, 4, 2):
            dve.wait_ge(self.y_turned, n + 1)
            dve.tensor_copy(self.yT_dst(n), self.turned_src(n)).then_inc(self.yT_dve, 1)

    def pe(self, pe):
        ident = self.core.ident
        for n in range(NT * 4):
            t, g = n // 4, n % 4
            pe.wait_ge(self.normed, n + 1)
            c = self.qk[g][0]
            for j in range(4):
                ins = pe.transpose(self.turned_src(n)[:, j, :], self.proj[:, t, c + j * P:c + (j + 1) * P], ident[:, :])
            ins.then_inc(self.turned, 1)
        pe.wait_ge(self.qkT_act, 4)
        pe.wait_ge(self.qkT_dve, 4)
        for i in range(MAPS + 2):
            if i < MAPS:
                if i >= 2:
                    pe.wait_ge(self.exped, 2 * (i - 1))
                a = i % 2 * HD
                for t in range(NT):
                    n = P * (t + 1)
                    out = self.core.psum[:, i % 2, P * t:P * t + n]
                    turn, tile = self.bias(i)
                    pe.matmul(out, turn[:, :], tile[:, P * t:P * t + n], start=True, stop=False)
                    ins = pe.matmul(out, self.qT[a:a + HD, i // 2, t * P:(t + 1) * P], self.kT[a:a + HD, i // 2, 0:n],
                                    start=False, stop=self.decay is None)
                    if self.decay is not None:
                        left, right = self.decay
                        ins = pe.matmul(out, left[:, i, t * P:(t + 1) * P], right[:, i, 0:n], start=False, stop=True)
                ins.then_inc(self.score_done, 1)
            if 1 <= i <= MAPS:
                h = i - 1
                pe.wait_ge(self.exped, 2 * (h + 1))
                if h >= 2:
                    pe.wait_ge(self.pT_ready, h - 1)
                for j in range(3):
                    ins = pe.transpose(self.core.psum[:, 2 + h % 2, j * P:(j + 1) * P],
                                       self.probs[:, h % 2, j * P:(j + 1) * P], ident[:, :])
                ins.then_inc(self.p_turned, 1)
            if i >= 2:
                h = i - 2
                pe.wait_ge(self.pT_ready, h + 1)
                if h >= 2:
                    pe.wait_ge(self.y_part, h - 1)
                pt = self.probsT[:, h % 2, :].rearrange("p (j q) -> p j q", j=3)
                pe.matmul(self.out(h, 0)[0], pt[:, 0, :], self.value(h, 0), start=True, stop=True)
                pe.matmul(self.out(h, 1)[0], pt[:, 1, :], self.value(h, 0), start=True, stop=False)
                pe.matmul(self.out(h, 1)[0], pt[:, 2, :], self.value(h, 1), start=False, stop=True)\
                  .then_inc(self.pv_done, 1)
        for n in range(4):
            t, g = n // 2, n % 2
            pe.wait_ge(self.y_ready, t + 1)
            for j in range(4):
                c = (4 * g + j) * P
                ins = pe.transpose(self.turned_src(n)[:, j, :], self.y[:, t, c:c + P], ident[:, :])
            ins.then_inc(self.y_turned, 1)
        pe.wait_ge(self.yT_act, 2)
        pe.wait_ge(self.yT_dve, 2)


def column_chunks(first, last):
    return [(c, min(BANK, last - c)) for c in range(first, last, BANK)]


def stage_start(core):
    nc, d = core.nc, core.dram
    landed, ones_set = core.sem("start_landed"), core.sem("ones_set")
    with nc.Block() as block:
        @block.sync
        def _(sp):
            sp.dma_start(core.x[:, :, :], d["x"].rearrange("b (t p) c -> p (b t) c", p=P)).then_inc(landed, 16)
            sp.dma_start(core.ident[:, :], d["c_ident"]).then_inc(landed, 16)
            sp.wait_ge(landed, 32)

        @block.vector
        def _(dve):
            dve.memset(core.ones[:, :], 1.0).then_inc(ones_set, 1)
            dve.wait_ge(ones_set, 1)


def stage_mix1(core):
    nc, d = core.nc, core.dram
    with ExitStack() as ctx:
        width = 3 * D
        proj = core.sbuf(ctx, "mix1_proj", [P, NT, width])
        bias = core.sbuf(ctx, "rel_bias_tiles", [P, N_REL_HEADS, CAUSAL])
        flip = core.sbuf(ctx, "flip", [P, P])
        with ExitStack() as inner:
            norm = Norm(core, inner, "norm1", d["norm1_g"][0])
            table = core.sbuf(inner, "rel_table", [N_BUCKETS + 1, N_REL_HEADS])
            buckets = core.sbuf(inner, "bucket_onehot", [N_BUCKETS + 1, BANK])
            curve = core.sbuf(inner, "bias_curve", [N_REL_HEADS, BANK])
            table_landed, mask_row = core.sem("rel_table_landed"), core.sem("rel_mask_row")
            curve_done, curve_copied = core.sem("curve_done"), core.sem("curve_copied")
            curve_stored, bias_landed = core.sem("curve_stored"), core.sem("bias_landed")

            def take(eng, c, c0, w, t, src):
                return copy_on(eng, proj[:, t, c0:c0 + w], src)

            win = Project(core, inner, "w_in", d["w_in"][0], core.hT, P, KD, column_chunks(0, width), take)
            with nc.Block() as block:
                @block.sync
                def _(sp):
                    norm.load(sp)
                    sp.dma_start(table[0:N_BUCKETS, :], d["rel_bias"]).then_inc(table_landed, 16)
                    sp.dma_start(flip[:, :], d["c_flip"]).then_inc(table_landed, 16)
                    sp.dma_start(buckets[:, :], d["c_buckets"]).then_inc(table_landed, 16)
                    win.load(sp)

                @block.gpsimd
                def _(pool):
                    pool.memset(table[N_BUCKETS:N_BUCKETS + 1, :], NEG).then_inc(mask_row, 1)
                    pool.wait_ge(curve_copied, 1)
                    pool.dma_start(d["curve"], curve[:, :]).then_inc(curve_stored, 16)
                    pool.wait_ge(curve_stored, 16)
                    t = d["curve"]
                    for tile in range(NT):
                        src = bass.AP(t.tensor, SEQ - (tile + 1) * P, [[1, P], [BANK, N_REL_HEADS], [1, P * (tile + 1)]])
                        pool.dma_start(bias[:, :, tile * P:tile * P + P * (tile + 1)], src).then_inc(bias_landed, 16)
                    pool.wait_ge(bias_landed, 32)

                @block.scalar
                def _(act):
                    norm.act(act)
                    win.take(act, [1])

                @block.vector
                def _(dve):
                    dve.wait_ge(curve_done, 1)
                    dve.tensor_copy(curve[:, :], core.psum[0:N_REL_HEADS, 4, :]).then_inc(curve_copied, 1)
                    norm.dve(dve)
                    win.take(dve, [0])

                @block.tensor
                def _(pe):
                    pe.wait_ge(table_landed, 48)
                    pe.wait_ge(mask_row, 1)
                    pe.matmul(core.psum[0:N_REL_HEADS, 4, :], table[:, :], buckets[:, :], start=True, stop=True)\
                      .then_inc(curve_done, 1)
                    norm.pe(pe)
                    norm.hT_done(pe)
                    pe.wait_ge(curve_copied, 1)
                    win.pe(pe)

        lam_rows = core.sbuf(ctx, "lambda_rows", [P, 4, HD])
        lam = core.sbuf(ctx, "lambda", [P, 4])
        subg = core.sbuf(ctx, "diff_sub_gain", [P, 2 * HD])
        rows_landed, lam_dot, lam_exp, lam_chain = (core.sem("lambda_rows_landed"), core.sem("lambda_dot"),
                                                    core.sem("lambda_exp"), core.sem("lambda_chain"))
        qk = [(0, d["diff_q_g"][0], True), (D // 2, d["diff_k_g"][0], False),
              (3 * D // 2, d["moba_q_g"][0], True), (2 * D, d["moba_k_g"][0], False)]

        def value(h, t):
            if h < DIFF_MAPS:
                return proj[:, t, D + (h // 2) * 2 * HD:D + (h // 2 + 1) * 2 * HD]
            c = 5 * D // 2 + (h - DIFF_MAPS) * HD
            return proj[:, t, c:c + HD]

        def bias_of(h):
            return flip, bias[:, h // 2 if h < DIFF_MAPS else h - DIFF_MAPS + 4, :]

        att = Attention(core, ctx, "mix1", proj, qk, value, bias_of, lam=lam[:, 3:4], sub_gain=subg[:, :])

        def add(eng, c, c0, w, t, src):
            return eng.tensor_tensor(core.x[:, t, c0:c0 + w], src, core.x[:, t, c0:c0 + w], ALU.add)

        wout = Project(core, ctx, "w_out", d["w_out"][0], att.yT, P, KD, column_chunks(0, D), add, slots=2)
        with nc.Block() as block:
            @block.sync
            def _(sp):
                att.load(sp)
                for n, name in enumerate(("lambda_q1", "lambda_k1", "lambda_q2", "lambda_k2")):
                    sp.dma_start(lam_rows[:, n, :], d[name][0].partition_broadcast(P)).then_inc(rows_landed, 16)
                sp.dma_start(subg[:, :], d["diff_sub_g"][0].partition_broadcast(P)).then_inc(rows_landed, 16)
                wout.load(sp)

            @block.gpsimd
            def _(pool):
                att.pool(pool)

            @block.scalar
            def _(act):
                act.wait_ge(lam_dot, 1)
                act.activation(lam[:, 0:2], lam[:, 0:2], ACT.Exp).then_inc(lam_exp, 1)
                att.act(act)

            @block.vector
            def _(dve):
                chain = Chain(dve, lam_chain)
                dve.wait_ge(rows_landed, 80)
                pairs = lam_rows[:, :, :].rearrange("p (a b) d -> p b a d", b=2)
                chain.step(dve.tensor_tensor(pairs[:, 0], pairs[:, 0], pairs[:, 1], ALU.mult))
                dve.tensor_reduce(lam[:, 0:2], pairs[:, 0], AX, ALU.add).then_inc(lam_dot, 1)
                dve.wait_ge(lam_exp, 1)
                chain.step(dve.tensor_tensor(lam[:, 2:3], lam[:, 1:2], lam[:, 0:1], ALU.subtract))
                chain.step(dve.tensor_scalar(lam[:, 3:4], lam[:, 2:3], -LAMBDA_INIT, None, ALU.add))
                att.dve(dve)
                wout.take(dve, [0, 1])

            @block.tensor
            def _(pe):
                att.pe(pe)
                wout.pe(pe)


def stage_moe(core):
    nc, d = core.nc, core.dram
    SLOTS = 4
    STEPS = EXPERTS // SLOTS
    with ExitStack() as ctx:
        route = core.sbuf(ctx, "route_w", [P, KD, GROUPS + EXPERTS])
        cw = core.sbuf(ctx, "combine_w", [P, NT, EXPERTS])
        with ExitStack() as inner:
            norm = Norm(core, inner, "norm2", d["norm2_g"][0])
            L = core.sbuf(inner, "route_logits", [P, NT, GROUPS + EXPERTS])
            rev = core.sbuf(inner, "route_rev", [P, PER_GROUP])
            small = core.sbuf(inner, "route_small", [P, 16, NT])
            g4 = core.sbuf(inner, "route_g4", [P, 4, NT, GROUPS])
            g8 = core.sbuf(inner, "route_g8", [P, 8, NT, PER_GROUP])
            masked = core.sbuf(inner, "route_masked", [P, NT, EXPERTS])
            route_landed, logits_done = core.sem("route_landed"), core.sem("route_logits_done")
            rc, to_exp, exp_done = core.sem("route_chain"), core.sem("route_to_exp"), core.sem("route_exp_done")
            with nc.Block() as block:
                @block.sync
                def _(sp):
                    norm.load(sp)
                    sp.dma_start(route[:, :, :], d["router"]).then_inc(route_landed, 16)
                    sp.dma_start(rev[:, :], d["c_rev"]).then_inc(route_landed, 16)

                @block.tensor
                def _(pe):
                    norm.pe(pe)
                    norm.hT_done(pe)
                    pe.wait_ge(route_landed, 32)
                    for t in range(NT):
                        for k in range(KD):
                            ins = pe.matmul(core.psum[:, 4 + t, 0:GROUPS + EXPERTS], core.hT[:, k, t * P:(t + 1) * P],
                                            route[:, k, :], start=k == 0, stop=k == KD - 1)
                    ins.then_inc(logits_done, 1)

                @block.scalar
                def _(act):
                    norm.act(act)
                    for n, v in enumerate((g4[:, 3], small[:, 5])):
                        act.wait_ge(to_exp, n + 1)
                        act.activation(v, v, ACT.Exp).then_inc(exp_done, 1)

                @block.vector
                def _(dve):
                    norm.dve(dve)
                    chain = Chain(dve, rc)
                    TT = lambda o, a, b, op: chain.step(dve.tensor_tensor(o, a, b, op))
                    RED = lambda o, a, op: chain.step(dve.tensor_reduce(o, a, AX, op))

                    def first_max(v, top, tmp, pos, onehot, n):
                        RED(top, v, ALU.max)
                        TT(tmp, v, spread(top, 2, n), ALU.is_equal)
                        TT(tmp, tmp, spread(rev[:, PER_GROUP - n:PER_GROUP], 1, NT), ALU.mult)
                        RED(pos, tmp, ALU.max)
                        TT(onehot, tmp, spread(pos, 2, n), ALU.is_equal)

                    dve.wait_ge(logits_done, 1)
                    chain.step(dve.tensor_copy(L[:, :, :], core.psum[:, 4:4 + NT, 0:GROUPS + EXPERTS]))
                    gl = L[:, :, 0:GROUPS]
                    gtop = small[:, 0]
                    group = g4[:, 1]
                    first_max(gl, gtop, g4[:, 0], small[:, 1], group, GROUPS)
                    dve.tensor_tensor(g4[:, 3], gl, spread(gtop, 2, GROUPS), ALU.subtract).then_inc(to_exp, 1)
                    dve.wait_ge(exp_done, 1)
                    RED(small[:, 2], g4[:, 3], ALU.add)
                    chain.step(dve.reciprocal(small[:, 2], small[:, 2]))
                    el = L[:, :, GROUPS:].rearrange("p t (g e) -> p t g e", g=GROUPS)
                    mk = masked[:, :, :].rearrange("p t (g e) -> p t g e", g=GROUPS)
                    for t in range(NT):
                        TT(mk[:, t], el[:, t], spread(group[:, t], 2, PER_GROUP), ALU.mult)
                        RED(g8[:, 0, t], mk[:, t].rearrange("p g e -> p e g"), ALU.add)
                    first_max(g8[:, 0], small[:, 3], g8[:, 1], small[:, 4], g8[:, 2], PER_GROUP)
                    chain.step(dve.scalar_tensor_tensor(g8[:, 3], g8[:, 2], NEG, g8[:, 0], ALU.mult, ALU.add))
                    first_max(g8[:, 3], small[:, 6], g8[:, 4], small[:, 4], g8[:, 5], PER_GROUP)
                    dve.tensor_tensor(small[:, 5], small[:, 6], small[:, 3], ALU.subtract).then_inc(to_exp, 1)
                    dve.wait_ge(exp_done, 2)
                    chain.step(dve.tensor_scalar(small[:, 7], small[:, 5], 1.0, None, ALU.add))
                    chain.step(dve.reciprocal(small[:, 8], small[:, 7]))
                    TT(small[:, 8], small[:, 8], small[:, 2], ALU.mult)
                    TT(small[:, 9], small[:, 8], small[:, 5], ALU.mult)
                    TT(g8[:, 2], g8[:, 2], spread(small[:, 8], 2, PER_GROUP), ALU.mult)
                    TT(g8[:, 5], g8[:, 5], spread(small[:, 9], 2, PER_GROUP), ALU.mult)
                    TT(g8[:, 6], g8[:, 2], g8[:, 5], ALU.add)
                    for t in range(NT):
                        TT(cw[:, t, :].rearrange("p (g e) -> p g e", g=GROUPS), spread(g8[:, 6, t], 1, GROUPS),
                           spread(group[:, t], 2, PER_GROUP), ALU.mult)

        up = core.sbuf(ctx, "moe_gate_up", [P, SLOTS, KD, 2 * HIDDEN])
        down = core.sbuf(ctx, "moe_down", [P, SLOTS, HIDDEN // P, D])
        silu = core.sbuf(ctx, "moe_silu", [P, NT, HIDDEN])
        hid = core.sbuf(ctx, "moe_hid", [P, NT, HIDDEN])
        hidT = core.sbuf(ctx, "moe_hidT", [P, NT, HIDDEN // P, P])
        zero = core.sbuf(ctx, "moe_zero", [P, P])
        acc = core.sbuf(ctx, "mod_acc", [P, MODS, MODW])
        modw = core.sbuf(ctx, "mod_w", [P, 2, MODW])
        modc = core.sbuf(ctx, "mod_c", [P, KD])
        up_landed = [core.sem(f"moe_up_landed{s}") for s in range(SLOTS)]
        down_landed = [core.sem(f"moe_down_landed{s}") for s in range(SLOTS)]
        mod_added = core.sem("mod_added")
        per_tile = lambda n: [core.sem(f"moe_{n}{t}") for t in range(NT)]
        gu_done, silu_done, hid_done = per_tile("gu_done"), per_tile("silu_done"), per_tile("hid_done")
        hid_turned, hidT_ready, down_done = per_tile("hid_turned"), per_tile("hidT_ready"), per_tile("down_done")
        zeroed, y_done, added = core.sem("moe_zeroed"), core.sem("moe_y_done"), core.sem("moe_added")
        modw_landed = [core.sem(f"mod_w_landed{s}") for s in range(2)]
        modc_landed, modc_ready = core.sem("mod_c_landed"), core.sem("mod_c_ready")

        GU = lambda t: core.psum[:, t, :]
        TP = lambda t: core.psum[:, 2 + t, 0:HIDDEN].rearrange("p (j n) -> p j n", j=HIDDEN // P)
        Y = lambda t, c: core.psum[:, 4 + 2 * t + c, :]

        with nc.Block() as block:
            @block.sync
            def _(sp):
                sp.dma_start(modc[:, :], d["c_col"]).then_inc(modc_landed, 16)

                def load(i, first=False):
                    for s in range(SLOTS):
                        e = i * SLOTS + s
                        if not first:
                            sp.wait_ge(gu_done[NT - 1], e - SLOTS + 1)
                        for part, name in enumerate(("w_gate", "w_up")):
                            src = d[name][0].rearrange("e (k p) c -> p (e k) c", p=P)[:, bass.ds(e * KD, KD), :]
                            sp.dma_start(up[:, s, :, part * HIDDEN:(part + 1) * HIDDEN], src).then_inc(up_landed[s], 16)
                        if not first:
                            sp.wait_ge(down_done[NT - 1], e - SLOTS + 1)
                        src = d["w_down"][0].rearrange("e (j p) c -> p (e j) c", p=P)[:, bass.ds(e * (HIDDEN // P), HIDDEN // P), :]
                        sp.dma_start(down[:, s], src).then_inc(down_landed[s], 16)
                        if not first or s >= 2:
                            sp.wait_ge(mod_added, e - 1)
                        sp.dma_start(modw[:, s % 2, :], d["mod_w"][s][bass.ds(i * P, P), :]).then_inc(modw_landed[s % 2], 16)

                load(0, first=True)
                with sp.Fori(1, STEPS) as i:
                    load(i)

            @block.tensor
            def _(pe):
                pe.wait_ge(zeroed, 1)
                for t in range(NT):
                    for c in range(2):
                        pe.matmul(Y(t, c), zero[:, :], core.hT[:, 0:2, :].rearrange("p k n -> p (k n)"),
                                  start=True, stop=False)

                def gate_up(e, i, s, t):
                    if t == 0:
                        pe.wait_ge(up_landed[s], 32 * i + 32)
                    wait_past(pe, hid_done[t], e)
                    for k in range(KD):
                        ins = pe.matmul(GU(t), core.hT[:, k, t * P:(t + 1) * P], up[:, s, k, :],
                                        start=k == 0, stop=k == KD - 1)
                    ins.then_inc(gu_done[t], 1)

                def turn(e, t):
                    pe.wait_ge(hid_done[t], e + 1)
                    wait_past(pe, hidT_ready[t], e)
                    for j in range(HIDDEN // P):
                        ins = pe.transpose(TP(t)[:, j, :], hid[:, t, j * P:(j + 1) * P], core.ident[:, :])
                    ins.then_inc(hid_turned[t], 1)

                def project_down(e, i, s, t):
                    if t == 0:
                        pe.wait_ge(down_landed[s], 16 * i + 16)
                    pe.wait_ge(hidT_ready[t], e + 1)
                    for j in range(HIDDEN // P):
                        for c in range(2):
                            ins = pe.matmul(Y(t, c), hidT[:, t, j, :], down[:, s, j, c * BANK:(c + 1) * BANK],
                                            start=False, stop=False)
                    ins.then_inc(down_done[t], 1)

                def step(i):
                    for s in range(SLOTS):
                        e = i * SLOTS + s
                        gate_up(e, i, s, 0)
                        if s:
                            project_down(e - 1, i, s - 1, 1)
                        turn(e, 0)
                        gate_up(e, i, s, 1)
                        project_down(e, i, s, 0)
                        turn(e, 1)
                    project_down(i * SLOTS + SLOTS - 1, i, SLOTS - 1, 1)

                step(0)
                with pe.Fori(1, STEPS) as i:
                    step(i)
                for t in range(NT):
                    for c in range(2):
                        ins = pe.matmul(Y(t, c), zero[:, :], core.hT[:, 0:2, :].rearrange("p k n -> p (k n)"),
                                        start=False, stop=True)
                ins.then_inc(y_done, 1)

            @block.scalar
            def _(act):
                act.wait_ge(modc_landed, 16)
                act.activation(modc[:, :], modc[:, :], ACT.Silu).then_inc(modc_ready, 1)
                def step(i):
                    for s in range(SLOTS):
                        e = i * SLOTS + s
                        for t in range(NT):
                            act.wait_ge(gu_done[t], e + 1)
                            wait_past(act, hid_done[t], e)
                            act.activation(silu[:, t, :], GU(t)[:, 0:HIDDEN], ACT.Silu).then_inc(silu_done[t], 1)
                            act.wait_ge(hid_turned[t], e + 1)
                            wait_past(act, down_done[t], e)
                            act.copy(hidT[:, t], TP(t)).then_inc(hidT_ready[t], 1)

                step(0)
                with act.Fori(1, STEPS) as i:
                    step(i)

            @block.vector
            def _(dve):
                dve.memset(zero[:, :], 0.0).then_inc(zeroed, 1)
                dve.memset(acc[:, :, :], 0.0).then_inc(zeroed, 1)
                dve.wait_ge(zeroed, 2)
                dve.wait_ge(modc_ready, 1)
                def step(i):
                    for s in range(SLOTS):
                        e = i * SLOTS + s
                        for t in range(NT):
                            dve.wait_ge(silu_done[t], e + 1)
                            wait_past(dve, hid_turned[t], e)
                            dve.scalar_tensor_tensor(hid[:, t, :], GU(t)[:, HIDDEN:], cw[:, t, bass.ds(e, 1)],
                                                     silu[:, t, :], ALU.mult, ALU.mult).then_inc(hid_done[t], 1)
                        dve.wait_ge(modw_landed[s % 2], 32 * i + 16 * (s // 2) + 16)
                        wait_past(dve, mod_added, e)
                        dve.scalar_tensor_tensor(acc[:, s, :], modw[:, s % 2, :], modc[:, bass.ds(i, 1)],
                                                 acc[:, s, :], ALU.mult, ALU.add).then_inc(mod_added, 1)

                step(0)
                with dve.Fori(1, STEPS) as i:
                    step(i)
                dve.wait_ge(y_done, 1)
                for t in range(NT):
                    for c in range(2):
                        x = core.x[:, t, c * BANK:(c + 1) * BANK]
                        dve.tensor_tensor(x, Y(t, c), x, ALU.add).then_inc(added, 1)
                dve.wait_ge(added, 4)
                dve.wait_ge(mod_added, EXPERTS)

        b_landed, b_added, summed, rows_ready, rows_stored = (core.sem("mod_b_landed"), core.sem("mod_b_added"),
            core.sem("mod_summed"), core.sem("mod_rows_ready"), core.sem("mod_rows_stored"))
        NC = MODW // BANK
        with nc.Block() as block:
            @block.sync
            def _(sp):
                for m in range(MODS):
                    if m >= 2:
                        sp.wait_ge(b_added, m - 1)
                    sp.dma_start(modw[0:1, m % 2, :], d["mod_b"][m].unsqueeze(0)).then_inc(b_landed, 16)
                    sp.wait_ge(b_landed, 16 * m + 16)
                for m in range(MODS):
                    sp.wait_ge(rows_ready, NC * (m + 1))
                    sp.dma_start(d["mod_rows"][m].unsqueeze(0), acc[0:1, m, :]).then_inc(rows_stored, 16)
                sp.wait_ge(rows_stored, 16 * MODS)

            @block.vector
            def _(dve):
                for m in range(MODS):
                    dve.wait_ge(b_landed, 16 * m + 16)
                    dve.tensor_tensor(acc[0:1, m, :], acc[0:1, m, :], modw[0:1, m % 2, :], ALU.add).then_inc(b_added, 1)
                for n in range(MODS * NC):
                    m, c = n // NC, n % NC
                    dve.wait_ge(summed, n + 1)
                    dve.tensor_copy(acc[0:1, m, c * BANK:(c + 1) * BANK], core.psum[0:1, n % 8, :]).then_inc(rows_ready, 1)

            @block.tensor
            def _(pe):
                for n in range(MODS * NC):
                    m, c = n // NC, n % NC
                    pe.wait_ge(b_added, m + 1)
                    if n >= 8:
                        pe.wait_ge(rows_ready, n - 7)
                    pe.matmul(core.psum[0:1, n % 8, :], core.ones[:, 0:1], acc[:, m, c * BANK:(c + 1) * BANK],
                              start=True, stop=True).then_inc(summed, 1)


def gated_add(core, dve_chain, eng, tmp, gate, c0, w, t, src):
    dve_chain.step(eng.tensor_tensor(tmp[:, 0:w], src, gate[:, c0:c0 + w], ALU.mult))
    x = core.x[:, t, c0:c0 + w]
    return eng.tensor_tensor(x, tmp[:, 0:w], x, ALU.add)


def stage_lru(core):
    nc, d = core.nc, core.dram
    with ExitStack() as ctx:
        xb = core.sbuf(ctx, "lru_x", [LW, LBLK, CONV - 1 + SEQ])
        gb = core.sbuf(ctx, "lru_gelu", [LW, LBLK, SEQ])
        vec = core.sbuf(ctx, "lru_vectors", [LW, 4 + CONV, LBLK])
        nsp = core.sbuf(ctx, "lru_decay", [LW, 2, LBLK])
        gate = core.sbuf(ctx, "lru_gate", [P, D])
        vec_landed, padded, gate_landed = core.sem("lru_vec_landed"), core.sem("lru_padded"), core.sem("lru_gate_landed")
        with ExitStack() as inner:
            norm = Norm(core, inner, "lru_norm", d["lru_g"], mod=0)

            def take(eng, b, src):
                if b < LBLK:
                    return copy_on(eng, xb[:, b, CONV - 1:], src)
                return copy_on(eng, gb[:, b - LBLK, :], src)

            win = ProjectT(core, inner, "lru_in", d["lru_in"], LW, 2 * LBLK, take)
            with nc.Block() as block:
                @block.sync
                def _(sp):
                    norm.load(sp)
                    sp.dma_start(vec[:, :, :], d["lru_vec"]).then_inc(vec_landed, 16)
                    sp.dma_start(gate[:, :], d["mod_rows"][0][2 * D:].partition_broadcast(P)).then_inc(gate_landed, 16)
                    win.load(sp)
                    sp.wait_ge(gate_landed, 16)
                    sp.wait_ge(vec_landed, 16)

                @block.gpsimd
                def _(pool):
                    pool.memset(xb[:, :, 0:CONV - 1], 0.0).then_inc(padded, 1)
                    pool.wait_ge(padded, 1)

                @block.scalar
                def _(act):
                    norm.act(act)
                    win.take(act, 1)

                @block.vector
                def _(dve):
                    norm.dve(dve)
                    win.take(dve, 0)

                @block.tensor
                def _(pe):
                    norm.pe(pe)
                    norm.hT_done(pe)
                    win.pe(pe)

        sb = lambda n, s: core.sbuf(ctx, "lru_" + n, s)
        xc, rr, ii, tt = (sb(n, [LW, LBLK, SEQ]) for n in ("xc", "r", "i", "t"))
        gw = sb("gate_w", [LW, 2, LBLK, LW])
        outw = sb("out_w", [LW, LBLK, BANK])
        tmp = sb("tmp", [P, BANK])
        s = lambda n: core.sem("lru_" + n)
        gw_landed, gates_done, conved, chain_sem = s("gw_landed"), s("gates_done"), s("conved"), s("chain")
        softplus, gelued, r_ready, i_ready, a_ready, t_ready, root_in, root = (s(n) for n in (
            "softplus", "gelued", "r_ready", "i_ready", "a_ready", "t_ready", "root_in", "root"))
        nsp_ready, y_ready, out_landed, out_done, out_taken, scanned = (s(n) for n in (
            "nsp_ready", "y_ready", "out_landed", "out_done", "out_taken", "scanned"))
        flat = lambda v: v.rearrange("p b t -> p (b t)")
        HALF = LBLK // 2
        with nc.Block() as block:
            @block.sync
            def _(sp):
                sp.dma_start(gw[:, :, :, :], d["lru_gate_w"]).then_inc(gw_landed, 16)
                view = d["lru_out"].rearrange("(b p) c -> p b c", p=LW)
                for c in range(2):
                    if c:
                        sp.wait_ge(out_done, NT)
                    sp.dma_start(outw[:, :, :], view[:, :, c * BANK:(c + 1) * BANK]).then_inc(out_landed, 16)

            @block.tensor
            def _(pe):
                pe.wait_ge(gw_landed, 16)
                for b in range(LBLK):
                    pe.wait_ge(conved, b + 1)
                    if b >= 4:
                        pe.wait_ge(i_ready, b - 3)
                    for g in range(2):
                        ins = pe.matmul(core.psum[0:LW, b % 4, g * SEQ:(g + 1) * SEQ], gw[:, g, b, :], xc[:, b, :],
                                        start=True, stop=True)
                    ins.then_inc(gates_done, 1)
                pe.wait_ge(y_ready, 1)
                for c in range(2):
                    pe.wait_ge(out_landed, 16 * (c + 1))
                    for t in range(NT):
                        for b in range(LBLK):
                            ins = pe.matmul(core.psum[:, 4 + 2 * c + t, :], xc[:, b, t * P:(t + 1) * P], outw[:, b, :],
                                            start=b == 0, stop=b == LBLK - 1)
                        ins.then_inc(out_done, 1)

            @block.scalar
            def _(act):
                act.activation(nsp[:, 0, :], vec[:, 7, :], ACT.Sigmoid).then_inc(softplus, 1)
                for b in range(LBLK):
                    act.wait_ge(gates_done, b + 1)
                    act.activation(rr[:, b, :], core.psum[0:LW, b % 4, 0:SEQ], ACT.Sigmoid,
                                   bias=vec[:, 5, b:b + 1]).then_inc(r_ready, 1)
                    act.activation(ii[:, b, :], core.psum[0:LW, b % 4, SEQ:], ACT.Sigmoid,
                                   bias=vec[:, 6, b:b + 1]).then_inc(i_ready, 1)
                act.wait_ge(softplus, 1)
                act.activation(nsp[:, 0, :], nsp[:, 0, :], ACT.Ln).then_inc(softplus, 1)
                act.activation(flat(gb[:, :, :]), flat(gb[:, :, :]), ACT.Gelu).then_inc(gelued, 1)
                act.wait_ge(nsp_ready, 1)
                act.wait_ge(r_ready, LBLK)
                for b in range(LBLK):
                    act.activation(tt[:, b, :], rr[:, b, :], ACT.Tanh, scale=nsp[:, 1, b:b + 1]).then_inc(t_ready, 1)
                act.wait_ge(t_ready, LBLK)
                for b in range(LBLK):
                    act.activation(rr[:, b, :], rr[:, b, :], ACT.Exp, scale=nsp[:, 0, b:b + 1]).then_inc(a_ready, 1)
                act.wait_ge(root_in, 1)
                act.activation(flat(tt[:, :, :]), flat(tt[:, :, :]), ACT.Sqrt).then_inc(root, 1)

            @block.vector
            def _(dve):
                chain = Chain(dve, chain_sem)
                for b in range(LBLK):
                    for j in range(CONV):
                        src = xb[:, b, j:j + SEQ]
                        if j == 0:
                            ins = dve.tensor_scalar(xc[:, b, :], src, vec[:, j, b:b + 1], vec[:, 4, b:b + 1], ALU.mult, ALU.add)
                        else:
                            ins = dve.scalar_tensor_tensor(xc[:, b, :], src, vec[:, j, b:b + 1], xc[:, b, :], ALU.mult, ALU.add)
                        if j < CONV - 1:
                            chain.step(ins)
                    ins.then_inc(conved, 1)
                dve.wait_ge(softplus, 2)
                chain.step(dve.tensor_scalar(nsp[:, 0, :], nsp[:, 0, :], 8.0, None, ALU.mult))
                dve.tensor_scalar(nsp[:, 1, :], nsp[:, 0, :], -1.0, None, ALU.mult).then_inc(nsp_ready, 1)
                dve.wait_ge(i_ready, LBLK)
                dve.wait_ge(conved, LBLK)
                chain.step(dve.tensor_tensor(flat(ii[:, :, :]), flat(ii[:, :, :]), flat(xc[:, :, :]), ALU.mult))
                dve.wait_ge(t_ready, LBLK)
                chain.step(dve.tensor_scalar(flat(xc[:, :, :]), flat(tt[:, :, :]), 1.0, None, ALU.add))
                chain.step(dve.reciprocal(flat(xc[:, :, :]), flat(xc[:, :, :])))
                dve.scalar_tensor_tensor(flat(tt[:, :, :]), flat(tt[:, :, :]), 2.0, flat(xc[:, :, :]), ALU.mult, ALU.mult)\
                   .then_inc(root_in, 1)
                dve.wait_ge(root, 1)
                chain.step(dve.tensor_tensor(flat(ii[:, :, :]), flat(ii[:, :, :]), flat(tt[:, :, :]), ALU.mult))
                dve.wait_ge(a_ready, LBLK)
                for b in range(LBLK):
                    dve.tensor_tensor_scan(tt[:, b, :], rr[:, b, :], ii[:, b, :], 0.0, ALU.mult, ALU.add).then_inc(scanned, 1)
                dve.wait_ge(scanned, LBLK)
                dve.wait_ge(gelued, 1)
                dve.tensor_tensor(flat(xc[:, :, :]), flat(tt[:, :, :]), flat(gb[:, :, :]), ALU.mult).then_inc(y_ready, 1)
                for c in range(2):
                    for t in range(NT):
                        dve.wait_ge(out_done, NT * c + t + 1)
                        gated_add(core, chain, dve, tmp, gate, c * BANK, BANK, t, core.psum[:, 4 + 2 * c + t, :])\
                            .then_inc(out_taken, 1)
                        dve.wait_ge(out_taken, NT * c + t + 1)


def stage_peer(core, layer):
    nc, d = core.nc, core.dram
    L = f"peer{layer}_"
    name = lambda n: L + n
    sem = lambda n: core.sem(L + n)
    N2 = 2 * PHEADS
    with ExitStack() as ctx:
        gate = core.sbuf(ctx, name("gate"), [P, D])
        e1T, e2T, gT = (core.sbuf(ctx, name(n), [P, SEQ]) for n in ("e1T", "e2T", "gT"))
        gate_landed = sem("gate_landed")
        with ExitStack() as inner:
            qT = core.sbuf(inner, name("qT"), [P, N2, SEQ])
            subT = core.sbuf(inner, name("subT"), [P, N2, KEYS])
            sub_landed = sem("sub_landed")
            with ExitStack() as first:
                norm = Norm(core, first, name("norm"), d[f"peer{layer}_g"], mod=2 * layer + 1)
                wq = ProjectT(core, first, name("q"), d[f"peer{layer}_q"], P, N2,
                              lambda eng, b, src: copy_on(eng, qT[:, b, :], src))
                with nc.Block() as block:
                    @block.sync
                    def _(sp):
                        norm.load(sp)
                        wq.load(sp)
                        sp.dma_start(subT[:, :, :], d[f"peer{layer}_sub"]).then_inc(sub_landed, 16)
                        sp.dma_start(gate[:, :], d["mod_rows"][2 * layer + 1][2 * D:].partition_broadcast(P))\
                          .then_inc(gate_landed, 16)
                        sp.wait_ge(sub_landed, 16)
                        sp.wait_ge(gate_landed, 16)

                    @block.scalar
                    def _(act):
                        norm.act(act)
                        wq.take(act, 1)

                    @block.vector
                    def _(dve):
                        norm.dve(dve)
                        wq.take(dve, 0)

                    @block.tensor
                    def _(pe):
                        norm.pe(pe)
                        norm.hT_done(pe)
                        wq.pe(pe)

            sb = lambda n, s, dt=F32: core.sbuf(inner, name(n), s, dt)
            sc = sb("sc", [P, NT, N2, KEYS])
            rest = sb("rest", [P, 2, TOPK * TOPK])
            val = sb("val", [P, NT, N2, TOPK])
            idx = sb("idx", [P, NT, N2, TOPK], U32)
            idxf = sb("idxf", [P, NT, N2, TOPK])
            cand = sb("cand", [P, PHEADS, TOPK * TOPK])
            top = sb("top", [P, NT, PHEADS, TOPK])
            place = sb("place", [P, NT, PHEADS, TOPK], U32)
            digit = sb("digit", [P, 2, PICKS], U32)
            digitf = sb("digitf", [P, 2, PICKS])
            hot = sb("hot", [P, PHEADS, TOPK, TOPK])
            pick = sb("pick", [P, NT, 3, PICKS])
            iota16 = sb("iota16", [P, TOPK])
            summed = sb("sum", [P, NT, PHEADS])
            sc_done, sc_taken, ch = sem("sc_done"), sem("sc_taken"), sem("pick_chain")
            to_exp, exp_done, picked, turned, pickT = sem("to_exp"), sem("exp_done"), sem("picked"), sem("turned"), sem("pickT")
            iota_landed = sem("iota_landed")
            with nc.Block() as block:
                @block.sync
                def _(sp):
                    sp.dma_start(iota16[:, :], d["c_iota"][:, 0:TOPK]).then_inc(iota_landed, 16)

                @block.tensor
                def _(pe):
                    for n in range(NT * N2 // 4):
                        t, b = n // 4, n % 4 * 4
                        for j in range(4):
                            ins = pe.matmul(core.psum[:, n, j * P:(j + 1) * P], qT[:, b + j, t * P:(t + 1) * P],
                                            subT[:, b + j, :], start=True, stop=True)
                        ins.then_inc(sc_done, 1)
                    pe.wait_ge(sc_taken, 8)
                    for t in range(NT):
                        pe.wait_ge(picked, t + 1)
                        for j in range(3):
                            ins = pe.transpose(core.psum[:, j, t * P:(t + 1) * P], pick[:, t, j, :], core.ident[:, :])
                    ins.then_inc(turned, 1)

                @block.scalar
                def _(act):
                    for n in range(8):
                        act.wait_ge(sc_done, n + 1)
                        t, b = n // 4, n % 4 * 4
                        act.copy(sc[:, t, b:b + 4, :], core.psum[:, n, :].rearrange("p (j c) -> p j c", j=4))\
                           .then_inc(sc_taken, 1)
                    for t in range(NT):
                        act.wait_ge(to_exp, t + 1)
                        act.activation(pick[:, t, 2, :], pick[:, t, 2, :], ACT.Exp).then_inc(exp_done, 1)
                    act.wait_ge(turned, 1)
                    for j, dst in enumerate((e1T, e2T, gT)):
                        act.copy(dst[:, :], core.psum[:, j, 0:SEQ]).then_inc(pickT, 1)
                    act.wait_ge(pickT, 3)

                @block.vector
                def _(dve):
                    chain = Chain(dve, ch)
                    step = chain.step

                    def top16(values, vals, where, spare):
                        step(dve.max(vals[:, 0:8], values))
                        dve.max_index(where[:, 0:8], vals[:, 0:8], values)
                        step(dve.match_replace(spare, vals[:, 0:8], values, -3.0e38))
                        step(dve.max(vals[:, 8:16], spare))
                        return dve.max_index(where[:, 8:16], vals[:, 8:16], spare)

                    dve.wait_ge(iota_landed, 16)
                    for t in range(NT):
                        for b in range(N2):
                            if b % 4 == 0:
                                dve.wait_ge(sc_taken, 4 * t + b // 4 + 1)
                            step(top16(sc[:, t, b, :], val[:, t, b, :], idx[:, t, b, :], rest[:, b % 2, 0:KEYS]))
                        step(dve.tensor_copy(idxf[:, t], idx[:, t]))
                        v = val[:, t].rearrange("p (h a) k -> p h a k", a=2)
                        f = idxf[:, t].rearrange("p (h a) k -> p h a k", a=2)
                        step(dve.tensor_tensor(cand[:, :, :].rearrange("p h (i j) -> p h i j", i=TOPK),
                                               spread(v[:, :, 0, :], 3, TOPK), spread(v[:, :, 1, :], 2, TOPK), ALU.add))
                        for h in range(PHEADS):
                            step(top16(cand[:, h, :], top[:, t, h, :], place[:, t, h, :], rest[:, h % 2, :]))
                        g = pick[:, t, 2, :].rearrange("p (h k) -> p h k", h=PHEADS)
                        dve.tensor_tensor(g, top[:, t], spread(top[:, t, :, 0], 2, TOPK), ALU.subtract).then_inc(to_exp, 1)
                        where = place[:, t].rearrange("p h k -> p (h k)")
                        dve.tensor_scalar(digit[:, 0, :], where, 4, None, ALU.logical_shift_right)
                        step(dve.tensor_scalar(digit[:, 1, :], where, 15, None, ALU.bitwise_and))
                        step(dve.tensor_copy(digitf[:, :, :], digit[:, :, :]))
                        for a in range(2):
                            dg = digitf[:, a, :].rearrange("p (h k) -> p h k", h=PHEADS)
                            step(dve.tensor_tensor(hot[:, :, :, :].rearrange("p h k j -> p (h k) j"),
                                                   spread(digitf[:, a, :], 2, TOPK), spread(iota16[:, :], 1, PICKS), ALU.is_equal))
                            step(dve.tensor_tensor(hot[:, :, :, :], hot[:, :, :, :], spread(f[:, :, a, :], 2, TOPK), ALU.mult))
                            step(dve.tensor_reduce(pick[:, t, a, :], hot[:, :, :, :].rearrange("p h k j -> p (h k) j"), AX, ALU.add))
                        dve.wait_ge(exp_done, t + 1)
                        step(dve.tensor_reduce(summed[:, t, :], g, AX, ALU.add))
                        step(dve.reciprocal(summed[:, t, :], summed[:, t, :]))
                        dve.tensor_tensor(g, g, spread(summed[:, t, :], 2, TOPK), ALU.mult).then_inc(picked, 1)

        W = core.sbuf(ctx, name("W"), [P, KEYS, SEQ])
        with ExitStack() as inner:
            TOK = 8
            iota = core.sbuf(inner, name("iota"), [P, KEYS])
            A = core.sbuf(inner, name("A"), [P, TOK, KEYS])
            B = core.sbuf(inner, name("B"), [P, TOK, KEYS])
            landed, a_ready = sem("iota128_landed"), sem("ab_ready")
            w_done, w_taken = [sem(f"w_done{h}") for h in range(2)], sem("w_taken")
            with nc.Block() as block:
                @block.sync
                def _(sp):
                    sp.dma_start(iota[:, :], d["c_iota"]).then_inc(landed, 16)
                    sp.wait_ge(landed, 16)

                @block.vector
                def _(dve):
                    dve.wait_ge(landed, 16)
                    def step(i):
                        for half in range(2):
                            wait_past(dve, w_done[half], i)
                            for j in range(4 * half, 4 * half + 4):
                                n = bass.ds(i * TOK + j, 1)
                                dve.tensor_scalar(B[:, j, :], iota[:, :], e2T[:, n], None, ALU.is_equal)
                                ins = dve.tensor_scalar(A[:, j, :], iota[:, :], e1T[:, n], gT[:, n], ALU.is_equal, ALU.mult)
                            ins.then_inc(a_ready, 1)

                    step(0)
                    with dve.Fori(1, SEQ // TOK) as i:
                        step(i)

                @block.tensor
                def _(pe):
                    def step(i):
                        for half in range(2):
                            pe.wait_ge(a_ready, 2 * i + half + 1)
                            wait_past(pe, w_taken, 2 * i + half)
                            for j in range(4 * half, 4 * half + 4):
                                ins = pe.matmul(core.psum[:, half, (j % 4) * KEYS:(j % 4 + 1) * KEYS], A[:, j, :], B[:, j, :],
                                                start=True, stop=True)
                            ins.then_inc(w_done[half], 1)

                    step(0)
                    with pe.Fori(1, SEQ // TOK) as i:
                        step(i)

                @block.scalar
                def _(act):
                    def step(i):
                        for half in range(2):
                            act.wait_ge(w_done[half], i + 1)
                            dst = W[:, :, bass.ds(i * TOK + 4 * half, 4)]
                            act.copy(dst.rearrange("p c n -> p n c"), core.psum[:, half, :].rearrange("p (n c) -> p n c", n=4))\
                               .then_inc(w_taken, 1)

                    step(0)
                    with act.Fori(1, SEQ // TOK) as i:
                        step(i)

        with ExitStack() as inner:
            SLOTS = 4
            STEPS = KEYS // SLOTS
            U = core.sbuf(inner, name("U"), [P, SLOTS, KD, P])
            V = core.sbuf(inner, name("V"), [P, SLOTS, D])
            act_ = core.sbuf(inner, name("act"), [P, 2, SEQ])
            wa = core.sbuf(inner, name("wa"), [P, 2, SEQ])
            tmp = core.sbuf(inner, name("tmp"), [P, BANK])
            u_landed = [sem(f"u_landed{s}") for s in range(SLOTS)]
            v_landed = [sem(f"v_landed{s}") for s in range(SLOTS)]
            s_done, act_done, wa_done, y_added = ([sem(f"{n}{s}") for s in range(2)] for n in (
                "s_done", "act_done", "wa_done", "y_added"))
            out_taken, out_chain = sem("out_taken"), sem("out_chain")
            S = lambda s: core.psum[:, s % 2, 0:SEQ]
            Y = lambda t, c: core.psum[:, 4 + 2 * t + c, :]
            with nc.Block() as block:
                @block.sync
                def _(sp):
                    def load(i, first=False):
                        for s in range(SLOTS):
                            e, h = i * SLOTS + s, 2 * i + s // 2
                            if not first:
                                sp.wait_ge(s_done[s % 2], h - 1)
                            sp.dma_start(U[:, s], d[f"peer{layer}_u"][bass.ds(e, 1)].rearrange("a p k c -> p (a k) c"))\
                              .then_inc(u_landed[s], 16)
                            if not first:
                                sp.wait_ge(y_added[s % 2], h - 1)
                            sp.dma_start(V[:, s, :], d[f"peer{layer}_v"][bass.ds(e * P, P), :]).then_inc(v_landed[s], 16)

                    load(0, first=True)
                    with sp.Fori(1, STEPS) as i:
                        load(i)

                @block.tensor
                def _(pe):
                    def scores(i, s):
                        h = 2 * i + s // 2
                        pe.wait_ge(u_landed[s], 16 * i + 16)
                        wait_past(pe, act_done[s % 2], h)
                        for k in range(KD):
                            ins = pe.matmul(S(s), U[:, s, k, :], core.hT[:, k, :], start=k == 0, stop=k == KD - 1)
                        ins.then_inc(s_done[s % 2], 1)

                    def add(i, s, first=False, last=False):
                        h = 2 * i + s // 2
                        pe.wait_ge(v_landed[s], 16 * i + 16)
                        pe.wait_ge(wa_done[s % 2], h + 1)
                        for t in range(NT):
                            for c in range(2):
                                ins = pe.matmul(Y(t, c), wa[:, s % 2, t * P:(t + 1) * P], V[:, s, c * BANK:(c + 1) * BANK],
                                                start=first, stop=last)
                        ins.then_inc(y_added[s % 2], 1)

                    def step(i, first=False):
                        for s in range(SLOTS):
                            if s + 1 < SLOTS:
                                scores(i, s + 1)
                            else:
                                scores(i + 1, 0)
                            add(i, s, first=first and s == 0)

                    scores(0, 0)
                    step(0, first=True)
                    with pe.Fori(1, STEPS - 1) as i:
                        step(i)
                    for s in range(SLOTS):
                        if s + 1 < SLOTS:
                            scores(STEPS - 1, s + 1)
                        add(STEPS - 1, s, last=s == SLOTS - 1)

                @block.scalar
                def _(act):
                    def step(h):
                        for b in range(2):
                            act.wait_ge(s_done[b], h + 1)
                            wait_past(act, wa_done[b], h)
                            act.activation(act_[:, b, :], S(b), ACT.Gelu).then_inc(act_done[b], 1)

                    step(0)
                    with act.Fori(1, KEYS // 2) as h:
                        step(h)

                @block.vector
                def _(dve):
                    def step(h):
                        for b in range(2):
                            dve.wait_ge(act_done[b], h + 1)
                            wait_past(dve, y_added[b], h)
                            w = W[:, bass.ds(2 * h + b, 1), :].rearrange("p a n -> p (a n)")
                            dve.tensor_tensor(wa[:, b, :], act_[:, b, :], w, ALU.mult).then_inc(wa_done[b], 1)

                    step(0)
                    with dve.Fori(1, KEYS // 2) as h:
                        step(h)
                    dve.wait_ge(y_added[1], KEYS // 2)
                    chain = Chain(dve, out_chain)
                    for t in range(NT):
                        for c in range(2):
                            gated_add(core, chain, dve, tmp, gate, c * BANK, BANK, t, Y(t, c)).then_inc(out_taken, 1)
                            dve.wait_ge(out_taken, 2 * t + c + 1)


def stage_fox(core):
    nc, d = core.nc, core.dram
    with ExitStack() as ctx:
        width = 4 * D + MAPS
        proj = core.sbuf(ctx, "fox_proj", [P, NT, width])
        gate = core.sbuf(ctx, "fox_gate", [P, D])
        mask = core.sbuf(ctx, "fox_mask", [P, CAUSAL])
        left = core.sbuf(ctx, "fox_left", [2, MAPS, SEQ])
        right = core.sbuf(ctx, "fox_right", [2, MAPS, SEQ])
        consts_landed = core.sem("fox_consts_landed")
        with ExitStack() as inner:
            norm = Norm(core, inner, "fox_norm", d["fox_g"], mod=2)

            def take(eng, c, c0, w, t, src):
                return copy_on(eng, proj[:, t, c0:c0 + w], src)

            win = Project(core, inner, "fox_in", d["fox_in"], core.hT, P, KD, column_chunks(0, width), take)
            with nc.Block() as block:
                @block.sync
                def _(sp):
                    norm.load(sp)
                    sp.dma_start(mask[:, :], d["c_mask"]).then_inc(consts_landed, 16)
                    sp.dma_start(gate[:, :], d["mod_rows"][2][2 * D:].partition_broadcast(P)).then_inc(consts_landed, 16)
                    win.load(sp)
                    sp.wait_ge(consts_landed, 32)

                @block.scalar
                def _(act):
                    norm.act(act)
                    win.take(act, [1])

                @block.vector
                def _(dve):
                    norm.dve(dve)
                    win.take(dve, [0])

                @block.tensor
                def _(pe):
                    norm.pe(pe)
                    norm.hT_done(pe)
                    win.pe(pe)

        sb = lambda n, s: core.sbuf(ctx, "fox_" + n, s)
        s = lambda n: core.sem("fox_" + n)
        fb, z, cum, onerow = sb("f_b", [MAPS, 1]), sb("z", [MAPS, 6, SEQ]), sb("cum", [MAPS, 2, SEQ]), sb("onerow", [MAPS, SEQ])
        fb_landed, f_turned, z_ready, e_ready, ln_ready, cum_chain, cum_ready, rows_landed, ones_ready, og_ready = (
            s(n) for n in ("fb_landed", "f_turned", "z_ready", "e_ready", "ln_ready", "cum_chain", "cum_ready",
                           "rows_landed", "ones_ready", "og_ready"))
        fcol = 3 * D
        with nc.Block() as block:
            @block.sync
            def _(sp):
                sp.dma_start(fb[:, :], d["fox_fb"]).then_inc(fb_landed, 16)
                sp.wait_ge(cum_ready, 1)
                sp.dma_start(left[1:2, :, :], cum[:, 0, :]).then_inc(rows_landed, 16)
                sp.dma_start(right[0:1, :, :], cum[:, 1, :]).then_inc(rows_landed, 16)
                sp.dma_start(left[0:1, :, :], onerow[:, :]).then_inc(rows_landed, 16)
                sp.dma_start(right[1:2, :, :], onerow[:, :]).then_inc(rows_landed, 16)
                sp.wait_ge(rows_landed, 64)

            @block.tensor
            def _(pe):
                for t in range(NT):
                    ins = pe.transpose(core.psum[0:MAPS, 0, t * P:(t + 1) * P], proj[:, t, fcol:fcol + MAPS], core.ident[:, :])
                ins.then_inc(f_turned, 1)

            @block.scalar
            def _(act):
                act.wait_ge(z_ready, 1)
                act.activation(z[:, 1, :], z[:, 1, :], ACT.Exp).then_inc(e_ready, 1)
                act.wait_ge(z_ready, 2)
                act.activation(z[:, 2, :], z[:, 3, :], ACT.Ln).then_inc(ln_ready, 1)
                for t in range(NT):
                    og = proj[:, t, fcol + MAPS:]
                    act.activation(og, og, ACT.Sigmoid).then_inc(og_ready, 1)
                act.wait_ge(og_ready, NT)

            @block.vector
            def _(dve):
                chain = Chain(dve, cum_chain)
                chain.step(dve.memset(onerow[:, :], 1.0))
                dve.wait_ge(f_turned, 1)
                dve.wait_ge(fb_landed, 16)
                chain.step(dve.tensor_scalar(z[:, 0, :], core.psum[0:MAPS, 0, 0:SEQ], fb[:, 0:1], None, ALU.add))
                chain.step(dve.tensor_scalar(z[:, 1, :], z[:, 0, :], -1.0, None, ALU.mult))
                dve.tensor_tensor(z[:, 1, :], z[:, 0, :], z[:, 1, :], ALU.min).then_inc(z_ready, 1)
                dve.wait_ge(z_ready, 1)
                chain.step(dve.tensor_scalar(z[:, 0, :], z[:, 0, :], 0.0, None, ALU.min))
                dve.wait_ge(e_ready, 1)
                dve.tensor_scalar(z[:, 3, :], z[:, 1, :], 1.0, None, ALU.add).then_inc(z_ready, 1)
                dve.wait_ge(ln_ready, 1)
                chain.step(dve.tensor_scalar(z[:, 5, :], z[:, 3, :], 1.0, None, ALU.is_equal))
                chain.step(dve.scalar_tensor_tensor(z[:, 4, :], z[:, 3, :], 1.0, z[:, 5, :], ALU.subtract, ALU.add))
                chain.step(dve.reciprocal(z[:, 4, :], z[:, 4, :]))
                chain.step(dve.tensor_tensor(z[:, 4, :], z[:, 2, :], z[:, 4, :], ALU.mult))
                chain.step(dve.tensor_tensor(z[:, 4, :], z[:, 4, :], z[:, 5, :], ALU.add))
                chain.step(dve.tensor_tensor(z[:, 4, :], z[:, 4, :], z[:, 1, :], ALU.mult))
                chain.step(dve.tensor_tensor(z[:, 0, :], z[:, 0, :], z[:, 4, :], ALU.subtract))
                chain.step(dve.tensor_tensor_scan(cum[:, 0, :], onerow[:, :], z[:, 0, :], 0.0, ALU.mult, ALU.add))
                dve.tensor_scalar(cum[:, 1, :], cum[:, 0, :], -1.0, None, ALU.mult).then_inc(cum_ready, 1)

        qk = [(0, d["fox_q_g"], True), (BANK, d["fox_q_g"], True), (D, d["fox_k_g"], False), (D + BANK, d["fox_k_g"], False)]
        att = Attention(core, ctx, "fox", proj, qk, lambda h, t: proj[:, t, 2 * D + h * HD:2 * D + (h + 1) * HD],
                        lambda h: (core.ident, mask[:, :]), decay=(left, right), gate=lambda dve, t: proj[:, t, fcol + MAPS:])
        tmp = core.sbuf(ctx, "fox_tmp", [P, 2 * NT, BANK])
        add_chain = core.sem("fox_add_chain")
        with ExitStack() as inner:
            hold = {}

            def add(eng, c, c0, w, t, src):
                return gated_add(core, hold["chain"], eng, tmp[:, NT * c + t, :], gate, c0, w, t, src)

            wout = Project(core, inner, "fox_out", d["fox_out"], att.yT, P, KD, column_chunks(0, D), add, slots=2)
            with nc.Block() as block:
                @block.sync
                def _(sp):
                    att.load(sp)
                    wout.load(sp)

                @block.gpsimd
                def _(pool):
                    att.pool(pool)

                @block.scalar
                def _(act):
                    att.act(act)

                @block.vector
                def _(dve):
                    att.dve(dve)
                    hold["chain"] = Chain(dve, add_chain)
                    wout.take(dve, [0, 1])
                    dve.wait_ge(wout.taken[1], 2)

                @block.tensor
                def _(pe):
                    att.pe(pe)
                    wout.pe(pe)


def stage_store(core, out):
    nc = core.nc
    stored = core.sem("out_stored")
    with nc.Block() as block:
        @block.sync
        def _(sp):
            sp.dma_start(out.rearrange("b (t p) c -> p (b t) c", p=P), core.x[:, :, :]).then_inc(stored, 16)
            sp.wait_ge(stored, 16)


def build(nc, dram, out, stages=("mix1", "moe", "lru", "peer0", "fox", "peer1")):
    with ExitStack() as ctx:
        core = Core(nc, ctx, dram)
        stage_start(core)
        run = {"mix1": lambda: stage_mix1(core), "moe": lambda: stage_moe(core), "lru": lambda: stage_lru(core),
               "peer0": lambda: stage_peer(core, 0), "fox": lambda: stage_fox(core), "peer1": lambda: stage_peer(core, 1)}
        for s in stages:
            run[s]()
            core.free_sems()
        stage_store(core, out)


def shape_constants():
    dist = SEQ - 1 - np.arange(2 * SEQ)
    n = np.maximum(dist, 1).astype(np.float32)
    exact = N_BUCKETS // 2
    large = exact + (np.log(n / exact) / np.float32(math.log(MAX_DISTANCE / exact)) * (N_BUCKETS - exact)).astype(np.int32)
    bucket = np.where(dist < exact, np.maximum(dist, 0), np.minimum(large, N_BUCKETS - 1))
    bucket = np.where(dist >= 0, bucket, N_BUCKETS)
    onehot = (np.arange(N_BUCKETS + 1)[:, None] == bucket[None, :]).astype(np.float32)
    q, k = np.arange(P)[:, None], np.arange(SEQ)[None, :]
    mask = np.concatenate([np.where(k[:, :P] <= q, 0, NEG), np.where(k <= q + P, 0, NEG)], 1).astype(np.float32)
    return {
        "c_ident": np.eye(P, dtype=np.float32),
        "c_flip": np.ascontiguousarray(np.eye(P, dtype=np.float32)[::-1]),
        "c_iota": np.tile(np.arange(KEYS, dtype=np.float32), (P, 1)),
        "c_rev": np.tile(np.arange(PER_GROUP, 0, -1, dtype=np.float32), (P, 1)),
        "c_buckets": onehot,
        "c_mask": mask,
    }


def laid_out(a):
    same = ["x", "norm1_g", "w_in", "diff_q_g", "diff_k_g", "lambda_q1", "lambda_k1", "lambda_q2", "lambda_k2",
            "diff_sub_g", "moba_q_g", "moba_k_g", "rel_bias", "w_out", "norm2_g", "w_gate", "w_up", "w_down"]
    m = {n: a[n] for n in same}
    rows = lambda v: v.reshape(KD, P, -1).transpose(1, 0, 2)
    experts = a["router_expert"][0].transpose(1, 0, 2).reshape(D, EXPERTS)
    m["router"] = rows(np.concatenate([a["router_group"][0], experts], axis=1))
    m["c_col"] = a["c_2"].reshape(KD, P).T
    for i, n in enumerate(("l0_mix", "l0_ffn", "l1_mix", "l1_ffn")):
        m[f"mod_w{i}"], m[f"mod_b{i}"] = a[n + "_mod_w_2"], a[n + "_mod_b_2"]
    blocks = lambda v: v.reshape(-1, LBLK, LW).transpose(2, 0, 1)
    m["lru_g"], m["lru_in"], m["lru_out"] = a["l0_mix_norm_g_2"], a["l0_lru_in_w_2"], a["l0_lru_out_w_2"]
    m["lru_vec"] = np.concatenate([blocks(a["l0_lru_" + n]) for n in (
        "conv_w_2", "conv_b_2", "ra_b_2", "ri_b_2", "lambda_2")], axis=1)
    m["lru_gate_w"] = np.stack([a["l0_lru_ra_w_2"], a["l0_lru_ri_w_2"]]).transpose(2, 0, 1, 3)
    for i in range(2):
        l = f"l{i}_"
        m[f"peer{i}_g"], m[f"peer{i}_q"] = a[l + "ffn_norm_g_2"], a[l + "peer_q_w_2"]
        m[f"peer{i}_sub"] = np.stack([a[l + "peer_subkey1_2"], a[l + "peer_subkey2_2"]], 1)\
            .reshape(2 * PHEADS, KEYS, -1).transpose(2, 0, 1)
        m[f"peer{i}_u"] = a[l + "peer_u_2"].reshape(KEYS, KEYS, KD, P).transpose(1, 3, 2, 0)
        m[f"peer{i}_v"] = a[l + "peer_v_2"].reshape(KEYS, KEYS, D).transpose(1, 0, 2).reshape(KEYS * KEYS, D)
    m["fox_g"], m["fox_in"], m["fox_out"] = a["l1_mix_norm_g_2"], a["l1_fox_in_w_2"], a["l1_fox_out_w_2"]
    m["fox_fb"] = a["l1_fox_f_b_2"].reshape(MAPS, 1)
    m["fox_q_g"], m["fox_k_g"] = a["l1_fox_q_norm_g_2"], a["l1_fox_k_norm_g_2"]
    return m


def declare(nc, arrays):
    dram = {n: nc.dram_tensor("in_" + n, v.shape, mybir.dt.from_np(v.dtype), kind="ExternalInput").ap()
            for n, v in arrays.items()}
    dram["mod_w"] = [dram[f"mod_w{i}"] for i in range(MODS)]
    dram["mod_b"] = [dram[f"mod_b{i}"] for i in range(MODS)]
    dram["mod_rows"] = nc.dram_tensor("mod_rows", (MODS, MODW), F32, kind="Internal").ap()
    dram["curve"] = nc.dram_tensor("bias_curve_rows", (N_REL_HEADS, BANK), F32, kind="Internal").ap()
    return dram


def kernel(**inputs):
    import concourse.bacc as bacc
    from concourse.bass_utils import run_bass_kernel_spmd

    a = {n: np.asarray(v) for n, v in inputs.items()}
    arrays = {n: np.ascontiguousarray(v) for n, v in {**laid_out(a), **shape_constants()}.items()}
    nc = bacc.Bacc("TRN2", target_bir_lowering=False, num_devices=1)
    dram = declare(nc, arrays)
    out = nc.dram_tensor("out", (1, SEQ, D), F32, kind="ExternalOutput").ap()
    build(nc, dram, out)
    r = run_bass_kernel_spmd(nc, [{"in_" + n: v for n, v in arrays.items()}], core_ids=[0])
    return r.results[0]["out"]
```

```python
import math
from contextlib import ExitStack

import numpy as np

import concourse.bass as bass
import concourse.mybir as mybir

ALU = mybir.AluOpType
ACT = mybir.ActivationFunctionType
AX = mybir.AxisListType.X
F32 = mybir.dt.float32
U32 = mybir.dt.uint32
F32R = mybir.dt.float32r

P = 128
SEQ = 256
NT = SEQ // P
D = 1024
KD = D // P
BANK = 512
HD = 64
EPS = 1e-6
NEG = -1e30
N_BUCKETS = 32
MAX_DISTANCE = 2048
N_REL_HEADS = 12
DIFF_MAPS = 8
MAPS = 16
LAMBDA_INIT = 0.8 - 0.6 * math.exp(-0.3 * 0)
GROUPS, PER_GROUP = 4, 8
EXPERTS = GROUPS * PER_GROUP
HIDDEN = 256
MODS = 4
MODW = 3 * D
RNN = 128 * round(4 * D / (3 * 128))
LBLK = RNN // P
GATE_BLOCKS = 16
GATE_W = RNN // GATE_BLOCKS
CONV = 4
KEYS = 128
PHEADS = 8
TOPK = 16
PICKS = PHEADS * TOPK
CAUSAL = P + SEQ


def gate_tiles():
    return [(i, j) for j in range(LBLK) for i in range(LBLK)
            if any(max(i, j) * P < (g + 1) * GATE_W and g * GATE_W < (min(i, j) + 1) * P for g in range(GATE_BLOCKS))]


def spread(ap, axis, n):
    a = ap.unsqueeze(axis)
    shape = list(a.shape)
    shape[axis] = n
    return a.to_broadcast(shape)


def wait_past(eng, sem, n):
    if not (isinstance(n, int) and n <= 0):
        eng.wait_ge(sem, n)


class Chain:

    def __init__(self, eng, sem):
        self.eng, self.sem, self.count = eng, sem, 0

    def step(self, ins):
        ins.then_inc(self.sem, 1)
        self.count += 1
        self.eng.wait_ge(self.sem, self.count)


class Core:

    def __init__(self, nc, ctx, dram):
        self.nc, self.dram, self.sems = nc, dram, []
        self.x = self.sbuf(ctx, "x", [P, NT, D])
        self.hTh = self.sbuf(ctx, "hTh", [P, KD, SEQ], F32R)
        self.hTl = self.sbuf(ctx, "hTl", [P, KD, SEQ], F32R)
        self.ident = self.sbuf(ctx, "ident", [P, P])
        self.ones = self.sbuf(ctx, "ones", [P, P])
        self.psum = ctx.enter_context(nc.psum_tensor("psum", [P, 8, BANK], F32))

    def sbuf(self, ctx, name, shape, dt=F32):
        return ctx.enter_context(self.nc.sbuf_tensor(name, shape, dt))

    def sem(self, name):
        self.sems.append(self.nc.alloc_semaphore(name))
        return self.sems[-1]

    def free_sems(self):
        self.nc.clear_and_free_semaphores(self.sems)
        self.sems = []
        self.nc.all_engine_barrier()


class Norm:

    BANKS = 4

    def __init__(self, core, ctx, name, gain, mod=None):
        self.core, self.gain, self.mod = core, gain, mod
        self.h = core.sbuf(ctx, name + "_h", [P, NT, D])
        self.v = core.sbuf(ctx, name + "_v", [P, 2, 4, P])
        self.stat = core.sbuf(ctx, name + "_stat", [P, 4, NT])
        self.rows = core.sbuf(ctx, name + "_rows", [3 * KD, P])
        self.cols = core.sbuf(ctx, name + "_cols", [P, 3 * KD])
        self.n_rows = 1 if mod is None else 3
        self.rows_landed, self.rows_turned = core.sem(name + "_rows_landed"), core.sem(name + "_rows_turned")
        self.squares_summed = core.sem(name + "_squares_summed")
        self.var_ready = core.sem(name + "_var_ready")
        self.std_ready = core.sem(name + "_std_ready")
        self.chain_sem = core.sem(name + "_dve_chain")
        self.h_ready = core.sem(name + "_h_ready")
        self.turned = core.sem(name + "_turned")
        self.v_ready = core.sem(name + "_v_ready")
        self.hT_act = core.sem(name + "_hT_by_act")
        self.hT_dve = core.sem(name + "_hT_by_dve")

    def load(self, sp):
        as_rows = lambda v: v.rearrange("(k p) -> k p", p=P)
        sp.dma_start(self.rows[0:KD, :], as_rows(self.gain)).then_inc(self.rows_landed, 16)
        if self.mod is not None:
            sp.dma_start(self.rows[KD:3 * KD, :], as_rows(self.core.dram["mod_rows"][self.mod][0:2 * D]))\
              .then_inc(self.rows_landed, 16)

    def bank(self, t, g):
        return self.core.psum[:, 2 * t + g, :].rearrange("p (k n) -> p k n", k=4)

    def at(self, t, g):
        return slice(None), slice(4 * g, 4 * g + 4), slice(t * P, (t + 1) * P)

    def act(self, act):
        for t in range(NT):
            act.activation(self.h[:, t, :], self.core.x[:, t, :], ACT.Square,
                           accum_out=self.stat[:, 0, t:t + 1]).then_inc(self.squares_summed, 1)
        act.wait_ge(self.var_ready, 1)
        act.activation(self.stat[:, 2, :], self.stat[:, 1, :], ACT.Sqrt).then_inc(self.std_ready, 1)
        for n in range(2 * NT):
            act.wait_ge(self.v_ready, n + 1)
            act.copy(self.core.hTh[self.at(n // 2, n % 2)], self.v[:, n % 2]).then_inc(self.hT_act, 1)

    def dve(self, dve):
        chain = Chain(dve, self.chain_sem)
        used = self.n_rows * KD
        dve.wait_ge(self.rows_turned, 1)
        chain.step(dve.tensor_copy(self.cols[:, 0:used], self.core.psum[:, 7, 0:used]))
        gain, shift, scale = (self.cols[:, j * KD:(j + 1) * KD] for j in range(3))
        if self.mod is not None:
            chain.step(dve.scalar_tensor_tensor(gain, scale, 1.0, gain, ALU.add, ALU.mult))
        dve.wait_ge(self.squares_summed, NT)
        dve.tensor_scalar(self.stat[:, 1, :], self.stat[:, 0, :], 1.0 / D, EPS,
                          ALU.mult, ALU.add).then_inc(self.var_ready, 1)
        dve.wait_ge(self.std_ready, 1)
        chain.step(dve.reciprocal(self.stat[:, 3, :], self.stat[:, 2, :]))
        for t in range(NT):
            for g in range(2):
                cols = slice(g * BANK, (g + 1) * BANK)
                dve.tensor_scalar(self.h[:, t, cols], self.core.x[:, t, cols], self.stat[:, 3, t:t + 1], None, ALU.mult)\
                   .then_inc(self.h_ready, 1)

        def low(n):
            at = self.at(n // 2, n % 2)
            dve.wait_ge(self.hT_act, n + 1)
            dve.tensor_tensor(self.core.hTl[at], self.v[:, n % 2], self.core.hTh[at].bitcast(F32), ALU.subtract)\
               .then_inc(self.hT_dve, 1)

        for n in range(2 * NT):
            t, g = n // 2, n % 2
            dve.wait_ge(self.turned, n + 1)
            if n >= 2:
                low(n - 2)
                dve.wait_ge(self.hT_dve, n - 1)
            for k in range(4):
                f = 4 * g + k
                ins = dve.tensor_scalar(self.v[:, n % 2, k, :], self.bank(t, g)[:, k, :], gain[:, f:f + 1],
                                        None if self.mod is None else shift[:, f:f + 1], ALU.mult,
                                        *(() if self.mod is None else (ALU.add,)))
            ins.then_inc(self.v_ready, 1)
        for n in (2 * NT - 2, 2 * NT - 1):
            low(n)

    def pe(self, pe):
        pe.wait_ge(self.rows_landed, 16 if self.mod is None else 32)
        used = self.n_rows * KD
        pe.transpose(self.core.psum[:, 7, 0:used], self.rows[0:used, :], self.core.ident[0:used, 0:used])\
          .then_inc(self.rows_turned, 1)
        for n in range(2 * NT):
            t, g = n // 2, n % 2
            pe.wait_ge(self.h_ready, n + 1)
            for k in range(4):
                c = (4 * g + k) * P
                ins = pe.transpose(self.bank(t, g)[:, k, :], self.h[:, t, c:c + P], self.core.ident[:, :])
            ins.then_inc(self.turned, 1)

    def hT_done(self, eng):
        eng.wait_ge(self.hT_act, 2 * NT)
        eng.wait_ge(self.hT_dve, 2 * NT)


class Stream:

    def __init__(self, core, ctx, name, rows, size, land=4, parts=4, lows=None):
        self.land, self.parts, self.lows = land, parts, lows or parts
        self.raw = core.sbuf(ctx, name + "_raw", [rows, land, size])
        self.h = core.sbuf(ctx, name + "_h", [rows, parts, size], F32R)
        self.l = core.sbuf(ctx, name + "_l", [rows, self.lows, size], F32R)
        self.landed = [core.sem(f"{name}_landed{k}") for k in range(land)]
        self.rounded, self.split, self.used = (core.sem(f"{name}_{n}") for n in ("rounded", "split", "used"))

    def load(self, sp, base, j, copy):
        wait_past(sp, self.split, base + j - self.land + 1)
        copy(self.raw[:, j % self.land, :]).then_inc(self.landed[j % self.land], 16)

    def round(self, act, base, j):
        act.wait_ge(self.landed[j % self.land], base * 16 // self.land + (j // self.land + 1) * 16
                    if isinstance(base, int) else base * (16 // self.land) + (j // self.land + 1) * 16)
        wait_past(act, self.used, base + j - self.parts + 1)
        act.copy(self.h[:, j % self.parts, :], self.raw[:, j % self.land, :]).then_inc(self.rounded, 1)

    def subtract(self, eng, base, j):
        eng.wait_ge(self.rounded, base + j + 1)
        if self.lows != self.parts:
            wait_past(eng, self.used, base + j - self.lows + 1)
        eng.tensor_tensor(self.l[:, j % self.lows, :], self.raw[:, j % self.land, :],
                          self.h[:, j % self.parts, :].bitcast(F32), ALU.subtract).then_inc(self.split, 1)

    def ready(self, pe, base, j):
        pe.wait_ge(self.split, base + j + 1)
        return self.h[:, j % self.parts, :], self.l[:, j % self.lows, :]


def three(pe, out, ah, al, bh, bl, start, stop):
    pe.matmul(out, ah, bh, start=start, stop=False)
    pe.matmul(out, ah, bl, start=False, stop=False)
    return pe.matmul(out, al, bh, start=False, stop=stop)


class Project:

    PER = 4
    BL = KD // PER

    def __init__(self, core, ctx, name, w, lT, chunks, evacuate, first_bank=4, land=8):
        self.core, self.w, self.lT, self.chunks, self.evacuate, self.first_bank = core, w, lT, chunks, evacuate, first_bank
        self.stream = Stream(core, ctx, name, P, self.BL * BANK, land=land)
        self.product = core.sem(name + "_product")
        self.taken = [core.sem(f"{name}_taken{t}") for t in range(NT)]

    def load(self, sp):
        view = self.w.rearrange("(k p) c -> p k c", p=P)
        for n in range(self.PER * len(self.chunks)):
            c0, width = self.chunks[n // self.PER]
            k = n % self.PER * self.BL
            self.stream.load(sp, 0, n, lambda place: sp.dma_start(
                place[:, 0:self.BL * width].rearrange("p (k c) -> p k c", k=self.BL), view[:, k:k + self.BL, c0:c0 + width]))

    def bank(self, c, t, width):
        return self.core.psum[:, self.first_bank + (NT * c + t) % 4, 0:width]

    def pe(self, pe):
        ah, al = self.lT
        for n in range(self.PER * len(self.chunks)):
            c, (c0, width) = n // self.PER, self.chunks[n // self.PER]
            if n % self.PER == 0 and c >= 2:
                for t in range(NT):
                    pe.wait_ge(self.taken[t], c - 1)
            wh, wl = self.stream.ready(pe, 0, n)
            for b in range(self.BL):
                k = n % self.PER * self.BL + b
                cols = slice(b * width, (b + 1) * width)
                for t in range(NT):
                    tok = slice(t * P, (t + 1) * P)
                    ins = three(pe, self.bank(c, t, width), ah[:, k, tok], al[:, k, tok], wh[:, cols], wl[:, cols],
                                k == 0, k == KD - 1)
                    if k == KD - 1 and t < NT - 1:
                        ins.then_inc(self.product, 1)
            ins.then_inc(self.stream.used, 1)

    def used_up(self, eng, c, t):
        if t < NT - 1:
            eng.wait_ge(self.product, c + 1)
        else:
            eng.wait_ge(self.stream.used, self.PER * (c + 1))

    def run(self, eng, work, tiles):
        for c in range(len(self.chunks) + 1):
            if c < len(self.chunks) and work is not None:
                for j in range(self.PER):
                    work(eng, 0, self.PER * c + j)
            if c:
                c0, width = self.chunks[c - 1]
                for t in tiles:
                    self.used_up(eng, c - 1, t)
                    self.evacuate(eng, c - 1, c0, width, t, self.bank(c - 1, t, width)).then_inc(self.taken[t], 1)


class ProjectT:

    def __init__(self, core, ctx, name, w, m, blocks, evacuate, first_bank=4, land=8):
        self.core, self.w, self.m, self.n = core, w, m, blocks
        self.evacuate, self.first_bank = evacuate, first_bank
        self.stream = Stream(core, ctx, name, P, KD * m, land=land)
        self.taken = [core.sem(f"{name}_taken{j}") for j in range(2)]

    def load(self, sp):
        view = self.w.rearrange("(k p) c -> p k c", p=P)
        for b in range(self.n):
            self.stream.load(sp, 0, b, lambda place: sp.dma_start(
                place.rearrange("p (k c) -> p k c", k=KD), view[:, :, b * self.m:(b + 1) * self.m]))

    def bank(self, b):
        return self.core.psum[0:self.m, self.first_bank + b // 2 % 4, b % 2 * SEQ:(b % 2 + 1) * SEQ]

    def pe(self, pe):
        for b in range(self.n):
            if b % 2 == 0 and b >= 8:
                pe.wait_ge(self.taken[b // 2 % 2], 2 * (b // 2 // 2 - 2) + 2)
            wh, wl = self.stream.ready(pe, 0, b)
            for k in range(KD):
                cols = slice(k * self.m, (k + 1) * self.m)
                ins = three(pe, self.bank(b), wh[:, cols], wl[:, cols], self.core.hTh[:, k, :], self.core.hTl[:, k, :],
                            k == 0, k == KD - 1)
            ins.then_inc(self.stream.used, 1)

    def run(self, eng, work, which):
        for b in range(self.n + 3):
            if b < self.n and work is not None:
                work(eng, 0, b)
            pair = (b - 3) // 2
            if b % 2 and pair >= 0 and pair % 2 == which:
                eng.wait_ge(self.stream.used, 2 * pair + 2)
                for c in (2 * pair, 2 * pair + 1):
                    self.evacuate(eng, c, self.bank(c)).then_inc(self.taken[which], 1)


def copy_on(eng, out, in_):
    return eng.copy(out, in_) if isinstance(eng, bass.BassScalarEngine) else eng.tensor_copy(out, in_)


class Attention:

    def __init__(self, core, ctx, name, proj, qk, value, bias, lam=None, decay=None, sub_gain=None, gate=None):
        self.core, self.proj, self.qk, self.value, self.bias = core, proj, qk, value, bias
        self.lam, self.decay, self.sub_gain, self.gate = lam, decay, sub_gain, gate
        sb = lambda n, s: core.sbuf(ctx, name + "_" + n, s)
        self.squares = sb("squares", [P, 2, BANK])
        self.stat = sb("stat", [P, 4, NT, 4, 8])
        self.gains = sb("gains", [P, 4, HD])
        self.qT = sb("qT", [P, 8, SEQ])
        self.kT = sb("kT", [P, 8, SEQ])
        self.probs = sb("probs", [P, 2, CAUSAL])
        self.probsT = sb("probsT", [P, 2, CAUSAL])
        self.negmax = sb("negmax", [P, MAPS, NT])
        self.rowsum = sb("rowsum", [P, MAPS, NT])
        self.inv = sb("inv", [P, MAPS, NT])
        self.y = sb("y", [P, NT, D])
        self.yTh, self.yTl = core.hTh, core.hTl
        s = lambda n: core.sem(name + "_" + n)
        self.gains_landed, self.gains_ready = s("gains_landed"), s("gains_ready")
        self.squared, self.summed, self.var_ready, self.std_ready = s("squared"), s("summed"), s("var_ready"), s("std_ready")
        self.scaled, self.normed, self.turned = s("scaled"), s("normed"), s("turned")
        self.qkT_act, self.qkT_dve = s("qkT_by_act"), s("qkT_by_dve")
        self.chain_sem = s("dve_chain")
        self.score_done, self.exped = s("score_done"), s("exped")
        self.p_turned, self.pT_ready, self.pv_done, self.y_part = s("p_turned"), s("pT_ready"), s("pv_done"), s("y_part")
        self.maxed = s("maxed")
        self.y_ready, self.y_turned, self.yT_act, self.yT_dve = s("y_ready"), s("y_turned"), s("yT_by_act"), s("yT_by_dve")
        if sub_gain is not None:
            self.sub_sum, self.sub_std = s("sub_sum"), s("sub_std")
            self.sub = sb("sub", [P, 4, NT, 4])

    def load(self, sp):
        for g, (_, gain, _) in enumerate(self.qk):
            sp.dma_start(self.gains[:, g, :], gain.partition_broadcast(P)).then_inc(self.gains_landed, 16)

    def group(self, t, g):
        c = self.qk[g][0]
        return self.proj[:, t, c:c + BANK].rearrange("p (h d) -> p h d", h=8)

    def pool(self, pool):
        pool.wait_ge(self.gains_landed, 64)
        for g, (_, _, query) in enumerate(self.qk):
            pool.tensor_scalar(self.gains[:, g, :], self.gains[:, g, :], HD ** -0.5 if query else 1.0, None,
                               ALU.mult).then_inc(self.gains_ready, 1)
        pool.wait_ge(self.gains_ready, 4)
        for n in range(NT * 4):
            t, g = n // 4, n % 4
            pool.wait_ge(self.scaled, n + 1)
            v = self.group(t, g)
            pool.tensor_tensor(v, v, spread(self.gains[:, g, :], 1, 8), ALU.mult).then_inc(self.normed, 1)

    def act(self, act):
        for n in range(NT * 4):
            t, g = n // 4, n % 4
            if n >= 2:
                act.wait_ge(self.summed, n - 1)
            act.activation(self.squares[:, n % 2, :].rearrange("p (h d) -> p h d", h=8), self.group(t, g),
                           ACT.Square).then_inc(self.squared, 1)
        act.wait_ge(self.var_ready, 1)
        act.activation(self.stat[:, 2], self.stat[:, 1], ACT.Sqrt).then_inc(self.std_ready, 1)
        for n in range(0, NT * 4, 2):
            act.wait_ge(self.turned, n + 1)
            copy_on(act, self.turned_dst(n), self.turned_src(n)).then_inc(self.qkT_act, 1)
        for i in range(MAPS + 1):
            if i < MAPS:
                act.wait_ge(self.maxed, i + 1)
                if i >= 2:
                    act.wait_ge(self.p_turned, i - 1)
                for t in range(NT):
                    a, b = (0, P) if t == 0 else (P, CAUSAL)
                    ins = act.activation(self.probs[:, i % 2, a:b], self.core.psum[:, i % 2, a:b], ACT.Exp,
                                         bias=self.negmax[:, i, t:t + 1],
                                         accum_out=self.rowsum[:, i, t:t + 1])
                    ins.then_inc(self.exped, 1)
            if i >= 1:
                h = i - 1
                act.wait_ge(self.p_turned, h + 1)
                if h >= 2:
                    act.wait_ge(self.pv_done, h - 1)
                act.copy(self.probsT[:, h % 2, :], self.core.psum[:, 2 + h % 2, 0:CAUSAL]).then_inc(self.pT_ready, 1)
        if self.sub_gain is not None:
            act.wait_ge(self.sub_sum, 1)
            act.activation(self.sub[:, 2], self.sub[:, 1], ACT.Sqrt).then_inc(self.sub_std, 1)
        for n in range(4):
            act.wait_ge(self.y_turned, n + 1)
            act.copy(self.yT_dst(self.yTh, n), self.turned_src(n)).then_inc(self.yT_act, 1)

    def turned_src(self, n):
        return self.core.psum[:, n, :].rearrange("p (j q) -> p j q", j=4)

    def turned_dst(self, n):
        t, g = n // 4, n % 4
        dst = self.qT if self.qk[g][2] else self.kT
        half = [j for j in range(4) if self.qk[j][2] == self.qk[g][2]].index(g)
        return dst[:, 4 * half:4 * half + 4, t * P:(t + 1) * P]

    def yT_dst(self, yT, n):
        t, g = n // 2, n % 2
        return yT[:, 4 * g:4 * g + 4, t * P:(t + 1) * P]

    def out(self, h, t):
        if self.lam is not None and h < DIFF_MAPS:
            w, c = 2 * HD, (h // 2) * 2 * HD
        else:
            w, c = HD, h * HD
        return self.core.psum[:, 4 + h % 2, t * P:t * P + w], self.y[:, t, c:c + w]

    def dve(self, dve):
        chain = Chain(dve, self.chain_sem)
        for n in range(NT * 4):
            t, g = n // 4, n % 4
            dve.wait_ge(self.squared, n + 1)
            dve.tensor_reduce(self.stat[:, 0, t, g, :], self.squares[:, n % 2, :].rearrange("p (h d) -> p h d", h=8),
                              AX, ALU.add).then_inc(self.summed, 1)
        dve.wait_ge(self.summed, 8)
        dve.tensor_scalar(self.stat[:, 1], self.stat[:, 0], 1.0 / HD, EPS, ALU.mult, ALU.add).then_inc(self.var_ready, 1)
        dve.wait_ge(self.std_ready, 1)
        chain.step(dve.reciprocal(self.stat[:, 3], self.stat[:, 2]))
        for n in range(NT * 4):
            t, g = n // 4, n % 4
            v = self.group(t, g)
            dve.tensor_tensor(v, v, spread(self.stat[:, 3, t, g, :], 2, HD), ALU.mult).then_inc(self.scaled, 1)
        for n in range(1, NT * 4, 2):
            dve.wait_ge(self.turned, n + 1)
            dve.tensor_copy(self.turned_dst(n), self.turned_src(n)).then_inc(self.qkT_dve, 1)
        for i in range(MAPS + 2):
            if i < MAPS:
                dve.wait_ge(self.score_done, i + 1)
                for t in range(NT):
                    a, b = (0, P) if t == 0 else (P, CAUSAL)
                    ins = dve.tensor_reduce(self.negmax[:, i, t:t + 1], self.core.psum[:, i % 2, a:b], AX, ALU.max,
                                            negate=True)
                ins.then_inc(self.maxed, 1)
            if i >= 2:
                h = i - 2
                dve.wait_ge(self.exped, 2 * (h + 1))
                chain.step(dve.reciprocal(self.inv[:, h, :], self.rowsum[:, h, :]))
                second = self.lam is not None and h < DIFF_MAPS and h % 2 == 1
                if second:
                    chain.step(dve.tensor_scalar(self.inv[:, h, :], self.inv[:, h, :], self.lam, None, ALU.mult))
                dve.wait_ge(self.pv_done, h + 1)
                for t in range(NT):
                    o, y = self.out(h, t)
                    if second:
                        dve.wait_ge(self.y_part, h)
                        ins = dve.scalar_tensor_tensor(y, o, self.inv[:, h, t:t + 1], y, ALU.mult, ALU.add)
                    else:
                        ins = dve.tensor_scalar(y, o, self.inv[:, h, t:t + 1], None, ALU.mult)
                ins.then_inc(self.y_part, 1)
        dve.wait_ge(self.y_part, MAPS)
        if self.sub_gain is not None:
            for t in range(NT):
                v = self.y[:, t, 0:BANK].rearrange("p (h d) -> p h d", h=4)
                sq = self.squares[:, t, :].rearrange("p (h d) -> p h d", h=4)
                chain.step(dve.tensor_tensor(sq, v, v, ALU.mult))
                chain.step(dve.tensor_reduce(self.sub[:, 0, t, :], sq, AX, ALU.add))
            dve.tensor_scalar(self.sub[:, 1], self.sub[:, 0], 1.0 / (2 * HD), EPS, ALU.mult, ALU.add)\
               .then_inc(self.sub_sum, 1)
            dve.wait_ge(self.sub_std, 1)
            chain.step(dve.reciprocal(self.sub[:, 3], self.sub[:, 2]))
            chain.step(dve.tensor_scalar(self.sub[:, 3], self.sub[:, 3], 1.0 - LAMBDA_INIT, None, ALU.mult))
            for t in range(NT):
                v = self.y[:, t, 0:BANK].rearrange("p (h d) -> p h d", h=4)
                chain.step(dve.tensor_tensor(v, v, spread(self.sub[:, 3, t, :], 2, 2 * HD), ALU.mult))
                dve.tensor_tensor(v, v, spread(self.sub_gain, 1, 4), ALU.mult).then_inc(self.y_ready, 1)
        elif self.gate is not None:
            for t in range(NT):
                dve.tensor_tensor(self.y[:, t, :], self.y[:, t, :], self.gate(dve, t), ALU.mult)\
                   .then_inc(self.y_ready, 1)
        for n in range(4):
            dve.wait_ge(self.yT_act, n + 1)
            dve.tensor_tensor(self.yT_dst(self.yTl, n), self.turned_src(n), self.yT_dst(self.yTh, n).bitcast(F32),
                              ALU.subtract).then_inc(self.yT_dve, 1)

    def pe(self, pe):
        ident = self.core.ident
        for n in range(NT * 4):
            t, g = n // 4, n % 4
            pe.wait_ge(self.normed, n + 1)
            c = self.qk[g][0]
            for j in range(4):
                ins = pe.transpose(self.turned_src(n)[:, j, :], self.proj[:, t, c + j * P:c + (j + 1) * P], ident[:, :])
            ins.then_inc(self.turned, 1)
        pe.wait_ge(self.qkT_act, 4)
        pe.wait_ge(self.qkT_dve, 4)
        for i in range(MAPS + 2):
            if i < MAPS:
                if i >= 2:
                    pe.wait_ge(self.exped, 2 * (i - 1))
                a = i % 2 * HD
                for t in range(NT):
                    n = P * (t + 1)
                    out = self.core.psum[:, i % 2, P * t:P * t + n]
                    turn, tile = self.bias(i)
                    pe.matmul(out, turn[:, :], tile[:, P * t:P * t + n], start=True, stop=False)
                    ins = pe.matmul(out, self.qT[a:a + HD, i // 2, t * P:(t + 1) * P], self.kT[a:a + HD, i // 2, 0:n],
                                    start=False, stop=self.decay is None)
                    if self.decay is not None:
                        left, right = self.decay
                        ins = pe.matmul(out, left[:, i, t * P:(t + 1) * P], right[:, i, 0:n], start=False, stop=True)
                ins.then_inc(self.score_done, 1)
            if 1 <= i <= MAPS:
                h = i - 1
                pe.wait_ge(self.exped, 2 * (h + 1))
                if h >= 2:
                    pe.wait_ge(self.pT_ready, h - 1)
                for j in range(3):
                    ins = pe.transpose(self.core.psum[:, 2 + h % 2, j * P:(j + 1) * P],
                                       self.probs[:, h % 2, j * P:(j + 1) * P], ident[:, :])
                ins.then_inc(self.p_turned, 1)
            if i >= 2:
                h = i - 2
                pe.wait_ge(self.pT_ready, h + 1)
                if h >= 2:
                    pe.wait_ge(self.y_part, h - 1)
                pt = self.probsT[:, h % 2, :].rearrange("p (j q) -> p j q", j=3)
                pe.matmul(self.out(h, 0)[0], pt[:, 0, :], self.value(h, 0), start=True, stop=True)
                pe.matmul(self.out(h, 1)[0], pt[:, 1, :], self.value(h, 0), start=True, stop=False)
                pe.matmul(self.out(h, 1)[0], pt[:, 2, :], self.value(h, 1), start=False, stop=True)\
                  .then_inc(self.pv_done, 1)
        for n in range(4):
            t, g = n // 2, n % 2
            pe.wait_ge(self.y_ready, t + 1)
            for j in range(4):
                c = (4 * g + j) * P
                ins = pe.transpose(self.turned_src(n)[:, j, :], self.y[:, t, c:c + P], ident[:, :])
            ins.then_inc(self.y_turned, 1)
        pe.wait_ge(self.yT_dve, 4)


def column_chunks(first, last):
    return [(c, min(BANK, last - c)) for c in range(first, last, BANK)]


def stage_start(core):
    nc, d = core.nc, core.dram
    landed, ones_set = core.sem("start_landed"), core.sem("ones_set")
    with nc.Block() as block:
        @block.sync
        def _(sp):
            sp.dma_start(core.x[:, :, :], d["x"].rearrange("b (t p) c -> p (b t) c", p=P)).then_inc(landed, 16)
            sp.dma_start(core.ident[:, :], d["c_ident"]).then_inc(landed, 16)
            sp.wait_ge(landed, 32)

        @block.vector
        def _(dve):
            dve.memset(core.ones[:, :], 1.0).then_inc(ones_set, 1)
            dve.wait_ge(ones_set, 1)


def stage_mix1(core):
    nc, d = core.nc, core.dram
    with ExitStack() as ctx:
        width = 3 * D
        proj = core.sbuf(ctx, "mix1_proj", [P, NT, width])
        bias = core.sbuf(ctx, "rel_bias_tiles", [P, N_REL_HEADS, CAUSAL])
        flip = core.sbuf(ctx, "flip", [P, P])
        with ExitStack() as inner:
            norm = Norm(core, inner, "norm1", d["norm1_g"][0])
            table = core.sbuf(inner, "rel_table", [N_BUCKETS + 1, N_REL_HEADS])
            buckets = core.sbuf(inner, "bucket_onehot", [N_BUCKETS + 1, BANK])
            curve = core.sbuf(inner, "bias_curve", [N_REL_HEADS, BANK])
            table_landed, mask_row = core.sem("rel_table_landed"), core.sem("rel_mask_row")
            curve_done, curve_copied = core.sem("curve_done"), core.sem("curve_copied")
            curve_stored, bias_landed = core.sem("curve_stored"), core.sem("bias_landed")

            def take(eng, c, c0, w, t, src):
                return copy_on(eng, proj[:, t, c0:c0 + w], src)

            win = Project(core, inner, "w_in", d["w_in"][0], (core.hTh, core.hTl), column_chunks(0, width), take)
            with nc.Block() as block:
                @block.sync
                def _(sp):
                    norm.load(sp)
                    sp.dma_start(table[0:N_BUCKETS, :], d["rel_bias"]).then_inc(table_landed, 16)
                    sp.dma_start(flip[:, :], d["c_flip"]).then_inc(table_landed, 16)
                    sp.dma_start(buckets[:, :], d["c_buckets"]).then_inc(table_landed, 16)
                    win.load(sp)

                @block.gpsimd
                def _(pool):
                    pool.memset(table[N_BUCKETS:N_BUCKETS + 1, :], NEG).then_inc(mask_row, 1)
                    pool.wait_ge(curve_copied, 1)
                    pool.dma_start(d["curve"], curve[:, :]).then_inc(curve_stored, 16)
                    pool.wait_ge(curve_stored, 16)
                    t = d["curve"]
                    for tile in range(NT):
                        src = bass.AP(t.tensor, SEQ - (tile + 1) * P, [[1, P], [BANK, N_REL_HEADS], [1, P * (tile + 1)]])
                        pool.dma_start(bias[:, :, tile * P:tile * P + P * (tile + 1)], src).then_inc(bias_landed, 16)
                    pool.wait_ge(bias_landed, 32)

                @block.scalar
                def _(act):
                    norm.act(act)
                    win.run(act, win.stream.round, [1])

                @block.vector
                def _(dve):
                    dve.wait_ge(curve_done, 1)
                    dve.tensor_copy(curve[:, :], core.psum[0:N_REL_HEADS, 4, :]).then_inc(curve_copied, 1)
                    norm.dve(dve)
                    win.run(dve, win.stream.subtract, [0])

                @block.tensor
                def _(pe):
                    pe.wait_ge(table_landed, 48)
                    pe.wait_ge(mask_row, 1)
                    pe.matmul(core.psum[0:N_REL_HEADS, 4, :], table[:, :], buckets[:, :], start=True, stop=True)\
                      .then_inc(curve_done, 1)
                    norm.pe(pe)
                    norm.hT_done(pe)
                    pe.wait_ge(curve_copied, 1)
                    win.pe(pe)

        lam_rows = core.sbuf(ctx, "lambda_rows", [P, 4, HD])
        lam = core.sbuf(ctx, "lambda", [P, 4])
        subg = core.sbuf(ctx, "diff_sub_gain", [P, 2 * HD])
        rows_landed, lam_dot, lam_exp, lam_chain = (core.sem("lambda_rows_landed"), core.sem("lambda_dot"),
                                                    core.sem("lambda_exp"), core.sem("lambda_chain"))
        qk = [(0, d["diff_q_g"][0], True), (D // 2, d["diff_k_g"][0], False),
              (3 * D // 2, d["moba_q_g"][0], True), (2 * D, d["moba_k_g"][0], False)]

        def value(h, t):
            if h < DIFF_MAPS:
                return proj[:, t, D + (h // 2) * 2 * HD:D + (h // 2 + 1) * 2 * HD]
            c = 5 * D // 2 + (h - DIFF_MAPS) * HD
            return proj[:, t, c:c + HD]

        def bias_of(h):
            return flip, bias[:, h // 2 if h < DIFF_MAPS else h - DIFF_MAPS + 4, :]

        att = Attention(core, ctx, "mix1", proj, qk, value, bias_of, lam=lam[:, 3:4], sub_gain=subg[:, :])

        def add(eng, c, c0, w, t, src):
            return eng.tensor_tensor(core.x[:, t, c0:c0 + w], src, core.x[:, t, c0:c0 + w], ALU.add)

        wout = Project(core, ctx, "w_out", d["w_out"][0], (att.yTh, att.yTl), column_chunks(0, D), add, land=4)
        with nc.Block() as block:
            @block.sync
            def _(sp):
                att.load(sp)
                for n, name in enumerate(("lambda_q1", "lambda_k1", "lambda_q2", "lambda_k2")):
                    sp.dma_start(lam_rows[:, n, :], d[name][0].partition_broadcast(P)).then_inc(rows_landed, 16)
                sp.dma_start(subg[:, :], d["diff_sub_g"][0].partition_broadcast(P)).then_inc(rows_landed, 16)
                wout.load(sp)

            @block.gpsimd
            def _(pool):
                att.pool(pool)

            @block.scalar
            def _(act):
                act.wait_ge(lam_dot, 1)
                act.activation(lam[:, 0:2], lam[:, 0:2], ACT.Exp).then_inc(lam_exp, 1)
                att.act(act)
                wout.run(act, wout.stream.round, [])

            @block.vector
            def _(dve):
                chain = Chain(dve, lam_chain)
                dve.wait_ge(rows_landed, 80)
                pairs = lam_rows[:, :, :].rearrange("p (a b) d -> p b a d", b=2)
                chain.step(dve.tensor_tensor(pairs[:, 0], pairs[:, 0], pairs[:, 1], ALU.mult))
                dve.tensor_reduce(lam[:, 0:2], pairs[:, 0], AX, ALU.add).then_inc(lam_dot, 1)
                dve.wait_ge(lam_exp, 1)
                chain.step(dve.tensor_tensor(lam[:, 2:3], lam[:, 1:2], lam[:, 0:1], ALU.subtract))
                chain.step(dve.tensor_scalar(lam[:, 3:4], lam[:, 2:3], -LAMBDA_INIT, None, ALU.add))
                att.dve(dve)
                wout.run(dve, wout.stream.subtract, [0, 1])

            @block.tensor
            def _(pe):
                att.pe(pe)
                wout.pe(pe)


def stage_moe(core):
    nc, d = core.nc, core.dram
    with ExitStack() as ctx:
        route = core.sbuf(ctx, "route_w", [P, KD, GROUPS + EXPERTS])
        cw = core.sbuf(ctx, "combine_w", [P, NT, EXPERTS])
        stream = Stream(core, ctx, "moe", P, D, land=8)
        gu0_done, hid_done = core.sem("moe_gate_up0_done"), [core.sem(f"moe_hid_done{t}") for t in range(NT)]
        GU = lambda t: core.psum[:, t, :]

        def gate_up(pe, e, base, j0):
            for j in range(4):
                wh, wl = stream.ready(pe, base, j0 + j)
                for b in range(2):
                    k = 2 * j + b
                    cols = slice(b * 2 * HIDDEN, (b + 1) * 2 * HIDDEN)
                    for t in range(NT):
                        if k == 0:
                            wait_past(pe, hid_done[t], e)
                        tok = slice(t * P, (t + 1) * P)
                        ins = three(pe, GU(t), core.hTh[:, k, tok], core.hTl[:, k, tok], wh[:, cols], wl[:, cols],
                                    k == 0, k == KD - 1)
                        if k == KD - 1 and t == 0:
                            ins.then_inc(gu0_done, 1)
                ins.then_inc(stream.used, 1)

        with ExitStack() as inner:
            norm = Norm(core, inner, "norm2", d["norm2_g"][0])
            L = core.sbuf(inner, "route_logits", [P, NT, GROUPS + EXPERTS])
            rev = core.sbuf(inner, "route_rev", [P, PER_GROUP])
            small = core.sbuf(inner, "route_small", [P, 16, NT])
            g4 = core.sbuf(inner, "route_g4", [P, 4, NT, GROUPS])
            g8 = core.sbuf(inner, "route_g8", [P, 8, NT, PER_GROUP])
            masked = core.sbuf(inner, "route_masked", [P, NT, EXPERTS])
            route_landed, logits_done = core.sem("route_landed"), core.sem("route_logits_done")
            route_split = core.sem("route_split")
            route_h, route_l = (core.sbuf(inner, n, [P, KD, GROUPS + EXPERTS], F32R) for n in ("route_h", "route_l"))
            rc, to_exp, exp_done = core.sem("route_chain"), core.sem("route_to_exp"), core.sem("route_exp_done")
            with nc.Block() as block:
                @block.sync
                def _(sp):
                    norm.load(sp)
                    sp.dma_start(route[:, :, :], d["router"]).then_inc(route_landed, 16)
                    sp.dma_start(rev[:, :], d["c_rev"]).then_inc(route_landed, 16)
                    for n in range(stream.land):
                        stream.load(sp, 0, n, lambda place: sp.dma_start(place, d["moe_w"][n]))

                @block.tensor
                def _(pe):
                    norm.pe(pe)
                    norm.hT_done(pe)
                    pe.wait_ge(route_split, 2)
                    for t in range(NT):
                        tok = slice(t * P, (t + 1) * P)
                        for k in range(KD):
                            ins = three(pe, core.psum[:, 4 + t, 0:GROUPS + EXPERTS], core.hTh[:, k, tok],
                                        core.hTl[:, k, tok], route_h[:, k, :], route_l[:, k, :], k == 0, k == KD - 1)
                    ins.then_inc(logits_done, 1)
                    gate_up(pe, 0, 0, 0)

                @block.scalar
                def _(act):
                    norm.act(act)
                    act.wait_ge(route_landed, 32)
                    act.copy(route_h[:, :, :], route[:, :, :]).then_inc(route_split, 1)
                    for n in range(4):
                        stream.round(act, 0, n)
                    for n, v in enumerate((g4[:, 3], small[:, 5])):
                        act.wait_ge(to_exp, n + 1)
                        act.activation(v, v, ACT.Exp).then_inc(exp_done, 1)

                @block.vector
                def _(dve):
                    norm.dve(dve)
                    chain = Chain(dve, rc)
                    TT = lambda o, a, b, op: chain.step(dve.tensor_tensor(o, a, b, op))
                    RED = lambda o, a, op: chain.step(dve.tensor_reduce(o, a, AX, op))

                    def first_max(v, top, tmp, pos, onehot, n):
                        RED(top, v, ALU.max)
                        TT(tmp, v, spread(top, 2, n), ALU.is_equal)
                        TT(tmp, tmp, spread(rev[:, PER_GROUP - n:PER_GROUP], 1, NT), ALU.mult)
                        RED(pos, tmp, ALU.max)
                        TT(onehot, tmp, spread(pos, 2, n), ALU.is_equal)

                    dve.wait_ge(route_split, 1)
                    dve.tensor_tensor(route_l[:, :, :], route[:, :, :], route_h[:, :, :].bitcast(F32), ALU.subtract)\
                       .then_inc(route_split, 1)
                    for n in range(4):
                        stream.subtract(dve, 0, n)
                    dve.wait_ge(logits_done, 1)
                    chain.step(dve.tensor_copy(L[:, :, :], core.psum[:, 4:4 + NT, 0:GROUPS + EXPERTS]))
                    gl = L[:, :, 0:GROUPS]
                    gtop = small[:, 0]
                    group = g4[:, 1]
                    first_max(gl, gtop, g4[:, 0], small[:, 1], group, GROUPS)
                    dve.tensor_tensor(g4[:, 3], gl, spread(gtop, 2, GROUPS), ALU.subtract).then_inc(to_exp, 1)
                    dve.wait_ge(exp_done, 1)
                    RED(small[:, 2], g4[:, 3], ALU.add)
                    chain.step(dve.reciprocal(small[:, 2], small[:, 2]))
                    el = L[:, :, GROUPS:].rearrange("p t (g e) -> p t g e", g=GROUPS)
                    mk = masked[:, :, :].rearrange("p t (g e) -> p t g e", g=GROUPS)
                    for t in range(NT):
                        TT(mk[:, t], el[:, t], spread(group[:, t], 2, PER_GROUP), ALU.mult)
                        RED(g8[:, 0, t], mk[:, t].rearrange("p g e -> p e g"), ALU.add)
                    first_max(g8[:, 0], small[:, 3], g8[:, 1], small[:, 4], g8[:, 2], PER_GROUP)
                    chain.step(dve.scalar_tensor_tensor(g8[:, 3], g8[:, 2], NEG, g8[:, 0], ALU.mult, ALU.add))
                    first_max(g8[:, 3], small[:, 6], g8[:, 4], small[:, 4], g8[:, 5], PER_GROUP)
                    dve.tensor_tensor(small[:, 5], small[:, 6], small[:, 3], ALU.subtract).then_inc(to_exp, 1)
                    dve.wait_ge(exp_done, 2)
                    chain.step(dve.tensor_scalar(small[:, 7], small[:, 5], 1.0, None, ALU.add))
                    chain.step(dve.reciprocal(small[:, 8], small[:, 7]))
                    TT(small[:, 8], small[:, 8], small[:, 2], ALU.mult)
                    TT(small[:, 9], small[:, 8], small[:, 5], ALU.mult)
                    TT(g8[:, 2], g8[:, 2], spread(small[:, 8], 2, PER_GROUP), ALU.mult)
                    TT(g8[:, 5], g8[:, 5], spread(small[:, 9], 2, PER_GROUP), ALU.mult)
                    TT(g8[:, 6], g8[:, 2], g8[:, 5], ALU.add)
                    for t in range(NT):
                        TT(cw[:, t, :].rearrange("p (g e) -> p g e", g=GROUPS), spread(g8[:, 6, t], 1, GROUPS),
                           spread(group[:, t], 2, PER_GROUP), ALU.mult)

        TURNS = 4
        PIECES = 6
        LOOPS = (EXPERTS - 1) // TURNS
        HJ = HIDDEN // P
        silu = core.sbuf(ctx, "moe_silu", [P, NT, HIDDEN])
        hid = core.sbuf(ctx, "moe_hid", [P, NT, HIDDEN])
        hidTh, hidTl = (core.sbuf(ctx, n, [P, 2, NT, HJ, P], F32R) for n in ("moe_hidTh", "moe_hidTl"))
        zero = core.sbuf(ctx, "moe_zero", [P, P])
        zeroT = core.sbuf(ctx, "moe_zeroT", [P, BANK])
        acc = core.sbuf(ctx, "mod_acc", [P, MODS, MODW])
        modw = core.sbuf(ctx, "mod_w", [P, 2, MODW])
        modc = core.sbuf(ctx, "mod_c", [P, KD])
        per_tile = lambda n: [core.sem(f"moe_{n}{t}") for t in range(NT)]
        silu_done = per_tile("silu_done")
        hid_turned, hidTh_ready, hidTl_ready = (core.sem("moe_" + n) for n in ("hid_turned", "hidTh_ready", "hidTl_ready"))
        zeroed, y_done, added = core.sem("moe_zeroed"), core.sem("moe_y_done"), core.sem("moe_added")
        mod_added, modw_landed = core.sem("mod_added"), [core.sem(f"mod_w_landed{s}") for s in range(2)]
        modc_landed, modc_ready = core.sem("mod_c_landed"), core.sem("mod_c_ready")

        TP = core.psum[:, 2, :].rearrange("p (t j n) -> p t j n", t=NT, j=HJ)
        Y = lambda t, c: core.psum[:, 4 + 2 * t + c, :]

        def over_experts(eng, first, turn, last):
            first()
            for s in range(TURNS):
                turn(0, s)
            with eng.Fori(1, LOOPS) as i:
                for s in range(TURNS):
                    turn(i, s)
            for s in range((EXPERTS - 1) % TURNS):
                turn(LOOPS, s)
            last()

        def number(i, s):
            return i * TURNS + s + 1, i * (TURNS * PIECES), 4 + PIECES * s

        LAST = PIECES * EXPERTS - 2

        with nc.Block() as block:
            @block.sync
            def _(sp):
                sp.dma_start(modc[:, :], d["c_col"]).then_inc(modc_landed, 16)

                def load(base, j):
                    stream.load(sp, base, j, lambda place: sp.dma_start(place, d["moe_w"][bass.ds(base + j, 1)].rearrange("a p c -> p (a c)")))

                def load_mod(i, s):
                    q = i * TURNS + s
                    wait_past(sp, mod_added, 2 * q - 2)
                    sp.dma_start(modw[:, s % 2, :], d["mod_w"][s][bass.ds(i * P, P), :]).then_inc(modw_landed[s % 2], 16)

                def turn(i, s):
                    e, base, j = number(i, s)
                    for n in range(j, j + PIECES):
                        if not (isinstance(base, int) and base + n < stream.land):
                            load(base, n)
                        if n == j + 2:
                            load_mod(i, s)

                def last():
                    load(0, LAST)
                    load(0, LAST + 1)
                    load_mod(LOOPS, TURNS - 1)

                over_experts(sp, lambda: None, turn, last)

            @block.tensor
            def _(pe):
                pe.wait_ge(zeroed, 2)
                for t in range(NT):
                    for c in range(2):
                        pe.matmul(Y(t, c), zero[:, :], zeroT[:, :], start=True, stop=False)

                def turn_hid(e):
                    wait_past(pe, hidTl_ready, e)
                    for t in range(NT):
                        pe.wait_ge(hid_done[t], e + 1)
                        for j in range(HJ):
                            ins = pe.transpose(TP[:, t, j, :], hid[:, t, j * P:(j + 1) * P], core.ident[:, :])
                    ins.then_inc(hid_turned, 1)

                def down(e, side, base, n, j):
                    pe.wait_ge(hidTl_ready, e + 1)
                    wh, wl = stream.ready(pe, base, n)
                    for t in range(NT):
                        for c in range(2):
                            cols = slice(c * BANK, (c + 1) * BANK)
                            ins = three(pe, Y(t, c), hidTh[:, side, t, j, :], hidTl[:, side, t, j, :], wh[:, cols],
                                        wl[:, cols], False, False)
                    ins.then_inc(stream.used, 1)

                def first():
                    turn_hid(0)

                def turn(i, s):
                    e, base, j = number(i, s)
                    gate_up(pe, e, base, j)
                    down(e - 1, s % 2, base, j + 4, 0)
                    turn_hid(e)
                    down(e - 1, s % 2, base, j + 5, 1)

                def last():
                    for j in range(HJ):
                        down(EXPERTS - 1, (EXPERTS - 1) % 2, 0, LAST + j, j)
                    for t in range(NT):
                        for c in range(2):
                            ins = pe.matmul(Y(t, c), zero[:, :], zeroT[:, :], start=False, stop=True)
                    ins.then_inc(y_done, 1)

                over_experts(pe, first, turn, last)

            @block.scalar
            def _(act):
                act.wait_ge(modc_landed, 16)
                act.activation(modc[:, :], modc[:, :], ACT.Silu).then_inc(modc_ready, 1)

                def gates(e, pieces):
                    for t in range(NT):
                        if t == 0:
                            act.wait_ge(gu0_done, e + 1)
                        else:
                            act.wait_ge(stream.used, pieces)
                        act.activation(silu[:, t, :], GU(t)[:, 0:HIDDEN], ACT.Silu).then_inc(silu_done[t], 1)

                def round_hidT(e, side):
                    act.wait_ge(hid_turned, e + 1)
                    act.copy(hidTh[:, side], TP).then_inc(hidTh_ready, 1)

                def first():
                    gates(0, 4)

                def turn(i, s):
                    e, base, j = number(i, s)
                    stream.round(act, base, j)
                    round_hidT(e - 1, s % 2)
                    for n in range(j + 1, j + PIECES):
                        stream.round(act, base, n)
                    gates(e, base + j + 4)

                def last():
                    stream.round(act, 0, LAST)
                    round_hidT(EXPERTS - 1, (EXPERTS - 1) % 2)
                    stream.round(act, 0, LAST + 1)

                over_experts(act, first, turn, last)

            @block.vector
            def _(dve):
                dve.memset(zero[:, :], 0.0).then_inc(zeroed, 1)
                dve.memset(zeroT[:, :], 0.0).then_inc(zeroed, 1)
                dve.wait_ge(modc_ready, 1)

                def make_hid(e):
                    wait_past(dve, hid_turned, e)
                    for t in range(NT):
                        dve.wait_ge(silu_done[t], e + 1)
                        dve.scalar_tensor_tensor(hid[:, t, :], GU(t)[:, HIDDEN:], cw[:, t, bass.ds(e, 1)],
                                                 silu[:, t, :], ALU.mult, ALU.mult).then_inc(hid_done[t], 1)

                def rest_hidT(e, side):
                    dve.wait_ge(hidTh_ready, e + 1)
                    dve.tensor_tensor(hidTl[:, side], TP, hidTh[:, side].bitcast(F32), ALU.subtract).then_inc(hidTl_ready, 1)

                def add_mod(i, s, half):
                    cols = slice(half * MODW // 2, (half + 1) * MODW // 2)
                    dve.wait_ge(modw_landed[s % 2], 32 * i + 16 * (s // 2) + 16)
                    if isinstance(i, int) and i == 0:
                        dve.tensor_scalar(acc[:, s, cols], modw[:, s % 2, cols], modc[:, 0:1], None, ALU.mult)\
                           .then_inc(mod_added, 1)
                        return
                    dve.wait_ge(mod_added, 2 * (i * TURNS + s) + half)
                    dve.scalar_tensor_tensor(acc[:, s, cols], modw[:, s % 2, cols], modc[:, bass.ds(i, 1)],
                                             acc[:, s, cols], ALU.mult, ALU.add).then_inc(mod_added, 1)

                def first():
                    make_hid(0)

                def turn(i, s):
                    e, base, j = number(i, s)
                    stream.subtract(dve, base, j)
                    rest_hidT(e - 1, s % 2)
                    stream.subtract(dve, base, j + 1)
                    stream.subtract(dve, base, j + 2)
                    add_mod(i, s, 0)
                    for n in range(j + 3, j + PIECES):
                        stream.subtract(dve, base, n)
                    make_hid(e)
                    add_mod(i, s, 1)

                def last():
                    stream.subtract(dve, 0, LAST)
                    rest_hidT(EXPERTS - 1, (EXPERTS - 1) % 2)
                    stream.subtract(dve, 0, LAST + 1)
                    add_mod(LOOPS, TURNS - 1, 0)
                    add_mod(LOOPS, TURNS - 1, 1)

                over_experts(dve, first, turn, last)
                dve.wait_ge(y_done, 1)
                for t in range(NT):
                    for c in range(2):
                        x = core.x[:, t, c * BANK:(c + 1) * BANK]
                        dve.tensor_tensor(x, Y(t, c), x, ALU.add).then_inc(added, 1)
                dve.wait_ge(added, 4)
                dve.wait_ge(mod_added, 2 * EXPERTS)

        NC = MODW // BANK
        b_landed, summed, rows_ready, rows_stored = (core.sem("mod_" + n) for n in (
            "b_landed", "summed", "rows_ready", "rows_stored"))
        with nc.Block() as block:
            @block.sync
            def _(sp):
                for m in range(MODS):
                    if m >= 2:
                        sp.wait_ge(rows_ready, NC * (m - 1))
                    sp.dma_start(modw[0:1, m % 2, :], d["mod_b"][m].unsqueeze(0)).then_inc(b_landed, 16)
                    sp.wait_ge(b_landed, 16 * m + 16)
                for m in range(MODS):
                    sp.wait_ge(rows_ready, NC * (m + 1))
                    sp.dma_start(d["mod_rows"][m].unsqueeze(0), acc[0:1, m, :]).then_inc(rows_stored, 16)
                sp.wait_ge(rows_stored, 16 * MODS)

            @block.tensor
            def _(pe):
                for n in range(MODS * NC):
                    m, c = n // NC, n % NC
                    wait_past(pe, rows_ready, n - 7)
                    pe.matmul(core.psum[0:1, n % 8, :], core.ones[:, 0:1], acc[:, m, c * BANK:(c + 1) * BANK],
                              start=True, stop=True).then_inc(summed, 1)

            @block.vector
            def _(dve):
                for n in range(MODS * NC):
                    m, c = n // NC, slice(n % NC * BANK, (n % NC + 1) * BANK)
                    dve.wait_ge(b_landed, 16 * m + 16)
                    dve.wait_ge(summed, n + 1)
                    dve.tensor_tensor(acc[0:1, m, c], core.psum[0:1, n % 8, :], modw[0:1, m % 2, c], ALU.add)\
                       .then_inc(rows_ready, 1)


def gated_add(core, dve_chain, eng, tmp, gate, c0, w, t, src):
    dve_chain.step(eng.tensor_tensor(tmp[:, 0:w], src, gate[:, c0:c0 + w], ALU.mult))
    x = core.x[:, t, c0:c0 + w]
    return eng.tensor_tensor(x, tmp[:, 0:w], x, ALU.add)


def stage_lru(core):
    nc, d = core.nc, core.dram
    with ExitStack() as ctx:
        xb = core.sbuf(ctx, "lru_x", [P, LBLK, CONV - 1 + SEQ])
        xc = core.sbuf(ctx, "lru_xc", [P, LBLK, SEQ])
        gb = core.sbuf(ctx, "lru_gelu", [P, LBLK, SEQ])
        vec = core.sbuf(ctx, "lru_vectors", [P, 4 + CONV, LBLK])
        nsp = core.sbuf(ctx, "lru_decay", [P, 2, LBLK])
        gate = core.sbuf(ctx, "lru_gate", [P, D])
        tiles = gate_tiles()
        gw = core.sbuf(ctx, "lru_gate_w", [P, 2, len(tiles), P])
        gw_landed = core.sem("lru_gw_landed")
        vec_landed, padded, gate_landed = core.sem("lru_vec_landed"), core.sem("lru_padded"), core.sem("lru_gate_landed")
        conved, conv_chain = core.sem("lru_conved"), core.sem("lru_conv_chain")
        with ExitStack() as inner:
            norm = Norm(core, inner, "lru_norm", d["lru_g"], mod=0)

            def take(eng, b, src):
                if b < LBLK:
                    return copy_on(eng, xb[:, b, CONV - 1:], src)
                return copy_on(eng, gb[:, b - LBLK, :], src)

            win = ProjectT(core, inner, "lru_in", d["lru_in"], P, 2 * LBLK, take)
            with nc.Block() as block:
                @block.sync
                def _(sp):
                    norm.load(sp)
                    sp.dma_start(vec[:, :, :], d["lru_vec"]).then_inc(vec_landed, 16)
                    sp.dma_start(gate[:, :], d["mod_rows"][0][2 * D:].partition_broadcast(P)).then_inc(gate_landed, 16)
                    win.load(sp)
                    sp.dma_start(gw[:, :, :, :], d["lru_gate_w"]).then_inc(gw_landed, 16)
                    sp.wait_ge(gate_landed, 16)
                    sp.wait_ge(vec_landed, 16)
                    sp.wait_ge(gw_landed, 16)

                @block.gpsimd
                def _(pool):
                    pool.memset(xb[:, :, 0:CONV - 1], 0.0).then_inc(padded, 1)
                    pool.wait_ge(padded, 1)

                @block.scalar
                def _(act):
                    norm.act(act)
                    win.run(act, win.stream.round, 1)

                @block.vector
                def _(dve):
                    norm.dve(dve)
                    chain = Chain(dve, conv_chain)

                    def conv(b):
                        dve.wait_ge(win.taken[b // 2 % 2], b // 4 * 2 + 2)
                        for j in range(CONV):
                            src = xb[:, b, j:j + SEQ]
                            if j == 0:
                                ins = dve.tensor_scalar(xc[:, b, :], src, vec[:, j, b:b + 1], vec[:, 4, b:b + 1], ALU.mult, ALU.add)
                            else:
                                ins = dve.scalar_tensor_tensor(xc[:, b, :], src, vec[:, j, b:b + 1], xc[:, b, :], ALU.mult, ALU.add)
                            if j < CONV - 1:
                                chain.step(ins)
                        ins.then_inc(conved, 1)

                    LAG = LBLK - 2

                    def work(eng, base, b):
                        if b == LAG:
                            dve.wait_ge(padded, 1)
                            dve.wait_ge(vec_landed, 16)
                        win.stream.subtract(eng, base, b)
                        if LAG <= b < LAG + LBLK:
                            conv(b - LAG)

                    win.run(dve, work, 0)
                    dve.wait_ge(conved, LBLK)

                @block.tensor
                def _(pe):
                    norm.pe(pe)
                    norm.hT_done(pe)
                    win.pe(pe)

        sb = lambda n, s: core.sbuf(ctx, "lru_" + n, s)
        rr, ii, tt = (sb(n, [P, LBLK, SEQ]) for n in ("r", "i", "t"))
        out = Stream(core, ctx, "lru_out", P, D, land=4)
        yh, yl = (core.sbuf(ctx, n, [P, LBLK, SEQ], F32R) for n in ("lru_yh", "lru_yl"))
        tmp = sb("tmp", [P, BANK])
        s = lambda n: core.sem("lru_" + n)
        gates_done, chain_sem = s("gates_done"), s("chain")
        softplus, gelued, r_ready, i_ready, a_ready, t_ready, root_in, root = (s(n) for n in (
            "softplus", "gelued", "r_ready", "i_ready", "a_ready", "t_ready", "root_in", "root"))
        nsp_ready, gated, squared, mixed, scanned = (s(n) for n in ("nsp_ready", "gated", "squared", "mixed", "scanned"))
        y_ready, yh_ready, yl_ready, out_taken = (s(n) for n in ("y_ready", "yh_ready", "yl_ready", "out_taken"))
        CHUNK = 3
        CHUNKS = -(-LBLK // CHUNK)
        end = lambda c: min(CHUNK * (c + 1), LBLK)
        chunk = lambda v, c: v[:, c * CHUNK:end(c), :].rearrange("p b t -> p (b t)")
        flat = lambda v: v.rearrange("p b t -> p (b t)")

        def pieces_after(c):
            return range(max(0, end(c - 2)) + out.land, min(end(c - 1) + out.land, LBLK))

        with nc.Block() as block:
            @block.sync
            def _(sp):
                for b in range(LBLK):
                    out.load(sp, 0, b, lambda place: sp.dma_start(place, d["lru_out"][b * P:(b + 1) * P, :]))

            @block.tensor
            def _(pe):
                for b in range(LBLK):
                    if b >= 4:
                        pe.wait_ge(i_ready, b - 3)
                    mine = [n for n, (_, j) in enumerate(tiles) if j == b]
                    for g in range(2):
                        for n in mine:
                            ins = pe.matmul(core.psum[:, b % 4, g * SEQ:(g + 1) * SEQ], gw[:, g, n, :], xc[:, tiles[n][0], :],
                                            start=n == mine[0], stop=n == mine[-1])
                    ins.then_inc(gates_done, 1)
                for b in range(LBLK):
                    pe.wait_ge(yl_ready, b // CHUNK + 1)
                    wh, wl = out.ready(pe, 0, b)
                    for t in range(NT):
                        tok = slice(t * P, (t + 1) * P)
                        for c in range(2):
                            cols = slice(c * BANK, (c + 1) * BANK)
                            ins = three(pe, core.psum[:, 4 + 2 * c + t, :], yh[:, b, tok], yl[:, b, tok], wh[:, cols],
                                        wl[:, cols], b == 0, b == LBLK - 1)
                    ins.then_inc(out.used, 1)

            @block.scalar
            def _(act):
                act.activation(flat(gb[:, :, :]), flat(gb[:, :, :]), ACT.Gelu).then_inc(gelued, 1)
                act.activation(nsp[:, 0, :], vec[:, 7, :], ACT.Sigmoid).then_inc(softplus, 1)
                act.wait_ge(softplus, 1)
                act.activation(nsp[:, 0, :], nsp[:, 0, :], ACT.Ln).then_inc(softplus, 1)
                for b in range(LBLK):
                    act.wait_ge(gates_done, b + 1)
                    act.activation(rr[:, b, :], core.psum[0:P, b % 4, 0:SEQ], ACT.Sigmoid,
                                   bias=vec[:, 5, b:b + 1]).then_inc(r_ready, 1)
                    act.activation(ii[:, b, :], core.psum[0:P, b % 4, SEQ:], ACT.Sigmoid,
                                   bias=vec[:, 6, b:b + 1]).then_inc(i_ready, 1)
                act.wait_ge(nsp_ready, 1)
                act.wait_ge(r_ready, LBLK)
                for b in range(LBLK):
                    act.activation(tt[:, b, :], rr[:, b, :], ACT.Tanh, scale=nsp[:, 1, b:b + 1]).then_inc(t_ready, 1)
                act.wait_ge(t_ready, LBLK)
                for b in range(LBLK):
                    act.activation(rr[:, b, :], rr[:, b, :], ACT.Exp, scale=nsp[:, 0, b:b + 1]).then_inc(a_ready, 1)
                for b in range(out.land):
                    out.round(act, 0, b)
                for c in range(CHUNKS + 2):
                    if c < CHUNKS:
                        act.wait_ge(root_in, c + 1)
                        act.activation(chunk(tt, c), chunk(tt, c), ACT.Sqrt).then_inc(root, 1)
                    if c >= 2:
                        act.wait_ge(y_ready, c - 1)
                        act.copy(chunk(yh, c - 2), chunk(xc, c - 2)).then_inc(yh_ready, 1)
                        for b in pieces_after(c - 2):
                            out.round(act, 0, b)

            @block.gpsimd
            def _(pool):
                for c in range(CHUNKS):
                    pool.wait_ge(i_ready, end(c))
                    pool.tensor_tensor(chunk(ii, c), chunk(ii, c), chunk(xc, c), ALU.mult).then_inc(gated, 1)

            @block.vector
            def _(dve):
                chain = Chain(dve, chain_sem)
                dve.wait_ge(softplus, 2)
                chain.step(dve.tensor_scalar(nsp[:, 0, :], nsp[:, 0, :], 8.0, None, ALU.mult))
                dve.tensor_scalar(nsp[:, 1, :], nsp[:, 0, :], -1.0, None, ALU.mult).then_inc(nsp_ready, 1)
                for b in range(out.land):
                    out.subtract(dve, 0, b)

                def square(c):
                    dve.wait_ge(gated, c + 1)
                    dve.wait_ge(a_ready, end(c))
                    chain.step(dve.tensor_tensor(chunk(xc, c), chunk(rr, c), chunk(rr, c), ALU.mult))
                    dve.wait_ge(t_ready, end(c))
                    dve.scalar_tensor_tensor(chunk(tt, c), chunk(xc, c), 1.0, chunk(tt, c), ALU.add, ALU.mult)\
                       .then_inc(root_in, 1)

                def scan(c):
                    dve.wait_ge(root, c + 1)
                    dve.tensor_tensor(chunk(ii, c), chunk(ii, c), chunk(tt, c), ALU.mult).then_inc(mixed, 1)
                    dve.wait_ge(mixed, c + 1)
                    for b in range(CHUNK * c, end(c)):
                        dve.tensor_tensor_scan(tt[:, b, :], rr[:, b, :], ii[:, b, :], 0.0, ALU.mult, ALU.add).then_inc(scanned, 1)
                    dve.wait_ge(scanned, end(c))
                    dve.wait_ge(gelued, 1)
                    dve.tensor_tensor(chunk(xc, c), chunk(tt, c), chunk(gb, c), ALU.mult).then_inc(y_ready, 1)

                def low(c):
                    dve.wait_ge(yh_ready, c + 1)
                    dve.wait_ge(y_ready, c + 1)
                    dve.tensor_tensor(chunk(yl, c), chunk(xc, c), chunk(yh, c).bitcast(F32), ALU.subtract).then_inc(yl_ready, 1)
                    for b in pieces_after(c):
                        out.subtract(dve, 0, b)

                square(0)
                for c in range(CHUNKS):
                    if c + 1 < CHUNKS:
                        square(c + 1)
                    scan(c)
                    if c:
                        low(c - 1)
                low(CHUNKS - 1)
                dve.wait_ge(out.used, LBLK)
                for c in range(2):
                    for t in range(NT):
                        gated_add(core, chain, dve, tmp, gate, c * BANK, BANK, t, core.psum[:, 4 + 2 * c + t, :])\
                            .then_inc(out_taken, 1)
                        dve.wait_ge(out_taken, NT * c + t + 1)


def stage_peer(core, layer):
    nc, d = core.nc, core.dram
    L = f"peer{layer}_"
    name = lambda n: L + n
    sem = lambda n: core.sem(L + n)
    N2 = 2 * PHEADS
    R = 4
    TILES = KEYS
    HALF = TILES // 2
    ROUND, SPLIT = 3, 2
    u, v, gelu_rows = d[f"peer{layer}_u"], d[f"peer{layer}_v"], d["gelu_rows"]
    with ExitStack() as ctx:
        stream = Stream(core, ctx, name("uv"), P, D, land=R, parts=R, lows=2)
        spare = core.sbuf(ctx, name("spare"), [P, 5, SEQ])
        G = spare[:, 0:2, :]
        e1T, e2T, gT = spare[:, 2, :], spare[:, 3, :], spare[:, 4, :]
        gelu_done, g_stored = sem("gelu_done"), [sem(f"gelu_stored{s}") for s in range(2)]
        S = lambda n: core.psum[:, n % R, 0:SEQ]
        Y = lambda t, c: core.psum[:, 4 + 2 * t + c, :]

        def load_u(sp, i):
            for j in range(R):
                stream.load(sp, R * i, j, lambda place: sp.dma_start(
                    place, u[bass.ds(R * i + j, 1)].rearrange("a p k c -> p (a k c)")))

        def load_v(sp, i, j):
            stream.load(sp, R * i, j, lambda place: sp.dma_start(place, v[bass.ds((R * i + j - TILES) * P, P), :]))

        def score(pe, i, j):
            wh, wl = stream.ready(pe, R * i, j)
            wait_past(pe, gelu_done, R * i + j - R + 1)
            for k in range(KD):
                cols = slice(k * P, (k + 1) * P)
                ins = three(pe, S(j), wh[:, cols], wl[:, cols], core.hTh[:, k, :], core.hTl[:, k, :], k == 0, k == KD - 1)
            ins.then_inc(stream.used, 1)

        def gelu(act, i, j):
            act.wait_ge(stream.used, R * i + j + 1)
            wait_past(act, g_stored[j % 2], 16 * (R // 2 * i + j // 2))
            act.activation(G[:, j % 2, :], S(j), ACT.Gelu).then_inc(gelu_done, 1)
            stream.round(act, R * i, j + ROUND)
            act.wait_ge(gelu_done, R * i + j + 1)
            act.dma_start(gelu_rows[bass.ds(R * i + j, 1)].rearrange("a p n -> p (a n)"), G[:, j % 2, :])\
               .then_inc(g_stored[j % 2], 16)

        with ExitStack() as inner:
            qT = core.sbuf(inner, name("qT"), [P, N2, SEQ])
            subT = core.sbuf(inner, name("subT"), [P, N2, KEYS])
            sub_landed = sem("sub_landed")
            with ExitStack() as first:
                norm = Norm(core, first, name("norm"), d[f"peer{layer}_g"], mod=2 * layer + 1)
                wq = ProjectT(core, first, name("q"), d[f"peer{layer}_q"], P, N2,
                              lambda eng, b, src: copy_on(eng, qT[:, b, :], src), land=4)
                with nc.Block() as block:
                    @block.sync
                    def _(sp):
                        norm.load(sp)
                        wq.load(sp)
                        sp.dma_start(subT[:, :, :], d[f"peer{layer}_sub"]).then_inc(sub_landed, 16)
                        load_u(sp, 0)
                        sp.wait_ge(sub_landed, 16)

                    @block.scalar
                    def _(act):
                        norm.act(act)
                        wq.run(act, wq.stream.round, 1)

                    @block.vector
                    def _(dve):
                        norm.dve(dve)
                        wq.run(dve, wq.stream.subtract, 0)

                    @block.tensor
                    def _(pe):
                        norm.pe(pe)
                        norm.hT_done(pe)
                        wq.pe(pe)

            sb = lambda n, s, dt=F32: core.sbuf(inner, name(n), s, dt)
            sc = sb("sc", [P, NT, N2, KEYS])
            rest = sb("rest", [P, 2, TOPK * TOPK])
            val = sb("val", [P, NT, N2, TOPK])
            idx = sb("idx", [P, NT, N2, TOPK], U32)
            idxf = sb("idxf", [P, NT, N2, TOPK])
            cand = sb("cand", [P, PHEADS, TOPK * TOPK])
            top = sb("top", [P, NT, PHEADS, TOPK])
            place = sb("place", [P, NT, PHEADS, TOPK], U32)
            digit = sb("digit", [P, 2, PICKS], U32)
            digitf = sb("digitf", [P, 2, PICKS])
            hot = sb("hot", [P, PHEADS, TOPK, TOPK])
            pick = sb("pick", [P, NT, 3, PICKS])
            iota16 = sb("iota16", [P, TOPK])
            summed = sb("sum", [P, NT, PHEADS])
            sc_done, sc_taken, ch = sem("sc_done"), sem("sc_taken"), sem("pick_chain")
            to_exp, exp_done, picked, turned, pickT = sem("to_exp"), sem("exp_done"), sem("picked"), sem("turned"), sem("pickT")
            iota_landed = sem("iota_landed")
            with nc.Block() as block:
                @block.sync
                def _(sp):
                    sp.dma_start(iota16[:, :], d["c_iota"][:, 0:TOPK]).then_inc(iota_landed, 16)
                    with sp.Fori(1, HALF // R + 1) as i:
                        load_u(sp, i)

                @block.tensor
                def _(pe):
                    for n in range(NT * N2 // 4):
                        t, b = n // 4, n % 4 * 4
                        wait_past(pe, sc_taken, n - 3)
                        for j in range(4):
                            ins = pe.matmul(core.psum[:, 4 + n % 4, j * P:(j + 1) * P], qT[:, b + j, t * P:(t + 1) * P],
                                            subT[:, b + j, :], start=True, stop=True)
                        ins.then_inc(sc_done, 1)
                    for j in range(R):
                        score(pe, 0, j)
                    with pe.Fori(1, HALF // R) as i:
                        for j in range(R):
                            score(pe, i, j)
                    pe.wait_ge(sc_taken, 8)
                    for t in range(NT):
                        pe.wait_ge(picked, t + 1)
                        for j in range(3):
                            ins = pe.transpose(core.psum[:, 4 + j, t * P:(t + 1) * P], pick[:, t, j, :], core.ident[:, :])
                    ins.then_inc(turned, 1)

                @block.scalar
                def _(act):
                    for n in range(8):
                        act.wait_ge(sc_done, n + 1)
                        t, b = n // 4, n % 4 * 4
                        act.copy(sc[:, t, b:b + 4, :], core.psum[:, 4 + n % 4, :].rearrange("p (j c) -> p j c", j=4))\
                           .then_inc(sc_taken, 1)
                        if n < ROUND:
                            stream.round(act, 0, n)
                    for j in range(R):
                        gelu(act, 0, j)
                    with act.Fori(1, HALF // R) as i:
                        for j in range(R):
                            gelu(act, i, j)
                    for t in range(NT):
                        act.wait_ge(to_exp, t + 1)
                        act.activation(pick[:, t, 2, :], pick[:, t, 2, :], ACT.Exp).then_inc(exp_done, 1)
                    act.wait_ge(turned, 1)
                    for j, dst in enumerate((e1T, e2T, gT)):
                        act.copy(dst, core.psum[:, 4 + j, 0:SEQ]).then_inc(pickT, 1)
                    act.wait_ge(pickT, 3)

                @block.gpsimd
                def _(pool):
                    for j in range(R + SPLIT):
                        stream.subtract(pool, 0, j)
                    with pool.Fori(1, HALF // R) as i:
                        for j in range(R):
                            stream.subtract(pool, R * i, j + SPLIT)

                @block.vector
                def _(dve):
                    chain = Chain(dve, ch)
                    step = chain.step

                    def top16(values, vals, where, spare):
                        step(dve.max(vals[:, 0:8], values))
                        dve.max_index(where[:, 0:8], vals[:, 0:8], values)
                        step(dve.match_replace(spare, vals[:, 0:8], values, -3.0e38))
                        step(dve.max(vals[:, 8:16], spare))
                        return dve.max_index(where[:, 8:16], vals[:, 8:16], spare)

                    weights = lambda t: pick[:, t, 2, :].rearrange("p (h k) -> p h k", h=PHEADS)
                    dve.wait_ge(iota_landed, 16)
                    for t in range(NT):
                        for b in range(N2):
                            if b % 4 == 0:
                                dve.wait_ge(sc_taken, 4 * t + b // 4 + 1)
                            step(top16(sc[:, t, b, :], val[:, t, b, :], idx[:, t, b, :], rest[:, b % 2, 0:KEYS]))
                        step(dve.tensor_copy(idxf[:, t], idx[:, t]))
                        vv = val[:, t].rearrange("p (h a) k -> p h a k", a=2)
                        f = idxf[:, t].rearrange("p (h a) k -> p h a k", a=2)
                        step(dve.tensor_tensor(cand[:, :, :].rearrange("p h (i j) -> p h i j", i=TOPK),
                                               spread(vv[:, :, 0, :], 3, TOPK), spread(vv[:, :, 1, :], 2, TOPK), ALU.add))
                        for h in range(PHEADS):
                            step(top16(cand[:, h, :], top[:, t, h, :], place[:, t, h, :], rest[:, h % 2, :]))
                        dve.tensor_tensor(weights(t), top[:, t], spread(top[:, t, :, 0], 2, TOPK), ALU.subtract)\
                           .then_inc(to_exp, 1)
                        where = place[:, t].rearrange("p h k -> p (h k)")
                        dve.tensor_scalar(digit[:, 0, :], where, 4, None, ALU.logical_shift_right)
                        step(dve.tensor_scalar(digit[:, 1, :], where, 15, None, ALU.bitwise_and))
                        step(dve.tensor_copy(digitf[:, :, :], digit[:, :, :]))
                        for a in range(2):
                            step(dve.tensor_tensor(hot[:, :, :, :].rearrange("p h k j -> p (h k) j"),
                                                   spread(digitf[:, a, :], 2, TOPK), spread(iota16[:, :], 1, PICKS), ALU.is_equal))
                            step(dve.tensor_tensor(hot[:, :, :, :], hot[:, :, :, :], spread(f[:, :, a, :], 2, TOPK), ALU.mult))
                            step(dve.tensor_reduce(pick[:, t, a, :], hot[:, :, :, :].rearrange("p h k j -> p (h k) j"), AX, ALU.add))
                    for t in range(NT):
                        g = weights(t)
                        dve.wait_ge(exp_done, t + 1)
                        step(dve.tensor_reduce(summed[:, t, :], g, AX, ALU.add))
                        step(dve.reciprocal(summed[:, t, :], summed[:, t, :]))
                        dve.tensor_tensor(g, g, spread(summed[:, t, :], 2, TOPK), ALU.mult).then_inc(picked, 1)

        W = core.sbuf(ctx, name("W"), [P, KEYS, SEQ])
        with ExitStack() as inner:
            TOK = 4
            assert TOK * (TILES - HALF) == SEQ
            iota = core.sbuf(inner, name("iota"), [P, KEYS])
            A = core.sbuf(inner, name("A"), [P, 2, TOK, KEYS])
            B = core.sbuf(inner, name("B"), [P, 2, TOK, KEYS])
            landed, ab_ready, w_done, w_taken = sem("iota128_landed"), sem("ab_ready"), sem("w_done"), sem("w_taken")
            FIRST, END = HALF // R, TILES // R
            w_bank = lambda j: core.psum[:, 4 + j % 2, :]
            with nc.Block() as block:
                @block.sync
                def _(sp):
                    sp.dma_start(iota[:, :], d["c_iota"]).then_inc(landed, 16)
                    with sp.Fori(FIRST + 1, END) as i:
                        load_u(sp, i)
                    for j in range(R):
                        load_v(sp, END, j)
                    sp.wait_ge(landed, 16)

                @block.vector
                def _(dve):
                    dve.wait_ge(landed, 16)

                    def step(i):
                        for j in range(R):
                            g = R * (i - FIRST) + j
                            wait_past(dve, w_done, g - 1)
                            for a in range(TOK):
                                n = bass.ds(TOK * g + a, 1)
                                dve.tensor_scalar(B[:, j % 2, a, :], iota[:, :], e2T[:, n], None, ALU.is_equal)
                                ins = dve.tensor_scalar(A[:, j % 2, a, :], iota[:, :], e1T[:, n], gT[:, n], ALU.is_equal, ALU.mult)
                            ins.then_inc(ab_ready, 1)
                            stream.subtract(dve, R * i, j + SPLIT)

                    step(FIRST)
                    with dve.Fori(FIRST + 1, END) as i:
                        step(i)

                @block.tensor
                def _(pe):
                    def step(i):
                        for j in range(R):
                            score(pe, i, j)
                            g = R * (i - FIRST) + j
                            pe.wait_ge(ab_ready, g + 1)
                            wait_past(pe, w_taken, g - 1)
                            for a in range(TOK):
                                ins = pe.matmul(w_bank(j)[:, a * KEYS:(a + 1) * KEYS], A[:, j % 2, a, :], B[:, j % 2, a, :],
                                                start=True, stop=True)
                            ins.then_inc(w_done, 1)

                    step(FIRST)
                    with pe.Fori(FIRST + 1, END) as i:
                        step(i)

                @block.scalar
                def _(act):
                    def step(i):
                        for j in range(R):
                            gelu(act, i, j)
                            g = R * (i - FIRST) + j
                            act.wait_ge(w_done, g + 1)
                            act.copy(W[:, :, bass.ds(TOK * g, TOK)].rearrange("p c n -> p n c"),
                                     w_bank(j).rearrange("p (n c) -> p n c", n=TOK)).then_inc(w_taken, 1)

                    step(FIRST)
                    with act.Fori(FIRST + 1, END) as i:
                        step(i)
                    for s in range(2):
                        act.wait_ge(g_stored[s], 16 * TILES // 2)
                    act.wait_ge(w_taken, TILES - HALF)

        with ExitStack() as inner:
            gate = core.sbuf(inner, name("gate"), [P, D])
            tmp = core.sbuf(inner, name("tmp"), [P, BANK])
            Ph, Pl = core.hTh, core.hTl
            gate_landed = sem("gate_landed")
            g_landed = [sem(f"gelu_landed{s}") for s in range(R)]
            p_ready, ph_ready, pl_ready = sem("p_ready"), sem("ph_ready"), sem("pl_ready")
            out_taken, out_chain = sem("out_taken"), sem("out_chain")
            FIRST, END = TILES // R, 2 * TILES // R
            with nc.Block() as block:
                @block.sync
                def _(sp):
                    def load_gelu(i, j):
                        n = R * (i - FIRST) + j
                        wait_past(sp, pl_ready, n - R + 1)
                        sp.dma_start(spare[:, j, :], gelu_rows[bass.ds(n, 1)].rearrange("a p n -> p (a n)"))\
                          .then_inc(g_landed[j], 16)

                    for j in range(R):
                        load_gelu(FIRST, j)
                    with sp.Fori(FIRST + 1, END) as i:
                        for j in range(R):
                            load_v(sp, i, j)
                            load_gelu(i, j)
                    sp.dma_start(gate[:, :], d["mod_rows"][2 * layer + 1][2 * D:].partition_broadcast(P))\
                      .then_inc(gate_landed, 16)

                @block.scalar
                def _(act):
                    def high(i, j):
                        act.wait_ge(p_ready, R * (i - FIRST) + j + 1)
                        act.copy(Ph[:, j % R, :], spare[:, j % R, :]).then_inc(ph_ready, 1)

                    def step(i, end=R + ROUND):
                        for j in range(R):
                            if j + ROUND < end:
                                stream.round(act, R * i, j + ROUND)
                            if j + SPLIT < end:
                                high(i, j + SPLIT)

                    for j in range(SPLIT):
                        high(FIRST, j)
                    with act.Fori(FIRST, END - 1) as i:
                        step(i)
                    step(END - 1, end=R)

                @block.vector
                def _(dve):
                    def product(i, j):
                        at = R * (i - FIRST) + j
                        dve.wait_ge(g_landed[j % R], 16 * (i - FIRST) + 16 * (j // R) + 16)
                        w = W[:, bass.ds(at, 1), :].rearrange("p a n -> p (a n)")
                        dve.tensor_tensor(spare[:, j % R, :], spare[:, j % R, :], w, ALU.mult).then_inc(p_ready, 1)

                    def low(i, j):
                        dve.wait_ge(ph_ready, R * (i - FIRST) + j + 1)
                        dve.tensor_tensor(Pl[:, j % R, :], spare[:, j % R, :], Ph[:, j % R, :].bitcast(F32), ALU.subtract)\
                           .then_inc(pl_ready, 1)

                    def step(i, end=R + ROUND):
                        for j in range(R):
                            if j + SPLIT < end:
                                product(i, j + SPLIT)
                            if j + 1 < end:
                                low(i, j + 1)
                            if j + SPLIT < end:
                                stream.subtract(dve, R * i, j + SPLIT)

                    for j in range(SPLIT):
                        product(FIRST, j)
                    low(FIRST, 0)
                    with dve.Fori(FIRST, END - 1) as i:
                        step(i)
                    step(END - 1, end=R)
                    dve.wait_ge(gate_landed, 16)
                    dve.wait_ge(stream.used, 2 * TILES)
                    chain = Chain(dve, out_chain)
                    for t in range(NT):
                        for c in range(2):
                            gated_add(core, chain, dve, tmp, gate, c * BANK, BANK, t, Y(t, c)).then_inc(out_taken, 1)
                            dve.wait_ge(out_taken, 2 * t + c + 1)

                @block.tensor
                def _(pe):
                    def add(i, j, first=False, last=False):
                        vh, vl = stream.ready(pe, R * i, j)
                        pe.wait_ge(pl_ready, R * (i - FIRST) + j + 1)
                        for t in range(NT):
                            tok = slice(t * P, (t + 1) * P)
                            for c in range(2):
                                cols = slice(c * BANK, (c + 1) * BANK)
                                ins = three(pe, Y(t, c), Ph[:, j, tok], Pl[:, j, tok], vh[:, cols], vl[:, cols], first, last)
                        ins.then_inc(stream.used, 1)

                    for j in range(R):
                        add(FIRST, j, first=j == 0)
                    with pe.Fori(FIRST + 1, END - 1) as i:
                        for j in range(R):
                            add(i, j)
                    for j in range(R):
                        add(END - 1, j, last=j == R - 1)


def stage_fox(core):
    nc, d = core.nc, core.dram
    with ExitStack() as ctx:
        width = 4 * D + MAPS
        proj = core.sbuf(ctx, "fox_proj", [P, NT, width])
        gate = core.sbuf(ctx, "fox_gate", [P, D])
        mask = core.sbuf(ctx, "fox_mask", [P, CAUSAL])
        left = core.sbuf(ctx, "fox_left", [2, MAPS, SEQ])
        right = core.sbuf(ctx, "fox_right", [2, MAPS, SEQ])
        consts_landed = core.sem("fox_consts_landed")
        with ExitStack() as inner:
            norm = Norm(core, inner, "fox_norm", d["fox_g"], mod=2)

            def take(eng, c, c0, w, t, src):
                return copy_on(eng, proj[:, t, c0:c0 + w], src)

            win = Project(core, inner, "fox_in", d["fox_in"], (core.hTh, core.hTl), column_chunks(0, width), take)
            with nc.Block() as block:
                @block.sync
                def _(sp):
                    norm.load(sp)
                    sp.dma_start(mask[:, :], d["c_mask"]).then_inc(consts_landed, 16)
                    sp.dma_start(gate[:, :], d["mod_rows"][2][2 * D:].partition_broadcast(P)).then_inc(consts_landed, 16)
                    win.load(sp)
                    sp.wait_ge(consts_landed, 32)

                @block.scalar
                def _(act):
                    norm.act(act)
                    win.run(act, win.stream.round, [1])

                @block.vector
                def _(dve):
                    norm.dve(dve)
                    win.run(dve, win.stream.subtract, [0])

                @block.tensor
                def _(pe):
                    norm.pe(pe)
                    norm.hT_done(pe)
                    win.pe(pe)

        sb = lambda n, s: core.sbuf(ctx, "fox_" + n, s)
        s = lambda n: core.sem("fox_" + n)
        fb, z, cum, onerow = sb("f_b", [MAPS, 1]), sb("z", [MAPS, 6, SEQ]), sb("cum", [MAPS, 2, SEQ]), sb("onerow", [MAPS, SEQ])
        fb_landed, f_turned, z_ready, e_ready, ln_ready, cum_chain, cum_ready, rows_landed, ones_ready, og_ready = (
            s(n) for n in ("fb_landed", "f_turned", "z_ready", "e_ready", "ln_ready", "cum_chain", "cum_ready",
                           "rows_landed", "ones_ready", "og_ready"))
        fcol = 3 * D
        with nc.Block() as block:
            @block.sync
            def _(sp):
                sp.dma_start(fb[:, :], d["fox_fb"]).then_inc(fb_landed, 16)
                sp.wait_ge(cum_ready, 1)
                sp.dma_start(left[1:2, :, :], cum[:, 0, :]).then_inc(rows_landed, 16)
                sp.dma_start(right[0:1, :, :], cum[:, 1, :]).then_inc(rows_landed, 16)
                sp.dma_start(left[0:1, :, :], onerow[:, :]).then_inc(rows_landed, 16)
                sp.dma_start(right[1:2, :, :], onerow[:, :]).then_inc(rows_landed, 16)
                sp.wait_ge(rows_landed, 64)

            @block.tensor
            def _(pe):
                for t in range(NT):
                    ins = pe.transpose(core.psum[0:MAPS, 0, t * P:(t + 1) * P], proj[:, t, fcol:fcol + MAPS], core.ident[:, :])
                ins.then_inc(f_turned, 1)

            @block.scalar
            def _(act):
                act.wait_ge(z_ready, 1)
                act.activation(z[:, 1, :], z[:, 1, :], ACT.Exp).then_inc(e_ready, 1)
                act.wait_ge(z_ready, 2)
                act.activation(z[:, 2, :], z[:, 3, :], ACT.Ln).then_inc(ln_ready, 1)
                for t in range(NT):
                    og = proj[:, t, fcol + MAPS:]
                    act.activation(og, og, ACT.Sigmoid).then_inc(og_ready, 1)
                act.wait_ge(og_ready, NT)

            @block.vector
            def _(dve):
                chain = Chain(dve, cum_chain)
                chain.step(dve.memset(onerow[:, :], 1.0))
                dve.wait_ge(f_turned, 1)
                dve.wait_ge(fb_landed, 16)
                chain.step(dve.tensor_scalar(z[:, 0, :], core.psum[0:MAPS, 0, 0:SEQ], fb[:, 0:1], None, ALU.add))
                chain.step(dve.tensor_scalar(z[:, 1, :], z[:, 0, :], -1.0, None, ALU.mult))
                dve.tensor_tensor(z[:, 1, :], z[:, 0, :], z[:, 1, :], ALU.min).then_inc(z_ready, 1)
                dve.wait_ge(z_ready, 1)
                chain.step(dve.tensor_scalar(z[:, 0, :], z[:, 0, :], 0.0, None, ALU.min))
                dve.wait_ge(e_ready, 1)
                dve.tensor_scalar(z[:, 3, :], z[:, 1, :], 1.0, None, ALU.add).then_inc(z_ready, 1)
                dve.wait_ge(ln_ready, 1)
                chain.step(dve.tensor_scalar(z[:, 5, :], z[:, 3, :], 1.0, None, ALU.is_equal))
                chain.step(dve.scalar_tensor_tensor(z[:, 4, :], z[:, 3, :], 1.0, z[:, 5, :], ALU.subtract, ALU.add))
                chain.step(dve.reciprocal(z[:, 4, :], z[:, 4, :]))
                chain.step(dve.tensor_tensor(z[:, 4, :], z[:, 2, :], z[:, 4, :], ALU.mult))
                chain.step(dve.tensor_tensor(z[:, 4, :], z[:, 4, :], z[:, 5, :], ALU.add))
                chain.step(dve.tensor_tensor(z[:, 4, :], z[:, 4, :], z[:, 1, :], ALU.mult))
                chain.step(dve.tensor_tensor(z[:, 0, :], z[:, 0, :], z[:, 4, :], ALU.subtract))
                chain.step(dve.tensor_tensor_scan(cum[:, 0, :], onerow[:, :], z[:, 0, :], 0.0, ALU.mult, ALU.add))
                dve.tensor_scalar(cum[:, 1, :], cum[:, 0, :], -1.0, None, ALU.mult).then_inc(cum_ready, 1)

        qk = [(0, d["fox_q_g"], True), (BANK, d["fox_q_g"], True), (D, d["fox_k_g"], False), (D + BANK, d["fox_k_g"], False)]
        att = Attention(core, ctx, "fox", proj, qk, lambda h, t: proj[:, t, 2 * D + h * HD:2 * D + (h + 1) * HD],
                        lambda h: (core.ident, mask[:, :]), decay=(left, right), gate=lambda dve, t: proj[:, t, fcol + MAPS:])
        tmp = core.sbuf(ctx, "fox_tmp", [P, 2 * NT, BANK])
        add_chain = core.sem("fox_add_chain")
        with ExitStack() as inner:
            hold = {}

            def add(eng, c, c0, w, t, src):
                return gated_add(core, hold["chain"], eng, tmp[:, NT * c + t, :], gate, c0, w, t, src)

            wout = Project(core, inner, "fox_out", d["fox_out"], (att.yTh, att.yTl), column_chunks(0, D), add, land=4)
            with nc.Block() as block:
                @block.sync
                def _(sp):
                    att.load(sp)
                    wout.load(sp)

                @block.gpsimd
                def _(pool):
                    att.pool(pool)

                @block.scalar
                def _(act):
                    att.act(act)
                    wout.run(act, wout.stream.round, [])

                @block.vector
                def _(dve):
                    att.dve(dve)
                    hold["chain"] = Chain(dve, add_chain)
                    wout.run(dve, wout.stream.subtract, [0, 1])
                    dve.wait_ge(wout.taken[1], 2)

                @block.tensor
                def _(pe):
                    att.pe(pe)
                    wout.pe(pe)


def stage_store(core, out):
    nc = core.nc
    stored = core.sem("out_stored")
    with nc.Block() as block:
        @block.sync
        def _(sp):
            sp.dma_start(out.rearrange("b (t p) c -> p (b t) c", p=P), core.x[:, :, :]).then_inc(stored, 16)
            sp.wait_ge(stored, 16)


def build(nc, dram, out, stages=("mix1", "moe", "lru", "peer0", "fox", "peer1")):
    with ExitStack() as ctx:
        core = Core(nc, ctx, dram)
        stage_start(core)
        run = {"mix1": lambda: stage_mix1(core), "moe": lambda: stage_moe(core), "lru": lambda: stage_lru(core),
               "peer0": lambda: stage_peer(core, 0), "fox": lambda: stage_fox(core), "peer1": lambda: stage_peer(core, 1)}
        for s in stages:
            run[s]()
            core.free_sems()
        stage_store(core, out)


def shape_constants():
    dist = SEQ - 1 - np.arange(2 * SEQ)
    n = np.maximum(dist, 1).astype(np.float32)
    exact = N_BUCKETS // 2
    large = exact + (np.log(n / exact) / np.float32(math.log(MAX_DISTANCE / exact)) * (N_BUCKETS - exact)).astype(np.int32)
    bucket = np.where(dist < exact, np.maximum(dist, 0), np.minimum(large, N_BUCKETS - 1))
    bucket = np.where(dist >= 0, bucket, N_BUCKETS)
    onehot = (np.arange(N_BUCKETS + 1)[:, None] == bucket[None, :]).astype(np.float32)
    q, k = np.arange(P)[:, None], np.arange(SEQ)[None, :]
    mask = np.concatenate([np.where(k[:, :P] <= q, 0, NEG), np.where(k <= q + P, 0, NEG)], 1).astype(np.float32)
    return {
        "c_ident": np.eye(P, dtype=np.float32),
        "c_flip": np.ascontiguousarray(np.eye(P, dtype=np.float32)[::-1]),
        "c_iota": np.tile(np.arange(KEYS, dtype=np.float32), (P, 1)),
        "c_rev": np.tile(np.arange(PER_GROUP, 0, -1, dtype=np.float32), (P, 1)),
        "c_buckets": onehot,
        "c_mask": mask,
    }


def laid_out(a):
    same = ["x", "norm1_g", "w_in", "diff_q_g", "diff_k_g", "lambda_q1", "lambda_k1", "lambda_q2", "lambda_k2",
            "diff_sub_g", "moba_q_g", "moba_k_g", "rel_bias", "w_out", "norm2_g"]
    m = {n: a[n] for n in same}
    rows = lambda v: v.reshape(KD, P, -1).transpose(1, 0, 2)
    experts = a["router_expert"][0].transpose(1, 0, 2).reshape(D, EXPERTS)
    gate_up = np.concatenate([a["w_gate"][0], a["w_up"][0]], axis=2)
    gate_up = gate_up.reshape(EXPERTS, 4, 2, P, 2 * HIDDEN).transpose(0, 1, 3, 2, 4).reshape(EXPERTS, 4, P, D)
    down = a["w_down"][0].reshape(EXPERTS, HIDDEN // P, P, D)
    turns = np.concatenate([gate_up[1:], down[:-1]], axis=1).reshape(-1, P, D)
    m["moe_w"] = np.concatenate([gate_up[0], turns, down[-1]])
    m["router"] = rows(np.concatenate([a["router_group"][0], experts], axis=1))
    m["c_col"] = a["c_2"].reshape(KD, P).T
    for i, n in enumerate(("l0_mix", "l0_ffn", "l1_mix", "l1_ffn")):
        m[f"mod_w{i}"], m[f"mod_b{i}"] = a[n + "_mod_w_2"], a[n + "_mod_b_2"]
    blocks = lambda v: v.reshape(-1, LBLK, P).transpose(2, 0, 1)
    m["lru_g"], m["lru_in"], m["lru_out"] = a["l0_mix_norm_g_2"], a["l0_lru_in_w_2"], a["l0_lru_out_w_2"]
    m["lru_vec"] = np.concatenate([blocks(a["l0_lru_" + n]) for n in (
        "conv_w_2", "conv_b_2", "ra_b_2", "ri_b_2", "lambda_2")], axis=1)
    gates = np.zeros((2, RNN, RNN), np.float32)
    for g, n in enumerate(("ra", "ri")):
        for b in range(GATE_BLOCKS):
            at = slice(b * GATE_W, (b + 1) * GATE_W)
            gates[g, at, at] = a[f"l0_lru_{n}_w_2"][b]
    m["lru_gate_w"] = np.stack([gates[:, i * P:(i + 1) * P, j * P:(j + 1) * P] for i, j in gate_tiles()], 1).transpose(2, 0, 1, 3)
    for i in range(2):
        l = f"l{i}_"
        m[f"peer{i}_g"], m[f"peer{i}_q"] = a[l + "ffn_norm_g_2"], a[l + "peer_q_w_2"]
        m[f"peer{i}_sub"] = np.stack([a[l + "peer_subkey1_2"], a[l + "peer_subkey2_2"]], 1)\
            .reshape(2 * PHEADS, KEYS, -1).transpose(2, 0, 1)
        m[f"peer{i}_u"] = a[l + "peer_u_2"].reshape(KEYS, KEYS, KD, P).transpose(1, 3, 2, 0)
        m[f"peer{i}_v"] = a[l + "peer_v_2"].reshape(KEYS, KEYS, D).transpose(1, 0, 2).reshape(KEYS * KEYS, D)
    m["fox_g"], m["fox_in"], m["fox_out"] = a["l1_mix_norm_g_2"], a["l1_fox_in_w_2"], a["l1_fox_out_w_2"]
    m["fox_fb"] = a["l1_fox_f_b_2"].reshape(MAPS, 1)
    m["fox_q_g"], m["fox_k_g"] = a["l1_fox_q_norm_g_2"], a["l1_fox_k_norm_g_2"]
    return m


def declare(nc, arrays):
    dram = {n: nc.dram_tensor("in_" + n, v.shape, mybir.dt.from_np(v.dtype), kind="ExternalInput").ap()
            for n, v in arrays.items()}
    dram["mod_w"] = [dram[f"mod_w{i}"] for i in range(MODS)]
    dram["mod_b"] = [dram[f"mod_b{i}"] for i in range(MODS)]
    dram["mod_rows"] = nc.dram_tensor("mod_rows", (MODS, MODW), F32, kind="Internal").ap()
    dram["gelu_rows"] = nc.dram_tensor("gelu_rows", (KEYS, P, SEQ), F32, kind="Internal").ap()
    dram["curve"] = nc.dram_tensor("bias_curve_rows", (N_REL_HEADS, BANK), F32, kind="Internal").ap()
    return dram


def kernel(**inputs):
    import concourse.bacc as bacc
    from concourse.bass_utils import run_bass_kernel_spmd

    a = {n: np.asarray(v) for n, v in inputs.items()}
    arrays = {n: np.ascontiguousarray(v) for n, v in {**laid_out(a), **shape_constants()}.items()}
    nc = bacc.Bacc("TRN2", target_bir_lowering=False, num_devices=1)
    dram = declare(nc, arrays)
    out = nc.dram_tensor("out", (1, SEQ, D), F32, kind="ExternalOutput").ap()
    build(nc, dram, out)
    r = run_bass_kernel_spmd(nc, [{"in_" + n: v for n, v in arrays.items()}], core_ids=[0])
    return r.results[0]["out"]
```
